# Optimizing a Trainium2 kernel written in Bass

```python
import jax, jax.numpy as jnp
from jax import lax
import numpy as np
import math

D_MODEL = 1024
BATCH = 1
SEQ = 256
DEPTH = 1

GRID_W = 64
CTX_LEN = 256
HG_HEADS = 4
HG_DK = 128
HG_DV = 128
GLA_HEADS = 4
GLA_DK = 64
GLA_DV = 128
GLA_GATE_RANK = 16
GLA_GATE_NORM = 16.0
HG_KW = HG_HEADS * HG_DK
HG_VW = HG_HEADS * HG_DV
GLA_KW = GLA_HEADS * GLA_DK
GLA_VW = GLA_HEADS * GLA_DV
D_MIX = HG_VW + GLA_VW
CHUNK = 64
PEER_HEADS = 8
PEER_NKEYS = 128
PEER_EXPERTS = PEER_NKEYS * PEER_NKEYS
PEER_DQ = 256
PEER_TOPK = 16
PEER_BLOCK = 128
ALPHA = (2.0 * DEPTH) ** 0.25
BETA = (8.0 * DEPTH) ** -0.25
EPS = 1e-6
LB_FLOOR = 1e-30
IN_SPLITS = (HG_KW, HG_KW, HG_KW, HG_VW, HG_VW, GLA_KW, GLA_KW, GLA_VW, GLA_VW, GLA_GATE_RANK, GLA_GATE_RANK)
D_IN = sum(IN_SPLITS)
IN_SPLIT_POINTS = [int(p) for p in np.cumsum(IN_SPLITS)[:-1]]


def layer_norm(x, gamma=None, beta=None):
    xf = x.astype(jnp.float32)
    mu = jnp.mean(xf, axis=-1, keepdims=True)
    var = jnp.mean(jnp.square(xf - mu), axis=-1, keepdims=True)
    y = (xf - mu) * lax.rsqrt(var + EPS)
    if gamma is not None:
        y = y * gamma.astype(jnp.float32) + beta.astype(jnp.float32)
    return y.astype(x.dtype)

def modulate(x, shift, scale):
    return layer_norm(x) * (1.0 + scale) + shift

def heads(t, n):
    B, L, _ = t.shape
    return t.reshape(B, L, n, -1).transpose(0, 2, 1, 3).astype(jnp.float32)

def head_rms_merge(o, gain):
    o = o * lax.rsqrt(jnp.mean(o * o, axis=-1, keepdims=True) + EPS) * gain.astype(jnp.float32)
    B, n, L, d = o.shape
    return o.transpose(0, 2, 1, 3).reshape(B, L, n * d)

def to_col_major(t, rows):
    B, L, C = t.shape
    return t.reshape(B, rows, GRID_W, C).transpose(0, 2, 1, 3).reshape(B, L, C)

def from_col_major(t, rows):
    B, L, C = t.shape
    return t.reshape(B, GRID_W, rows, C).transpose(0, 2, 1, 3).reshape(B, L, C)

def chunk_scan(q, k, v, log_a, s0):
    B, H, L, dk = q.shape
    dv = v.shape[-1]
    n = L // CHUNK

    def split(t):
        return jnp.moveaxis(t.reshape(B, H, n, CHUNK, t.shape[-1]), 2, 0)

    incl = jnp.tril(jnp.ones((CHUNK, CHUNK), dtype=bool))[:, :, None]

    def step(s, inp):
        qc, kc, vc, ac = inp
        b = jnp.cumsum(ac, axis=-2)
        rel = b[..., :, None, :] - b[..., None, :, :]
        decay = jnp.where(incl, jnp.exp(jnp.minimum(rel, 0.0)), 0.0)
        scores = jnp.einsum('bhtk,bhsk,bhtsk->bhts', qc, kc, decay)
        o = jnp.einsum('bhts,bhsv->bhtv', scores, vc) + jnp.einsum('bhtk,bhkv->bhtv', qc * jnp.exp(b), s)
        b_end = b[..., -1:, :]
        s_new = jnp.exp(b_end[..., 0, :])[..., None] * s + jnp.einsum('bhsk,bhsv->bhkv', kc * jnp.exp(b_end - b), vc)
        return s_new, o

    s_end, o = lax.scan(step, s0, (split(q), split(k), split(v), split(log_a)))
    return jnp.moveaxis(o, 0, 2).reshape(B, H, L, dv), s_end

def scan_two_way(ctx_parts, lat_parts):
    qc, vc, kcf, acf, kcb, acb = ctx_parts
    ql, vl, klf, alf, klb, alb = lat_parts
    B, H, _, dk = qc.shape
    s0 = jnp.zeros((B, H, dk, vc.shape[-1]), jnp.float32)
    flip = lambda t: jnp.flip(t, axis=2)
    oc_f, sc_f = chunk_scan(qc, kcf, vc, acf, s0)
    ol_f, _ = chunk_scan(ql, klf, vl, alf, sc_f)
    oc_b, sc_b = chunk_scan(flip(qc), flip(kcb), flip(vc), flip(acb), s0)
    ol_b, _ = chunk_scan(flip(ql), flip(klb), flip(vl), flip(alb), sc_b)
    return oc_f + flip(oc_b), ol_f + flip(ol_b)

def hgrn2_inputs(hq, hff, hfb, hi, lb_f, lb_b):
    def gate(z, lb):
        z = z.astype(jnp.float32)
        log_lb = jnp.log(jnp.maximum(lb, LB_FLOOR))
        log_f = jnp.logaddexp(log_lb, jnp.log1p(-lb) + jax.nn.log_sigmoid(z))
        k = (1.0 - lb) * jax.nn.sigmoid(-z)
        return heads(k, HG_HEADS), heads(log_f, HG_HEADS)
    kf, af = gate(hff, lb_f)
    kb, ab = gate(hfb, lb_b)
    return (heads(hq, HG_HEADS), heads(hi, HG_HEADS), kf, af, kb, ab)

def gla_inputs(gq, gk, gv, glf, glb, w_gk2, b_gk):
    def gate(r, w, b):
        la = jax.nn.log_sigmoid((r @ w + b).astype(jnp.float32)) / GLA_GATE_NORM
        return heads(la, GLA_HEADS)
    k = heads(gk, GLA_HEADS)
    q = heads(gq, GLA_HEADS) * (GLA_DK ** -0.5)
    return (q, heads(gv, GLA_HEADS), k, gate(glf, w_gk2[0], b_gk[0]), k, gate(glb, w_gk2[1], b_gk[1]))

def token_mixer(u_c, u_l, rows, lb_f, lb_b, w_gk2, b_gk, hg_gain, gla_gain):
    pc = jnp.split(u_c, IN_SPLIT_POINTS, axis=-1)
    pl = jnp.split(u_l, IN_SPLIT_POINTS, axis=-1)
    a_c, a_l = scan_two_way(hgrn2_inputs(pc[0], pc[1], pc[2], pc[3], lb_f, lb_b),
                            hgrn2_inputs(pl[0], pl[1], pl[2], pl[3], lb_f, lb_b))
    out_a_c = head_rms_merge(a_c, hg_gain).astype(u_c.dtype) * jax.nn.silu(pc[4])
    out_a_l = head_rms_merge(a_l, hg_gain).astype(u_l.dtype) * jax.nn.silu(pl[4])
    gl = [to_col_major(pl[j], rows) for j in (5, 6, 7, 9, 10)]
    b_c, b_l = scan_two_way(gla_inputs(pc[5], pc[6], pc[7], pc[9], pc[10], w_gk2, b_gk),
                            gla_inputs(gl[0], gl[1], gl[2], gl[3], gl[4], w_gk2, b_gk))
    out_b_c = head_rms_merge(b_c, gla_gain).astype(u_c.dtype) * jax.nn.silu(pc[8])
    out_b_l = from_col_major(head_rms_merge(b_l, gla_gain), rows).astype(u_l.dtype) * jax.nn.silu(pl[8])
    return (jnp.concatenate([out_a_c, out_b_c], axis=-1), jnp.concatenate([out_a_l, out_b_l], axis=-1))

def peer(h, w_query, sub_keys, expert_u, expert_v):
    B, L, D = h.shape
    tok = h.reshape(-1, PEER_BLOCK, D)
    k1 = sub_keys[0].astype(jnp.float32)
    k2 = sub_keys[1].astype(jnp.float32)

    def block(t):
        q = (t @ w_query).reshape(PEER_BLOCK, PEER_HEADS, 2, PEER_DQ // 2).astype(jnp.float32)
        s1 = jnp.einsum('thd,nd->thn', q[:, :, 0], k1)
        s2 = jnp.einsum('thd,nd->thn', q[:, :, 1], k2)
        v1, i1 = lax.top_k(s1, PEER_TOPK)
        v2, i2 = lax.top_k(s2, PEER_TOPK)
        cand_s = (v1[..., :, None] + v2[..., None, :]).reshape(PEER_BLOCK, PEER_HEADS, PEER_TOPK * PEER_TOPK)
        cand_i = (i1[..., :, None] * PEER_NKEYS + i2[..., None, :]).reshape(PEER_BLOCK, PEER_HEADS, PEER_TOPK * PEER_TOPK)
        top_s, pos = lax.top_k(cand_s, PEER_TOPK)
        idx = jnp.take_along_axis(cand_i, pos, axis=-1)
        g = jax.nn.softmax(top_s, axis=-1)
        act = jax.nn.gelu(jnp.einsum('thkd,td->thk', expert_u[idx], t).astype(jnp.float32))
        return jnp.einsum('thk,thkd->td', (g * act).astype(t.dtype), expert_v[idx])

    return lax.map(block, tok).reshape(B, L, D)

def first_inputs(seed: int = 0) -> dict:
    key = jax.random.key(seed)
    ks = jax.random.split(key, 20)
    f32 = jnp.float32
    nrm = lambda k, shape, s: jax.random.normal(k, shape, f32) * s
    return {
        'x': nrm(ks[0], (BATCH, SEQ, D_MODEL), 1.0),
        'c': nrm(ks[1], (BATCH, D_MODEL), 1.0),
        'ctx': nrm(ks[2], (BATCH, CTX_LEN, D_MODEL), 1.0),
        'c_ctx': nrm(ks[3], (D_MODEL,), 1.0),
        'w_ada': nrm(ks[4], (DEPTH, D_MODEL, 6 * D_MODEL), 0.5 * D_MODEL ** -0.5),
        'b_ada': nrm(ks[5], (DEPTH, 6 * D_MODEL), 0.01),
        'w_in': nrm(ks[6], (DEPTH, D_MODEL, D_IN), D_MODEL ** -0.5),
        'w_gk2': nrm(ks[7], (DEPTH, 2, GLA_GATE_RANK, GLA_KW), GLA_GATE_RANK ** -0.5),
        'b_gk': nrm(ks[8], (DEPTH, 2, GLA_KW), 0.01),
        'hg_lower_bounds': nrm(ks[9], (2, DEPTH, HG_KW), 0.1),
        'hg_norm': 1.0 + nrm(ks[10], (DEPTH, HG_DV), 0.01),
        'gla_norm': 1.0 + nrm(ks[11], (DEPTH, GLA_DV), 0.01),
        'w_out': nrm(ks[12], (DEPTH, D_MIX, D_MODEL), BETA * D_MIX ** -0.5),
        'ln_gamma': 1.0 + nrm(ks[13], (DEPTH, 2, D_MODEL), 0.01),
        'ln_beta': nrm(ks[14], (DEPTH, 2, D_MODEL), 0.01),
        'peer_w_query': nrm(ks[15], (DEPTH, D_MODEL, PEER_HEADS * PEER_DQ), D_MODEL ** -0.5),
        'peer_sub_keys': nrm(ks[16], (DEPTH, 2, PEER_NKEYS, PEER_DQ // 2), (PEER_DQ // 2) ** -0.5),
        'peer_u': nrm(ks[17], (DEPTH, PEER_EXPERTS, D_MODEL), D_MODEL ** -0.5),
        'peer_v': nrm(ks[18], (DEPTH, PEER_EXPERTS, D_MODEL), BETA),
    }

def first_block(x, c, ctx, c_ctx, w_ada, b_ada, w_in, w_gk2, b_gk, hg_lower_bounds, hg_norm, gla_norm,
              w_out, ln_gamma, ln_beta, peer_w_query, peer_sub_keys, peer_u, peer_v):
    rows = x.shape[1] // GRID_W
    sm = jax.nn.softmax(hg_lower_bounds.astype(jnp.float32), axis=1)
    lb_all = jnp.clip(jnp.cumsum(sm, axis=1) - sm[:, :1], 0.0, 1.0 - 1e-6)
    xc = ctx
    for i in range(DEPTH):
        last = i == DEPTH - 1
        m_l = jax.nn.silu(c) @ w_ada[i] + b_ada[i]
        m_c = jax.nn.silu(c_ctx) @ w_ada[i] + b_ada[i]
        sh1_l, sc1_l, g1_l, sh2_l, sc2_l, g2_l = [t[:, None, :] for t in jnp.split(m_l, 6, axis=-1)]
        sh1_c, sc1_c, g1_c, sh2_c, sc2_c, g2_c = jnp.split(m_c, 6, axis=-1)
        u_l = modulate(x, sh1_l, sc1_l) @ w_in[i]
        u_c = modulate(xc, sh1_c, sc1_c) @ w_in[i]
        mix_c, mix_l = token_mixer(u_c, u_l, rows, lb_all[0, i], lb_all[1, i], w_gk2[i], b_gk[i],
                                   hg_norm[i], gla_norm[i])
        x = layer_norm(ALPHA * x + g1_l * (mix_l @ w_out[i]), ln_gamma[i, 0], ln_beta[i, 0])
        if not last:
            xc = layer_norm(ALPHA * xc + g1_c * (mix_c @ w_out[i]), ln_gamma[i, 0], ln_beta[i, 0])
        y_l = peer(modulate(x, sh2_l, sc2_l), peer_w_query[i], peer_sub_keys[i], peer_u[i], peer_v[i])
        x = layer_norm(ALPHA * x + g2_l * y_l, ln_gamma[i, 1], ln_beta[i, 1])
        if not last:
            y_c = peer(modulate(xc, sh2_c, sc2_c), peer_w_query[i], peer_sub_keys[i], peer_u[i], peer_v[i])
            xc = layer_norm(ALPHA * xc + g2_c * y_c, ln_gamma[i, 1], ln_beta[i, 1])
    return x


DEPTH_2 = 2

Q_BLOCK = 128
D_MIX_2 = D_MODEL
LRU_WIDTH = D_MIX_2 // 2
LRU_BLOCKS = 8
LRU_BLOCK_W = LRU_WIDTH // LRU_BLOCKS
CONV_W = 4
RG_C = 8.0
ATTN_WIDTH = D_MIX_2 - LRU_WIDTH
DIFF_HEADS = 4
DIFF_VDIM = ATTN_WIDTH // DIFF_HEADS
DIFF_DH = DIFF_VDIM // 2
ROPE_THETA = 10000.0
D_IN_2 = 2 * LRU_WIDTH + 3 * ATTN_WIDTH
D_FF = 3 * D_MODEL
N_EXPERTS = 8
TOP_K = 2
N_DENSE = (DEPTH_2 + 1) // 2
N_MOE = DEPTH_2 // 2
MAX_OFFSET_CHUNKS = 64


def rmsnorm(x, g):
    x32 = x.astype(jnp.float32)
    y = x32 * lax.rsqrt(jnp.mean(x32 * x32, axis=-1, keepdims=True) + EPS)
    return y.astype(x.dtype) * g

def rope5(x, pos):
    inv = ROPE_THETA ** (-jnp.arange(0, DIFF_DH, 2, dtype=jnp.float32) / DIFF_DH)
    ang = pos.astype(jnp.float32)[..., None] * inv
    ang = jnp.concatenate([ang, ang], axis=-1)[:, :, None, None, :]
    cos, sin = jnp.cos(ang), jnp.sin(ang)
    x1, x2 = jnp.split(x, 2, axis=-1)
    rot = jnp.concatenate([-x2, x1], axis=-1)
    return (x * cos + rot * sin).astype(x.dtype)

def causal_conv(x, w, b):
    rhs = w[:, None, :]
    y = lax.conv_general_dilated(x, rhs, window_strides=(1,), padding=[(CONV_W - 1, 0)],
                                 dimension_numbers=('NWC', 'WIO', 'NWC'),
                                 feature_group_count=x.shape[-1])
    return y + b

def _lin_rec(e1, e2):
    a1, b1 = e1
    a2, b2 = e2
    return a1 * a2, a2 * b1 + b2

def rg_lru(x, wa, ba, wx, bx, lam):
    B, S, W = x.shape
    xb = x.reshape(B, S, LRU_BLOCKS, LRU_BLOCK_W)
    r = jax.nn.sigmoid(jnp.einsum('bsnh,nhk->bsnk', xb, wa).reshape(B, S, W) + ba)
    i = jax.nn.sigmoid(jnp.einsum('bsnh,nhk->bsnk', xb, wx).reshape(B, S, W) + bx)
    log_a = -RG_C * r.astype(jnp.float32) * jax.nn.softplus(-lam.astype(jnp.float32))
    a = jnp.exp(log_a)
    mult = jnp.sqrt(-jnp.expm1(2.0 * log_a))
    bt = mult * (i * x).astype(jnp.float32)
    _, h = lax.associative_scan(_lin_rec, (a, bt), axis=1)
    return h.astype(x.dtype)

def diff_attention(q, k, v, pos, lq1, lk1, lq2, lk2, subln_g, lambda_init):
    B, S, _ = q.shape
    q = rope5(q.reshape(B, S, DIFF_HEADS, 2, DIFF_DH), pos)
    k = rope5(k.reshape(B, S, DIFF_HEADS, 2, DIFF_DH), pos)
    v = v.reshape(B, S, DIFF_HEADS, DIFF_VDIM)
    lam = (jnp.exp(jnp.sum(lq1.astype(jnp.float32) * lk1.astype(jnp.float32)))
           - jnp.exp(jnp.sum(lq2.astype(jnp.float32) * lk2.astype(jnp.float32)))
           + lambda_init)
    chunk = pos // CHUNK
    nqb = S // Q_BLOCK
    qs = q.reshape(B, nqb, Q_BLOCK, DIFF_HEADS, 2, DIFF_DH).transpose(1, 0, 3, 4, 2, 5)
    qc = chunk.reshape(B, nqb, Q_BLOCK).transpose(1, 0, 2)
    kt = k.transpose(0, 2, 3, 1, 4)
    vt = v.transpose(0, 2, 1, 3)
    scale = DIFF_DH ** -0.5
    neg = jnp.finfo(jnp.float32).min

    def attend(args):
        qb, qcb = args
        s = jnp.einsum('bhcqd,bhckd->bhcqk', qb, kt).astype(jnp.float32) * scale
        mask = (chunk[:, None, :] <= qcb[:, :, None])[:, None, None]
        p = jax.nn.softmax(jnp.where(mask, s, neg), axis=-1)
        pd = p[:, :, 0] - lam * p[:, :, 1]
        return jnp.einsum('bhqk,bhkd->bhqd', pd.astype(vt.dtype), vt)

    o = lax.map(attend, (qs, qc))
    o = o.transpose(1, 0, 3, 2, 4).reshape(B, S, DIFF_HEADS, DIFF_VDIM)
    o = rmsnorm(o, subln_g) * (1.0 - lambda_init)
    return o.reshape(B, S, ATTN_WIDTH)

def swiglu(h, wg, wu, wd):
    return (jax.nn.silu(h @ wg) * (h @ wu)) @ wd

def moe(h, router, wg, wu, wd):
    logits = (h @ router).astype(jnp.float32)
    vals, idx = lax.top_k(logits, TOP_K)
    w = jax.nn.softmax(vals, axis=-1)
    gates = jnp.sum(jax.nn.one_hot(idx, N_EXPERTS, dtype=jnp.float32) * w[..., None], axis=-2)
    y = jnp.zeros_like(h)
    for e in range(N_EXPERTS):
        y = y + gates[..., e:e + 1].astype(h.dtype) * swiglu(h, wg[e], wu[e], wd[e])
    return y

def second_inputs(seed: int = 0) -> dict:
    key = jax.random.key(seed)
    ks = iter(jax.random.split(key, 40))
    f32 = jnp.float32

    def nrm(shape, scale):
        return jax.random.normal(next(ks), shape, f32) * scale

    a0 = jax.random.uniform(next(ks), (DEPTH_2, LRU_WIDTH), f32, 0.9, 0.999)
    s0 = a0 ** (1.0 / RG_C)
    lru_lambda = jnp.log(s0) - jnp.log1p(-s0)
    offsets = jax.random.randint(next(ks), (BATCH, 1), 0, MAX_OFFSET_CHUNKS) * CHUNK
    positions = (offsets + jnp.arange(SEQ, dtype=jnp.int32)[None, :]).astype(jnp.int32)
    return {
        'x': nrm((BATCH, SEQ, D_MODEL), 1.0),
        'c': nrm((BATCH, D_MODEL), 1.0),
        'positions': positions,
        'ada_w': nrm((DEPTH_2, D_MODEL, 6 * D_MODEL), 0.5 * D_MODEL ** -0.5),
        'ada_b': nrm((DEPTH_2, 6 * D_MODEL), 0.02),
        'ln1_g': 1.0 + nrm((DEPTH_2, D_MODEL), 0.02),
        'ln2_g': 1.0 + nrm((DEPTH_2, D_MODEL), 0.02),
        'w_in': nrm((DEPTH_2, D_MODEL, D_IN_2), D_MODEL ** -0.5),
        'conv_w': nrm((DEPTH_2, CONV_W, LRU_WIDTH), CONV_W ** -0.5),
        'conv_b': nrm((DEPTH_2, LRU_WIDTH), 0.02),
        'gate_a_w': nrm((DEPTH_2, LRU_BLOCKS, LRU_BLOCK_W, LRU_BLOCK_W), LRU_BLOCK_W ** -0.5),
        'gate_a_b': nrm((DEPTH_2, LRU_WIDTH), 0.02),
        'gate_x_w': nrm((DEPTH_2, LRU_BLOCKS, LRU_BLOCK_W, LRU_BLOCK_W), LRU_BLOCK_W ** -0.5),
        'gate_x_b': nrm((DEPTH_2, LRU_WIDTH), 0.02),
        'lru_lambda': lru_lambda,
        'lam_q1': nrm((DEPTH_2, DIFF_DH), 0.1),
        'lam_k1': nrm((DEPTH_2, DIFF_DH), 0.1),
        'lam_q2': nrm((DEPTH_2, DIFF_DH), 0.1),
        'lam_k2': nrm((DEPTH_2, DIFF_DH), 0.1),
        'subln_g': 1.0 + nrm((DEPTH_2, DIFF_VDIM), 0.02),
        'w_out': nrm((DEPTH_2, D_MIX_2, D_MODEL), D_MIX_2 ** -0.5),
        'ffn_w_gate': nrm((N_DENSE, D_MODEL, D_FF), D_MODEL ** -0.5),
        'ffn_w_up': nrm((N_DENSE, D_MODEL, D_FF), D_MODEL ** -0.5),
        'ffn_w_down': nrm((N_DENSE, D_FF, D_MODEL), D_FF ** -0.5),
        'moe_router': nrm((N_MOE, D_MODEL, N_EXPERTS), D_MODEL ** -0.5),
        'moe_w_gate': nrm((N_MOE, N_EXPERTS, D_MODEL, D_FF), D_MODEL ** -0.5),
        'moe_w_up': nrm((N_MOE, N_EXPERTS, D_MODEL, D_FF), D_MODEL ** -0.5),
        'moe_w_down': nrm((N_MOE, N_EXPERTS, D_FF, D_MODEL), D_FF ** -0.5),
        'final_g': 1.0 + nrm((D_MODEL,), 0.02),
    }

def second_block(x, c, positions, ada_w, ada_b, ln1_g, ln2_g, w_in, conv_w, conv_b,
              gate_a_w, gate_a_b, gate_x_w, gate_x_b, lru_lambda, lam_q1, lam_k1,
              lam_q2, lam_k2, subln_g, w_out, ffn_w_gate, ffn_w_up, ffn_w_down,
              moe_router, moe_w_gate, moe_w_up, moe_w_down, final_g):
    splits = [LRU_WIDTH, 2 * LRU_WIDTH, 2 * LRU_WIDTH + ATTN_WIDTH, 2 * LRU_WIDTH + 2 * ATTN_WIDTH]
    for l in range(DEPTH_2):
        lambda_init = 0.8 - 0.6 * math.exp(-0.3 * l)
        mod = jax.nn.silu(c) @ ada_w[l] + ada_b[l]
        sh1, sc1, g1, sh2, sc2, g2 = jnp.split(mod[:, None, :], 6, axis=-1)
        h = rmsnorm(x, ln1_g[l]) * (1.0 + sc1) + sh1
        z = h @ w_in[l]
        xr, yr, q, k, v = jnp.split(z, splits, axis=-1)
        lru = rg_lru(causal_conv(xr, conv_w[l], conv_b[l]), gate_a_w[l], gate_a_b[l],
                     gate_x_w[l], gate_x_b[l], lru_lambda[l]) * jax.nn.gelu(yr)
        att = diff_attention(q, k, v, positions, lam_q1[l], lam_k1[l], lam_q2[l], lam_k2[l],
                             subln_g[l], lambda_init)
        x = x + g1 * (jnp.concatenate([lru, att], axis=-1) @ w_out[l])
        h = rmsnorm(x, ln2_g[l]) * (1.0 + sc2) + sh2
        if l % 2 == 0:
            j = l // 2
            f = swiglu(h, ffn_w_gate[j], ffn_w_up[j], ffn_w_down[j])
        else:
            j = l // 2
            f = moe(h, moe_router[j], moe_w_gate[j], moe_w_up[j], moe_w_down[j])
        x = x + g2 * f
    return rmsnorm(x, final_g)


def setup_inputs(seed=0):
    out = dict(first_inputs(seed))
    for name, value in second_inputs(seed + 1).items():
        if name != "x":
            out[name + "_2"] = value
    return out


def reference(
    x, c, ctx, c_ctx, w_ada, b_ada, w_in, w_gk2, b_gk, hg_lower_bounds, hg_norm, gla_norm,
    w_out, ln_gamma, ln_beta, peer_w_query, peer_sub_keys, peer_u, peer_v, c_2, positions_2,
    ada_w_2, ada_b_2, ln1_g_2, ln2_g_2, w_in_2, conv_w_2, conv_b_2, gate_a_w_2, gate_a_b_2,
    gate_x_w_2, gate_x_b_2, lru_lambda_2, lam_q1_2, lam_k1_2, lam_q2_2, lam_k2_2, subln_g_2,
    w_out_2, ffn_w_gate_2, ffn_w_up_2, ffn_w_down_2, moe_router_2, moe_w_gate_2, moe_w_up_2,
    moe_w_down_2, final_g_2,
):
    x = first_block(
        x, c, ctx, c_ctx, w_ada, b_ada, w_in, w_gk2, b_gk, hg_lower_bounds, hg_norm, gla_norm,
        w_out, ln_gamma, ln_beta, peer_w_query, peer_sub_keys, peer_u, peer_v,
    )
    return second_block(
        x, c_2, positions_2, ada_w_2, ada_b_2, ln1_g_2, ln2_g_2, w_in_2, conv_w_2, conv_b_2,
        gate_a_w_2, gate_a_b_2, gate_x_w_2, gate_x_b_2, lru_lambda_2, lam_q1_2, lam_k1_2,
        lam_q2_2, lam_k2_2, subln_g_2, w_out_2, ffn_w_gate_2, ffn_w_up_2, ffn_w_down_2,
        moe_router_2, moe_w_gate_2, moe_w_up_2, moe_w_down_2, final_g_2,
    )


_drawn_inputs = setup_inputs


def setup_inputs(seed=0):
    import zlib

    import numpy as np

    out = dict(_drawn_inputs(seed))
    spreads = {}
    factors = {'ctx': 3.005,
     'c_ctx': 3.117,
     'b_ada': 3.127,
     'b_gk': 8.0,
     'hg_norm': 8.0,
     'gla_norm': 8.0,
     'ln1_g_2': 3.965,
     'ln2_g_2': 2.983,
     'gate_a_b_2': 8.0,
     'gate_x_b_2': 8.0,
     'lam_q1_2': 8.0,
     'lam_k1_2': 4.793,
     'lam_k2_2': 3.232,
     'subln_g_2': 8.0,
     'final_g_2': 2.889}
    for name, (base, spread) in spreads.items():
        noise = np.random.default_rng([zlib.crc32(name.encode()), seed]).standard_normal(out[name].shape)
        drawn = base * np.exp(spread * noise) if base else spread * noise
        out[name] = __import__('jax').numpy.asarray(drawn.astype(out[name].dtype))
    for name, factor in factors.items():
        out[name] = (out[name] * factor).astype(out[name].dtype)
    return out
```

```python
from contextlib import ExitStack

import numpy as np

import concourse.bass as bass
from concourse import mybir

F32 = mybir.dt.float32
I32 = mybir.dt.int32
U32 = mybir.dt.uint32
ALU = mybir.AluOpType
ACT = mybir.ActivationFunctionType
AX = mybir.AxisListType

P = 128
D = 1024
C = D // P
N = 256
NC = 256
L = N + NC
U = 4
EPS = 1e-6
ALPHA = 2.0 ** 0.25
LB_FLOOR = 1e-30
GRID_W = 64
ROWS = N // GRID_W
CH = 128
LEVELS = 7
TOPK = 16
HEADS = 8
LN2 = 0.6931471805599453
NEG = -3.0e38
PLACED = (0, 1, 2, 3, 4, 6, 5, 7)
TWO_PI = 6.283185307179586
PI_A = 6.28125
PI_B = 0.0019350051879882812
PI_C = TWO_PI - PI_A - PI_B
ROUND = 12582912.0
DEPTH_2 = 2
D_FF = 3072
FT = D_FF // P
EXPERTS = 8
MORE = 3
ROUNDS = EXPERTS + MORE
FAR = 1.0e6
DH = 64


def column_map():
    sizes = [("c", 16), ("b_ada", 48), ("lb", 8), ("b_gk", 4), ("hg_norm", 1), ("gla_norm", 1),
             ("ln_gamma0", 8), ("ln_gamma1", 8), ("ln_beta0", 8), ("ln_beta1", 8), ("c_2", 8),
             ("final_g", 8), ("inv_freq", 1), ("one", 1), ("eps", 1), ("halfpi", 1),
             ("partition", 1)]
    for l in range(DEPTH_2):
        sizes += [(f"ada_b{l}", 48), (f"ln1_g{l}", 8), (f"ln2_g{l}", 8), (f"conv_w{l}", 16), (f"conv_b{l}", 4),
                  (f"gate_a_b{l}", 4), (f"gate_x_b{l}", 4), (f"lru_lambda{l}", 4), (f"subln_g{l}", 1)]
    at, out = 0, {}
    for name, n in sizes:
        out[name] = (at, n)
        at += n
    return out, at


COLS, NVEC = column_map()
N_CONST = 4 + EXPERTS


class Count:

    def __init__(self, sem):
        self.sem = sem
        self.base = 0

    def at(self, k):
        return self.base + k

    def passed(self, k):
        self.base += k


class Steps:

    def __init__(self, eng, count, start=0):
        self.eng, self.count, self.k, self.start = eng, count, 0, start

    def then(self, ins):
        ins.then_inc(self.count.sem, 1)
        self.k += 1
        self.eng.wait_ge(self.count.sem, self.start + self.count.at(self.k))


class Core:

    def __init__(self, nc, ctx):
        self.nc, self.ctx = nc, ctx
        self.counts = {}
        self.bank = [ctx.enter_context(nc.psum_tensor(f"bank{i}", [P, 512], F32)) for i in range(8)]
        self.slot = [ctx.enter_context(nc.sbuf_tensor(f"slot{u}", [P, C, P], F32)) for u in range(U)]
        self.landed = [self.count(f"tile_landed_{u}") for u in range(U)]
        self.tiles_used = self.count("tiles_used")
        self.bank_free = self.count("bank_free")
        self.pair_free = self.count("pair_free")

    def sb(self, ctx, name, shape, dt=F32):
        return ctx.enter_context(self.nc.sbuf_tensor(name, shape, dt))

    def count(self, name):
        if name not in self.counts:
            self.counts[name] = Count(self.ctx.enter_context(self.nc.semaphore(name)))
        return self.counts[name]

    def load_tile(self, sp, u, tile):
        sp.dma_start(self.slot[u][:].rearrange("p c m -> p (c m)"), tile).then_inc(self.landed[u].sem, 16)


def project(core, tiles, T, products, evacuate, next_tiles, engine="vector", done="tiles_out"):
    nc = core.nc
    used, free = core.tiles_used, core.bank_free
    rounds = T // U
    with nc.Block() as block:

        @block.sync
        def _(sp):
            if rounds > 1:
                with sp.Fori(1, rounds) as i:
                    for u in range(U):
                        sp.wait_ge(used.sem, used.at(1 - U) + i * U + u)
                        core.load_tile(sp, u, tiles(i * U + u))
            for u in range(U):
                sp.wait_ge(used.sem, used.at(T - U + u + 1))
                if next_tiles is not None:
                    core.load_tile(sp, u, next_tiles(u))

        @block.tensor
        def _(pe):
            with pe.Fori(0, rounds) as i:
                for u in range(U):
                    pe.wait_ge(core.landed[u].sem, core.landed[u].at(16) + i * 16)
                    pe.wait_ge(free.sem, free.at(u + 1) + i * U)
                    products(pe, i * U + u, u).then_inc(used.sem, 1)

        def empty(eng):
            with eng.Fori(0, rounds) as i:
                for u in range(U):
                    eng.wait_ge(used.sem, used.at(u + 1) + i * U)
                    evacuate(eng, i * U + u, u).then_inc(free.sem, 1)

        if engine == "vector":
            block.vector(empty)
        else:
            block.scalar(empty)
    used.passed(T)
    free.passed(T)
    for u in range(U):
        core.landed[u].passed(16 * rounds)


def feature_products(core, moving, lo, n):

    def products(pe, t, u):
        for c in range(C):
            last = core.nc.tensor.matmul(core.bank[u][:, 0:n], core.slot[u][:, c, :], moving[:, c, lo:lo + n],
                                         start=(c == 0), stop=(c == C - 1))
        return last

    return products


def norm(core, x, n, out, centre, groups, xc, sq):
    nc = core.nc
    mean_ready, centred, squared = core.count("mean_ready"), core.count("centred"), core.count("squared")
    var_ready, std_ready = core.count("var_ready"), core.count("std_ready")
    scaled, shifted, own = core.count("scaled"), core.count("shifted"), core.count("norm_vector_steps")
    mean, var, std, rstd = core.bank[4], core.bank[5], core.std, core.rstd
    src = xc if centre else x
    n_scaled = C * len(groups)
    with nc.Block() as block:

        @block.tensor
        def _(pe):
            if centre:
                for c in range(C):
                    last = nc.tensor.matmul(mean[:, 0:n], core.avg[:], x[:, c, 0:n], start=(c == 0), stop=(c == C - 1))
                last.then_inc(mean_ready.sem, 1)
            for c in range(C):
                pe.wait_ge(squared.sem, squared.at(c + 1))
                last = nc.tensor.matmul(var[:, 0:n], core.avg[:], sq[:, c, 0:n], start=(c == 0), stop=(c == C - 1))
            last.then_inc(var_ready.sem, 1)

        @block.vector
        def _(dve):
            steps = Steps(dve, own)
            if centre:
                dve.wait_ge(mean_ready.sem, mean_ready.at(1))
                for c in range(C):
                    nc.vector.tensor_tensor(xc[:, c, 0:n], x[:, c, 0:n], mean[:, 0:n], ALU.subtract)\
                        .then_inc(centred.sem, 1)
            dve.wait_ge(std_ready.sem, std_ready.at(1))
            if centre:
                dve.wait_ge(centred.sem, centred.at(C))
            steps.then(nc.vector.reciprocal(rstd[:, 0:n], std[:, 0:n]))
            for lo, hi, gain, shift in groups:
                for c in range(C):
                    nc.vector.scalar_tensor_tensor(out[:, c, lo:hi], src[:, c, lo:hi], gain[:, c:c + 1],
                                                   rstd[:, lo:hi], ALU.mult, ALU.mult).then_inc(scaled.sem, 1)

        @block.scalar
        def _(act):
            for c in range(C):
                if centre:
                    act.wait_ge(centred.sem, centred.at(c + 1))
                nc.scalar.activation(sq[:, c, 0:n], src[:, c, 0:n], ACT.Square).then_inc(squared.sem, 1)
            act.wait_ge(var_ready.sem, var_ready.at(1))
            nc.scalar.activation(std[:, 0:n], var[:, 0:n], ACT.Sqrt, bias=core.col("eps", 0)).then_inc(std_ready.sem, 1)
            k = 0
            for lo, hi, gain, shift in groups:
                for c in range(C):
                    k += 1
                    if shift is not None:
                        act.wait_ge(scaled.sem, scaled.at(k))
                        nc.scalar.activation(out[:, c, lo:hi], out[:, c, lo:hi], ACT.Identity, bias=shift[:, c:c + 1])\
                            .then_inc(shifted.sem, 1)

    mean_ready.passed(1 if centre else 0)
    centred.passed(C if centre else 0)
    squared.passed(C)
    var_ready.passed(1)
    std_ready.passed(1)
    own.passed(1)
    scaled.passed(n_scaled)
    shifted.passed(sum(C for g in groups if g[3] is not None))


def modulation(core, a):
    nc = core.nc
    used = core.tiles_used
    S = 6
    summed, column, added, silued, own = (core.count(n) for n in ("mod_rows_summed", "mod_columns_made", "mod_added", "vector_silu", "mod_vector_steps"))
    with ExitStack() as ctx:
        cs = core.sb(ctx, "cs", [P, C, 2])
        acc = core.sb(ctx, "acc", [P, 2, 2, D])
        ones = core.sb(ctx, "ones_col", [P, 2])
        with nc.Block() as block:

            @block.sync
            def _(sp):
                with sp.Fori(1, S * C // U) as i:
                    for u in range(U):
                        sp.wait_ge(used.sem, used.at(1 - U) + i * U + u)
                        core.load_tile(sp, u, a["w_ada"][i * U + u])
                for u in range(U):
                    sp.wait_ge(used.sem, used.at(S * C - U + u + 1))
                    core.load_tile(sp, u, a["w_in"][u])

            @block.scalar
            def _(act):
                nc.scalar.activation(cs[:].rearrange("p c n -> p (c n)"), core.vcols("c"), ACT.Silu).then_inc(silued.sem, 1)
                nc.scalar.activation(core.c2s[:].rearrange("p c n -> p (c n)"), core.vcols("c_2"), ACT.Silu).then_inc(silued.sem, 1)

            def round_(dve, i, vectors, s0):
                k = 0
                for w in range(2):
                    if not isinstance(i, int):
                        dve.wait_ge(column.sem, column.at(w + 1) + i * 2 - 2)
                    for c in range(C):
                        t = w * C + c
                        dve.wait_ge(core.landed[t % U].sem, core.landed[t % U].at(16 * (t // U + 1)) + i * (16 * 4))
                        src = core.slot[t % U][:].rearrange("p c m -> p (c m)")
                        for j in range(vectors):
                            if c > 0:
                                dve.wait_ge(own.sem, own.at(s0 + k - vectors + 1) + i * (16 * vectors))
                            if c == 0:
                                ins = nc.vector.tensor_scalar(acc[:, w, j, :], src, cs[:, c, j:j + 1], None, ALU.mult)
                            else:
                                ins = nc.vector.scalar_tensor_tensor(acc[:, w, j, :], src, cs[:, c, j:j + 1], acc[:, w, j, :], ALU.mult, ALU.add)
                            ins.then_inc(own.sem, 1)
                            k += 1
                        dve.wait_ge(own.sem, own.at(s0 + k) + i * (16 * vectors))
                        dve.sem_inc(used.sem, 1)
                    dve.sem_inc(summed.sem, 1)

            @block.vector
            def _(dve):
                nc.vector.memset(ones[:], 1.0).then_inc(added.sem, 1)
                dve.wait_ge(silued.sem, silued.at(1))
                round_(dve, 0, 2, 0)
                with dve.Fori(1, S // 2) as i:
                    round_(dve, i, 1, 16)
                dve.wait_ge(column.sem, column.at(S))
                nc.vector.tensor_tensor(core.mod[:, 0:16, :], core.bank[0][:, 0:32].rearrange("p (t n) -> p t n", n=2),
                                        core.vcols("b_ada")[:, 0:16].rearrange("p (t n) -> p t n", n=1).broadcast_to([P, 16, 2]), ALU.add)\
                    .then_inc(added.sem, 1)
                nc.vector.tensor_tensor(core.mod[:, 16:48, 0], core.bank[1][:, 0:32], core.vcols("b_ada")[:, 16:48], ALU.add)\
                    .then_inc(added.sem, 1)
                dve.wait_ge(added.sem, added.at(3))
                nc.vector.tensor_scalar(core.mod[:, 8:16, :], core.mod[:, 8:16, :], 1.0, None, ALU.add).then_inc(added.sem, 1)
                nc.vector.tensor_scalar(core.mod[:, 32:40, 0], core.mod[:, 32:40, 0], 1.0, None, ALU.add).then_inc(added.sem, 1)

            @block.tensor
            def _(pe):
                pe.wait_ge(added.sem, added.at(1))
                for w in range(2):
                    pe.wait_ge(summed.sem, summed.at(w + 1))
                    for m in range(C):
                        for j in range(2):
                            t = 2 * (w * C + m) + j
                            last = nc.tensor.matmul(core.bank[0][:, t:t + 1], acc[:, w, j, m * P:m * P + P], ones[:, 0:1], start=True, stop=True)
                    last.then_inc(column.sem, 1)
                with pe.Fori(1, S // 2) as i:
                    for w in range(2):
                        pe.wait_ge(summed.sem, summed.at(w + 1) + i * 2)
                        for m in range(C):
                            last = nc.tensor.matmul(core.bank[1][:, bass.ds((i - 1) * (2 * C) + w * C + m, 1)], acc[:, w, 0, m * P:m * P + P], ones[:, 0:1],
                                                    start=True, stop=True)
                        last.then_inc(column.sem, 1)
    used.passed(S * C)
    silued.passed(2)
    summed.passed(S)
    column.passed(S)
    added.passed(5)
    own.passed(32 + 32)
    for u in range(U):
        core.landed[u].passed(16 * S * C // U)


def gates(core, z, la, k_f, k_b, zt, lb):
    nc = core.nc
    own_a, own_v = core.count("gates_scalar_steps"), core.count("gates_vector_steps")
    soft, ls_ready, diff, keyed = (core.count(x) for x in ("softplus_ready", "log_sigmoid_ready", "key_log_ready", "keys_ready"))
    bound, lse = core.count("bounds_ready"), core.count("excess_ready")
    zf = z[:].rearrange("p s t n -> p (s t n)")
    tf = zt[:].rearrange("p s t n -> p (s t n)")
    lf = la[:].rearrange("p s t n -> p (s t n)")
    one = core.col("one", 0)
    hg = [(s, t) for s in range(2) for t in (0, 1, 2, 3, 6, 7, 8, 9)]
    lbv, lbe, log_lb, log_1mlb, lb_gap, lbt = (lb[:, 8 * i:8 * i + 8] for i in range(6))
    which = {t: j for j, t in enumerate((0, 1, 2, 3, 6, 7, 8, 9))}
    with nc.Block() as block:

        @block.vector
        def _(dve):
            steps = Steps(dve, own_v)
            steps.then(nc.vector.tensor_tensor(lbv, core.vcols("lb"), core.vcols("lb"), ALU.subtract))
            nc.vector.tensor_copy(lbt, lbv).then_inc(bound.sem, 1)
            dve.wait_ge(own_a.sem, own_a.at(1))
            steps.then(nc.vector.reciprocal(lbv, lbe))
            steps.then(nc.vector.tensor_tensor(lbv, lbv, lbe, ALU.mult))
            steps.then(nc.vector.tensor_tensor(lbv, lbv, lbv, ALU.subtract))
            steps.then(nc.vector.tensor_scalar(lbv, lbv, 0.0, 1.0 - 1e-6, ALU.max, ALU.min))
            nc.vector.tensor_scalar(lbt, lbv, LB_FLOOR, None, ALU.max).then_inc(bound.sem, 1)
            dve.wait_ge(own_a.sem, own_a.at(3))
            steps.then(nc.vector.tensor_scalar(log_lb, log_lb, 60.0 * LN2, None, ALU.subtract))
            nc.vector.tensor_tensor(lb_gap, log_1mlb, log_lb, ALU.subtract).then_inc(bound.sem, 1)
            dve.wait_ge(soft.sem, soft.at(1))
            nc.vector.scalar_tensor_tensor(lf, zf, 0.0, tf, ALU.min, ALU.subtract).then_inc(ls_ready.sem, 1)
            dve.wait_ge(ls_ready.sem, ls_ready.at(1))
            nc.vector.tensor_tensor(zf, lf, zf, ALU.subtract).then_inc(diff.sem, 1)
            dve.wait_ge(lse.sem, lse.at(1))
            for s, t in hg:
                j = which[t]
                ins = nc.vector.tensor_scalar(la[:, s, t, :], la[:, s, t, :], log_1mlb[:, j:j + 1], log_lb[:, j:j + 1],
                                              ALU.add, ALU.max)
            steps.then(ins)
            for s in range(2):
                for t in (0, 6):
                    nc.vector.tensor_tensor(la[:, s, t:t + 4, :], la[:, s, t:t + 4, :], zt[:, s, t:t + 4, :], ALU.add)
                    ins = nc.vector.tensor_scalar(la[:, s, t + 4:t + 6, :], la[:, s, t + 4:t + 6, :], 1.0 / 16.0, None, ALU.mult)
            steps.then(ins)

        @block.scalar
        def _(act):
            steps = Steps(act, own_a)
            act.wait_ge(bound.sem, bound.at(1))
            steps.then(nc.scalar.activation(lbe, lbt, ACT.Exp))
            act.wait_ge(bound.sem, bound.at(2))
            steps.then(nc.scalar.activation(log_lb, lbt, ACT.Ln, scale=2.0 ** 60))
            steps.then(nc.scalar.activation(log_1mlb, lbv, ACT.Ln, scale=-1.0, bias=one))
            steps.then(nc.scalar.activation(tf, zf, ACT.Abs))
            steps.then(nc.scalar.activation(tf, tf, ACT.Exp, scale=-1.0))
            nc.scalar.activation(tf, tf, ACT.Ln, bias=one).then_inc(soft.sem, 1)
            act.wait_ge(bound.sem, bound.at(3))
            act.wait_ge(diff.sem, diff.at(1))
            for s, t in hg:
                j = which[t]
                ins = nc.scalar.activation(zt[:, s, t, :], la[:, s, t, :], ACT.Abs, bias=lb_gap[:, j:j + 1])
                keys = k_f if t < 6 else k_b
                nc.scalar.activation(keys[:, s, t % 6, :], z[:, s, t, :], ACT.Exp, bias=log_1mlb[:, j:j + 1])\
                    .then_inc(keyed.sem, 1)
            act.wait_ge(keyed.sem, keyed.at(16))
            steps.then(nc.scalar.activation(tf, tf, ACT.Exp, scale=-1.0))
            nc.scalar.activation(tf, tf, ACT.Ln, bias=one).then_inc(lse.sem, 1)
    own_a.passed(6)
    own_v.passed(8)
    for s, k in ((soft, 1), (ls_ready, 1), (diff, 1), (keyed, 16), (bound, 3), (lse, 1)):
        s.passed(k)


def kernel_program(nc, a):
    with ExitStack() as ctx:
        core = Core(nc, ctx)
        vec = core.sb(ctx, "vec", [P, NVEC])
        const = core.sb(ctx, "const", [P, N_CONST, P])
        core.avg = core.sb(ctx, "avg", [P, P])
        core.avg_head = core.sb(ctx, "avg_head", [P, P])
        core.std = core.sb(ctx, "std", [P, L])
        core.rstd = core.sb(ctx, "rstd", [P, L])
        core.zeros = core.sb(ctx, "zeros", [P, 512])
        core.vcols = lambda name: vec[:, COLS[name][0]:COLS[name][0] + COLS[name][1]]
        core.col = lambda name, j: vec[:, COLS[name][0] + j:COLS[name][0] + j + 1]
        core.ident = const[:, 0, :]
        core.rot = const[:, 1, :]
        core.iota = const[:, 2, :]
        core.sel = const[:, 3:3 + EXPERTS, :]
        core.before = const[:, 3 + EXPERTS, :]
        core.x1 = core.sb(ctx, "x1", [P, C, N])
        core.mod = core.sb(ctx, "mod", [P, 48, 2])
        core.mod2 = core.sb(ctx, "mod2", [P, DEPTH_2 * 48, 1])
        core.h = core.sb(ctx, "h", [P, C, N])
        core.c2s = core.sb(ctx, "c2s", [P, C, 1])
        start(core, a, vec, const)
        modulation(core, a)
        first_mixer(core, a)
        retrieval(core, a)
        second_block(core, a)


def start(core, a, vec, const):
    nc = core.nc
    loaded, filled = core.count("start_loaded"), core.count("start_filled")
    with nc.Block() as block:

        @block.sync
        def _(sp):
            sp.dma_start(vec[:], a["vec"]).then_inc(loaded.sem, 16)
            for u in range(U):
                core.load_tile(sp, u, a["w_ada"][u])
            sp.dma_start(const[:], a["const"].rearrange("b p n -> p b n")).then_inc(loaded.sem, 16)
            sp.wait_ge(loaded.sem, 32)

        @block.vector
        def _(dve):
            nc.vector.memset(core.avg[:], 1.0 / D).then_inc(filled.sem, 1)
            nc.vector.memset(core.avg_head[:], 1.0 / P).then_inc(filled.sem, 1)
            nc.vector.memset(core.zeros[:], 0.0).then_inc(filled.sem, 1)
            dve.wait_ge(filled.sem, 3)
            dve.sem_inc(core.bank_free.sem, U)
            dve.sem_inc(core.pair_free.sem, 2)
    loaded.passed(32)
    filled.passed(3)


def swap_grid(ap):
    return ap.rearrange("p t (r c) -> p t c r", c=GRID_W)


def as_grid(ap):
    return ap.rearrange("p t (c r) -> p t c r", r=ROWS)


def first_mixer(core, a):
    nc = core.nc
    with ExitStack() as ctx:
        sb = lambda name, shape, dt=F32: core.sb(ctx, name, shape, dt)
        v_a = sb("v_a", [P, 4, 512])
        v_b = sb("v_b", [P, 4, 512])
        lat = sb("lat", [P, 12, N])
        k_f = sb("k_f", [P, 2, 6, N])
        k_b = sb("k_b", [P, 2, 6, N])
        q = sb("q", [P, 6, N])
        la = sb("la", [P, 2, 12, N])
        with ExitStack() as c1:
            z = core.sb(c1, "z", [P, 2, 12, N])
            with ExitStack() as c2:
                x = core.sb(c2, "x", [P, C, L])
                s2 = core.sb(c2, "s2", [P, C, L])
                mixer_inputs(core, a, x, s2, z, v_a, v_b, lat, k_f, k_b, q)
            with ExitStack() as c3:
                zt = core.sb(c3, "zt", [P, 2, 12, N])
                lb = core.sb(c3, "lb_cols", [P, 48])
                gates(core, z, la, k_f, k_b, zt, lb)
        b = sb("b", [P, 2, 12, N])
        o = core.x1
        st = sb("state", [P, 2, 2, 6, P])
        running_sums(core, la, b)
        with ExitStack() as c4:
            states(core, c4, a, k_f, k_b, b, v_a, v_b, st, la)
        with ExitStack() as c5:
            scores = core.sb(c5, "scores", [P, 16, P])
            chunk_scores(core, c5, a, q, k_f, k_b, b, scores, la)
            mixer_outputs(core, q, b, st, v_a, v_b, scores, o, la)
        mix = sb("mix", [P, 8, N])
        with ExitStack() as c6:
            head_norms(core, c6, o, lat, mix)
        xl = sb("xl", [P, C, N])
        pre = core.h
        tmp = sb("tmp", [P, U, N])
        add_residual(core, a, "w_out", mix, xl, pre, tmp, lambda t: core.mod[:, bass.ds(t + 16, 1), 0],
                     lambda u: a["w_query"][u], load_x=a["x"][:, :, NC:L], alpha=ALPHA)
        xc = sb("xc1", [P, C, N])
        norm(core, pre, N, core.x1, True, [(0, N, core.vcols("ln_gamma0"), core.vcols("ln_beta0"))], xc, pre)


def add_residual(core, a, w, moving, x, out, tmp, gate, next_tiles, load_x=None, alpha=None):
    nc = core.nc
    own = core.count("residual_gated")
    base = own.base
    if load_x is not None:
        loaded = core.count("residual_loaded")
        with nc.Block() as block:

            @block.sync
            def _(sp):
                sp.dma_start(x[:], load_x).then_inc(loaded.sem, 16)
                sp.wait_ge(loaded.sem, loaded.at(16))
        loaded.passed(16)

    def evacuate(dve, t, u):
        nc.vector.tensor_scalar(tmp[:, u, :], core.bank[u][:, 0:N], gate(t), None, ALU.mult).then_inc(own.sem, 1)
        dve.wait_ge(own.sem, base + t + 1)
        return nc.vector.scalar_tensor_tensor(out[:, bass.ds(t, 1), :], x[:, bass.ds(t, 1), :],
                                              1.0 if alpha is None else alpha,
                                              tmp[:, u:u + 1, :], ALU.mult, ALU.add)

    project(core, lambda t: a[w][t], C, feature_products(core, moving, 0, N), evacuate, next_tiles)
    own.passed(C)


def mixer_inputs(core, a, x, s2, z, v_a, v_b, lat, k_f, k_b, q):
    nc = core.nc
    with ExitStack() as ctx:
        sb = lambda name, shape, dt=F32: core.sb(ctx, name, shape, dt)
        rank_w = sb("rank_w", [P, C, 32])
        gk2 = sb("gk2", [16, 2, 256])
        rank = sb("rank", [16, 2, L])
        loaded = core.count("mixer_loaded")
        with nc.Block() as block:

            @block.sync
            def _(sp):
                sp.dma_start(x[:], a["x"]).then_inc(loaded.sem, 16)
                sp.dma_start(rank_w[:], a["w_rank"]).then_inc(loaded.sem, 16)
                sp.dma_start(gk2[:], a["w_gk2"]).then_inc(loaded.sem, 16)
                sp.wait_ge(loaded.sem, loaded.at(48))

        loaded.passed(48)
        gain = [core.mod[:, 8:16, j] for j in range(2)]
        shift = [core.mod[:, 0:8, j] for j in range(2)]
        norm(core, x, L, x, True, [(0, NC, gain[1], shift[1]), (NC, L, gain[0], shift[0])], x, s2)
        h = x

        def to_z(dve, t, u):
            return nc.vector.tensor_copy(s2[:, bass.ds(t, 1), :], core.bank[u][:, :].rearrange("p (o n) -> p o n", o=1))

        zz = s2
        project(core, lambda t: a["w_in"][t], 8, feature_products(core, h, 0, L), to_z, lambda u: a["w_in"][8 + u])
        own = core.count("inputs_spread")
        with nc.Block() as block:

            @block.vector
            def _(dve):
                for d in range(2):
                    for s in range(2):
                        nc.vector.tensor_copy(z[:, s, 6 * d:6 * d + 4, :], zz[:, 4 * d:4 * d + 4, s * NC:s * NC + N])\
                            .then_inc(own.sem, 1)
        own.passed(4)

        def to_kq(dve, t, u):
            return nc.vector.tensor_copy(s2[:, bass.ds(t, 1), :], core.bank[u][:, :].rearrange("p (o n) -> p o n", o=1))

        project(core, lambda t: a["w_in"][t + 8], 4, feature_products(core, h, 0, L), to_kq, lambda u: a["w_in"][12 + u])
        with nc.Block() as block:

            @block.vector
            def _(dve):
                for k in (k_f, k_b):
                    nc.vector.tensor_copy(k[:, 0, 4:6, :], s2[:, 0:2, 0:NC]).then_inc(own.sem, 1)
                    for j in range(2):
                        nc.vector.tensor_copy(as_grid(k[:, 1, 4 + j:5 + j, :]), swap_grid(s2[:, j:j + 1, NC:L])).then_inc(own.sem, 1)
                for j in range(2):
                    nc.vector.tensor_scalar(as_grid(q[:, 4 + j:5 + j, :]), swap_grid(s2[:, 2 + j:3 + j, NC:L]), 0.125, None, ALU.mult)\
                        .then_inc(own.sem, 1)
        own.passed(8)

        def to_lat(dve, t, u):
            return nc.vector.tensor_copy(lat[:, bass.ds(t, 1), :], core.bank[u][:, 0:N].rearrange("p (o n) -> p o n", o=1))

        project(core, lambda t: a["w_in"][t + 12], 12, feature_products(core, h, NC, N), to_lat, lambda u: a["w_in"][24 + u])

        def token_products(src):
            def products(pe, t, u):
                for tt in range(4):
                    for c in range(C):
                        last = nc.tensor.matmul(core.bank[u][:, tt * P:tt * P + P], src[:, c, tt * P:tt * P + P],
                                                core.slot[u][:, c, :], start=(c == 0), stop=(c == C - 1))
                return last
            return products

        def to_values(v):
            def evacuate(dve, t, u):
                return nc.vector.tensor_copy(v[:, :, bass.ds(t * P, P)], core.bank[u][:, :].rearrange("p (t n) -> p t n", t=4))
            return evacuate

        project(core, lambda t: a["w_in"][t + 24], 4, token_products(h), to_values(v_a), lambda u: a["w_in"][28 + u])

        rank_ready, spread = core.count("rank_ready"), core.count("rank_spread")
        gated = core.count("gate_inputs")
        with nc.Block() as block:

            @block.tensor
            def _(pe):
                for d in range(2):
                    for c in range(C):
                        last = nc.tensor.matmul(core.bank[4 + d][0:16, :], rank_w[:, c, 16 * d:16 * d + 16], h[:, c, :],
                                                start=(c == 0), stop=(c == C - 1))
                    last.then_inc(rank_ready.sem, 1)
                pe.wait_ge(spread.sem, spread.at(4))
                for d in range(2):
                    for j in range(2):
                        nc.tensor.matmul(core.bank[4 + 2 * d + j][:, :], gk2[:, d, j * P:j * P + P], rank[:, d, :],
                                         start=True, stop=True).then_inc(gated.sem, 1)

            @block.vector
            def _(dve):
                for d in range(2):
                    dve.wait_ge(rank_ready.sem, rank_ready.at(d + 1))
                    nc.vector.tensor_copy(rank[:, d, 0:NC], core.bank[4 + d][0:16, 0:NC]).then_inc(spread.sem, 1)
                    nc.vector.tensor_copy(as_grid(rank[:, d:d + 1, NC:L]),
                                          swap_grid(core.bank[4 + d][0:16, NC:L].rearrange("p (o n) -> p o n", o=1)))\
                        .then_inc(spread.sem, 1)
                for d in range(2):
                    for j in range(2):
                        dve.wait_ge(gated.sem, gated.at(2 * d + j + 1))
                        for s in range(2):
                            nc.vector.tensor_scalar(z[:, s, 6 * d + 4 + j, :], core.bank[4 + 2 * d + j][:, s * NC:s * NC + N],
                                                    core.col("b_gk", 2 * d + j), None, ALU.add).then_inc(own.sem, 1)
                nc.vector.tensor_copy(s2[:, :, 0:NC], h[:, :, 0:NC]).then_inc(own.sem, 1)
                for c in range(C):
                    nc.vector.tensor_copy(as_grid(s2[:, c:c + 1, NC:L]), swap_grid(h[:, c:c + 1, NC:L])).then_inc(own.sem, 1)

            @block.scalar
            def _(act):
                nc.scalar.activation(q[:, 0:4, :], lat[:, 0:4, :], ACT.Copy).then_inc(core.count("queries_copied").sem, 1)
        core.count("queries_copied").passed(1)
        rank_ready.passed(2)
        spread.passed(4)
        gated.passed(4)
        own.passed(17)
        project(core, lambda t: a["w_in"][t + 28], 4, token_products(s2), to_values(v_b), lambda u: a["w_out"][u])


def running_sums(core, la, b):
    nc = core.nc
    with ExitStack() as ctx:
        keep = core.sb(ctx, "keep", [P, 6 * N])
        filled, summed = core.count("keep_filled"), core.count("sums_ready")
        with nc.Block() as block:

            @block.vector
            def _(dve):
                nc.vector.memset(keep[:], 1.0).then_inc(filled.sem, 1)
                dve.wait_ge(filled.sem, filled.at(1))
                nc.vector.memset(keep[:].rearrange("p (k n) -> p k n", n=CH)[:, :, 0:1], 0.0).then_inc(filled.sem, 1)
                dve.wait_ge(filled.sem, filled.at(2))
                for s in range(2):
                    src = la[:, s, 0:6, :].rearrange("p t n -> p (t n)")
                    dst = b[:, s, 0:6, :].rearrange("p t n -> p (t n)")
                    nc.vector.tensor_tensor_scan(dst, keep[:], src, 0.0, ALU.mult, ALU.add).then_inc(summed.sem, 1)
                    src = la[:, s, 6:12, :].rearrange("p t n -> p (t n)")
                    dst = b[:, s, 6:12, :].rearrange("p t n -> p (t n)")
                    nc.vector.tensor_tensor_scan(dst[:, ::-1], keep[:], src[:, ::-1], 0.0, ALU.mult, ALU.add).then_inc(summed.sem, 1)
        filled.passed(2)
        summed.passed(4)


def states(core, ctx, a, k_f, k_b, b, v_a, v_b, st, kd):
    nc = core.nc
    sb = lambda name, shape, dt=F32: core.sb(ctx, name, shape, dt)
    kt = sb("kt", [P, 2, 3, 6, P])
    end = sb("end", [P, 2, 2, 6, 2])
    work = sb("state_work", [P, 2, 6, P])
    gaps, decays, keyed = core.count("gaps_ready"), core.count("end_decays_ready"), core.count("decayed_keys")
    turned, kt_ready, grown = core.count("keys_turned"), core.count("turned_keys_ready"), core.count("growth_ready")
    stepped = core.count("states_stepped")
    keys = (k_f, k_b)
    met = (((0, 0), (0, 1), (1, 0)), ((0, 1), (0, 0), (1, 1)))

    def by_chunk(t, s, d):
        return t[:, s, 6 * d:6 * d + 6, :].rearrange("p t (c n) -> p (t c) n", n=CH)

    with nc.Block() as block:

        @block.vector
        def _(dve):
            for d in range(2):
                e = CH - 1 if d == 0 else 0
                for s in range(2):
                    last = by_chunk(b, s, d)[:, :, e:e + 1]
                    nc.vector.tensor_copy(end[:, s, d, :, :].rearrange("p t c -> p (t c)"), last).then_inc(gaps.sem, 1)
                    nc.vector.tensor_tensor(by_chunk(kd, s, d), last.broadcast_to([P, 12, CH]), by_chunk(b, s, d), ALU.subtract)\
                        .then_inc(gaps.sem, 1)
            for d in range(2):
                for s in range(2):
                    dve.wait_ge(decays.sem, decays.at(2 * d + s + 1))
                    nc.vector.tensor_tensor(kd[:, s, 6 * d:6 * d + 6, :], kd[:, s, 6 * d:6 * d + 6, :], keys[d][:, s, :, :], ALU.mult)\
                        .then_inc(keyed.sem, 1)
            n = 0
            for i in range(3):
                for d in range(2):
                    for half in range(2):
                        n += 1
                        dve.wait_ge(turned.sem, turned.at(n))
                        nc.vector.tensor_copy(kt[:, d, i, 3 * half:3 * half + 3, :],
                                              core.bank[(n - 1) % 4][:, 0:3 * P].rearrange("p (t n) -> p t n", n=P))\
                            .then_inc(kt_ready.sem, 1)
            k = 0
            for i in range(3):
                for d in range(2):
                    dve.wait_ge(grown.sem, grown.at(2 * i + d + 1))
                    if i > 0:
                        dve.wait_ge(stepped.sem, stepped.at(k))
                    s, c = met[d][i]
                    x, y = core.bank[4 + 2 * d], core.bank[5 + 2 * d]
                    before = work[:, d] if i == 1 else st[:, d, 0]
                    after = work[:, d] if i == 0 else st[:, d, i - 1]
                    parts = [(slice(0, P), t, x[:, t * P:t * P + P]) for t in range(4)]
                    parts += [(slice(64 * r, 64 * r + 64), 4 + j, y[64 * r:64 * r + 64, 256 * j + 128 * r:256 * j + 128 * r + 128])
                              for j in range(2) for r in range(2)]
                    for rows, t, new in parts:
                        if i == 0:
                            ins = nc.vector.tensor_copy(after[rows, t, :], new)
                        else:
                            ins = nc.vector.scalar_tensor_tensor(after[rows, t, :], before[rows, t, :], end[rows, s, d, t, c:c + 1],
                                                                 new, ALU.mult, ALU.add)
                        ins.then_inc(stepped.sem, 1)
                        k += 1

        @block.scalar
        def _(act):
            for d in range(2):
                for s in range(2):
                    act.wait_ge(gaps.sem, gaps.at(4 * d + 2 * s + 2))
                    nc.scalar.activation(end[:, s, d, :, :], end[:, s, d, :, :], ACT.Exp)
                    nc.scalar.activation(kd[:, s, 6 * d:6 * d + 6, :], kd[:, s, 6 * d:6 * d + 6, :], ACT.Exp).then_inc(decays.sem, 1)

        @block.tensor
        def _(pe):
            pe.wait_ge(keyed.sem, keyed.at(4))
            n = 0
            for i in range(3):
                for d in range(2):
                    s, c = met[d][i]
                    for half in range(2):
                        if n >= 4:
                            pe.wait_ge(kt_ready.sem, kt_ready.at(n - 3))
                        for j in range(3):
                            t = 3 * half + j
                            last = nc.tensor.transpose(core.bank[n % 4][:, j * P:j * P + P],
                                                       kd[:, s, 6 * d + t, c * CH:c * CH + CH], core.ident)
                        last.then_inc(turned.sem, 1)
                        n += 1
            for i in range(3):
                for d in range(2):
                    s, c = met[d][i]
                    tt = 2 * s + c
                    pe.wait_ge(kt_ready.sem, kt_ready.at(4 * i + 2 * d + 2))
                    if i > 0:
                        pe.wait_ge(stepped.sem, stepped.at(8 * (2 * (i - 1) + d + 1)))
                    for t in range(4):
                        nc.tensor.matmul(core.bank[4 + 2 * d][:, t * P:t * P + P], kt[:, d, i, t, :], v_a[:, tt, t * P:t * P + P],
                                         start=True, stop=True)
                    for j in range(2):
                        last = nc.tensor.matmul(core.bank[5 + 2 * d][:, 256 * j:256 * j + 256], kt[:, d, i, 4 + j, :],
                                                v_b[:, tt, 256 * j:256 * j + 256], start=True, stop=True)
                    last.then_inc(grown.sem, 1)
    for s, k in ((gaps, 8), (decays, 4), (keyed, 4), (turned, 12), (kt_ready, 12), (grown, 6), (stepped, 48)):
        s.passed(k)


def chunk_scores(core, ctx, a, q, k_f, k_b, b, scores, la):
    nc = core.nc
    sb = lambda name, shape, dt=F32: core.sb(ctx, name, shape, dt)
    mask = sb("mask", [P, LEVELS + 1, P], I32)
    df, db = (la[:, s].rearrange("p (w t) n -> p w (t n)", w=2) for s in range(2))
    ql = sb("ql", [P, 2, 6, N])
    kl = sb("kl", [P, 2, 6, N])
    loaded = core.count("mask_loaded")
    gaps, factors, sided = core.count("level_gaps"), core.count("level_factors"), core.count("level_sided")
    made, kept = core.count("level_products"), core.count("level_kept")
    bf = b[:, 1, 0:6, :].rearrange("p t n -> p (t n)")
    bb = b[:, 1, 6:12, :].rearrange("p t n -> p (t n)")
    qf = q[:].rearrange("p t n -> p (t n)")
    kf = k_f[:, 1].rearrange("p t n -> p (t n)")
    kb = k_b[:, 1].rearrange("p t n -> p (t n)")
    flat = lambda t, w: t[:, w].rearrange("p t n -> p (t n)")

    def halves(ap, h):
        return ap.rearrange("p (n two h) -> p n two h", two=2, h=h)

    with nc.Block() as block:

        @block.sync
        def _(sp):
            sp.dma_start(mask[:], a["mask"].rearrange("l p n -> p l n")).then_inc(loaded.sem, 16)
            sp.wait_ge(loaded.sem, loaded.at(16))

        def keep(dve, l):
            if l == 0:
                dve.wait_ge(loaded.sem, loaded.at(16))
            else:
                dve.wait_ge(kept.sem, kept.at(4 * l))
            dve.wait_ge(made.sem, made.at(l + 1))
            for g in range(4):
                nc.vector.copy_predicated(scores[:, 4 * g:4 * g + 4, :],
                                          mask[:, l:l + 1, :].broadcast_to([P, 4, P]),
                                          core.bank[4 * (l % 2) + g][:, :].rearrange("p (g n) -> p g n", n=P))\
                    .then_inc(kept.sem, 1)

        @block.vector
        def _(dve):
            def gap(l):
                h, w = 1 << l, l % 2
                nb = 6 * N // (2 * h)
                blocks = lambda ap: ap.rearrange("p (n m) -> p n m", m=2 * h)
                mid_f = blocks(bf)[:, :, h - 1:h].broadcast_to([P, nb, 2 * h])
                mid_b = blocks(bb)[:, :, h:h + 1].broadcast_to([P, nb, 2 * h])
                nc.vector.tensor_tensor(blocks(df[:, w]), blocks(bf), mid_f, ALU.subtract).then_inc(gaps.sem, 1)
                nc.vector.tensor_tensor(blocks(db[:, w]), blocks(bb), mid_b, ALU.subtract).then_inc(gaps.sem, 1)

            gap(0)
            for l in range(LEVELS + 1):
                w = l % 2
                if l + 1 < LEVELS:
                    if l >= 1:
                        dve.wait_ge(sided.sem, sided.at(4 * l))
                    gap(l + 1)
                if l >= 2:
                    dve.wait_ge(made.sem, made.at(l - 1))
                if l < LEVELS:
                    h = 1 << l
                    dve.wait_ge(factors.sem, factors.at(4 * l + 4))
                    for out, x, f, side in ((ql, qf, df, 1), (ql, qf, db, 0), (kl, kf, df, 0), (kl, kb, db, 1)):
                        nc.vector.tensor_tensor(halves(flat(out, w), h)[:, :, side, :], halves(x, h)[:, :, side, :],
                                                halves(f[:, w], h)[:, :, side, :], ALU.mult).then_inc(sided.sem, 1)
                else:
                    nc.vector.tensor_copy(flat(ql, w), qf).then_inc(sided.sem, 1)
                    nc.vector.tensor_tensor(flat(kl, w), kf, kb, ALU.add).then_inc(sided.sem, 1)
                if l >= 1:
                    keep(dve, l - 1)
            keep(dve, LEVELS)

        @block.scalar
        def _(act):
            for l in range(LEVELS):
                h, w = 1 << l, l % 2
                act.wait_ge(gaps.sem, gaps.at(2 * l + 2))
                for f, side, sign in ((df, 1, 1.0), (df, 0, -1.0), (db, 0, 1.0), (db, 1, -1.0)):
                    v = halves(f[:, w], h)[:, :, side, :]
                    nc.scalar.activation(v, v, ACT.Exp, scale=sign).then_inc(factors.sem, 1)

        @block.tensor
        def _(pe):
            for l in range(LEVELS + 1):
                w = l % 2
                pe.wait_ge(sided.sem, sided.at(4 * l + (4 if l < LEVELS else 2)))
                if l >= 2:
                    pe.wait_ge(kept.sem, kept.at(4 * (l - 1)))
                for place, head in enumerate(PLACED):
                    rows = slice(0, P) if head < 4 else slice(64 * (head % 2), 64 * (head % 2) + 64)
                    t = head if head < 4 else 4 + (head - 4) // 2
                    for c in range(2):
                        j = 2 * place + c
                        last = nc.tensor.matmul(core.bank[4 * w + j // 4][:, (j % 4) * P:(j % 4) * P + P],
                                                kl[rows, w, t, c * CH:c * CH + CH], ql[rows, w, t, c * CH:c * CH + CH],
                                                start=True, stop=True)
                last.then_inc(made.sem, 1)
    loaded.passed(16)
    for s, k in ((gaps, 2 * LEVELS), (factors, 4 * LEVELS), (sided, 4 * LEVELS + 2), (made, LEVELS + 1), (kept, 4 * (LEVELS + 1))):
        s.passed(k)


def mixer_outputs(core, q, b, st, v_a, v_b, scores, o, la):
    nc = core.nc
    qd = la[:, 0].rearrange("p (d t) n -> p d t n", d=2)
    decay, ready, made, out = core.count("query_decay"), core.count("queries_decayed"), core.count("outputs_made"), core.count("outputs_copied")
    with nc.Block() as block:

        @block.scalar
        def _(act):
            for d in range(2):
                nc.scalar.activation(qd[:, d], b[:, 1, 6 * d:6 * d + 6, :], ACT.Exp).then_inc(decay.sem, 1)

        @block.vector
        def _(dve):
            for d in range(2):
                dve.wait_ge(decay.sem, decay.at(d + 1))
                nc.vector.tensor_tensor(qd[:, d], qd[:, d], q[:], ALU.mult).then_inc(ready.sem, 1)
            for g in range(4):
                dve.wait_ge(made.sem, made.at(g + 1))
                src = core.bank[g][:, :].rearrange("p (h n) -> p h n", n=N)
                if g < 2:
                    nc.vector.tensor_copy(o[:, 2 * g:2 * g + 2, :], src).then_inc(out.sem, 1)
                else:
                    for r in range(2):
                        head = PLACED[2 * g + r]
                        nc.vector.tensor_copy(swap_grid(o[:, head:head + 1, :]), as_grid(src[:, r:r + 1, :])).then_inc(out.sem, 1)

        @block.tensor
        def _(pe):
            pe.wait_ge(ready.sem, ready.at(2))
            for place, head in enumerate(PLACED):
                rows = slice(0, P) if head < 4 else slice(64 * (head % 2), 64 * (head % 2) + 64)
                t = head if head < 4 else 4 + (head - 4) // 2
                v = v_a if head < 4 else v_b
                for c in range(2):
                    dst = core.bank[place // 2][:, (place % 2) * N + c * CH:(place % 2) * N + c * CH + CH]
                    nc.tensor.matmul(dst, v[:, 2 + c, (head % 4) * P:(head % 4) * P + P], scores[:, 2 * place + c, :], start=True, stop=False)
                    for d in range(2):
                        step = c if d == 0 else 1 - c
                        last = nc.tensor.matmul(dst, st[rows, d, step, t, :], qd[rows, d, t, c * CH:c * CH + CH],
                                                start=False, stop=(d == 1))
                if place % 2:
                    last.then_inc(made.sem, 1)
    decay.passed(2)
    ready.passed(2)
    made.passed(4)
    out.passed(6)


def head_norms(core, ctx, o, lat, mix):
    nc = core.nc
    sq = core.sb(ctx, "head_sq", [P, 8, N])
    sg = core.sb(ctx, "head_gate", [P, 8, N])
    squared, meant, rooted, own, gated = (core.count(x) for x in ("head_squared", "head_mean", "head_root", "head_vector_steps", "head_gates"))
    with nc.Block() as block:

        @block.scalar
        def _(act):
            nc.scalar.activation(sg[:], lat[:, 4:12, :], ACT.Silu).then_inc(gated.sem, 1)
            for g in range(4):
                nc.scalar.activation(sq[:, 2 * g:2 * g + 2, :], o[:, 2 * g:2 * g + 2, :], ACT.Square).then_inc(squared.sem, 1)
            for g in range(4):
                act.wait_ge(meant.sem, meant.at(g + 1))
                nc.scalar.activation(sq[:, 2 * g:2 * g + 2, :], core.bank[g][:, :].rearrange("p (h n) -> p h n", n=N), ACT.Sqrt,
                                     bias=core.col("eps", 0)).then_inc(rooted.sem, 1)

        @block.tensor
        def _(pe):
            for g in range(4):
                pe.wait_ge(squared.sem, squared.at(g + 1))
                nc.tensor.matmul(core.bank[g][:, :], core.avg_head[:], sq[:, 2 * g:2 * g + 2, :].rearrange("p h n -> p (h n)"),
                                 start=True, stop=True).then_inc(meant.sem, 1)

        @block.vector
        def _(dve):
            steps = Steps(dve, own)
            dve.wait_ge(rooted.sem, rooted.at(4))
            steps.then(nc.vector.reciprocal(sq[:], sq[:]))
            for g in range(2):
                ins = nc.vector.scalar_tensor_tensor(sq[:, 4 * g:4 * g + 4, :], o[:, 4 * g:4 * g + 4, :],
                                                     core.col("hg_norm" if g == 0 else "gla_norm", 0), sq[:, 4 * g:4 * g + 4, :],
                                                     ALU.mult, ALU.mult)
            steps.then(ins)
            dve.wait_ge(gated.sem, gated.at(1))
            steps.then(nc.vector.tensor_tensor(mix[:], sq[:], sg[:], ALU.mult))
    for s, k in ((squared, 4), (meant, 4), (rooted, 4), (own, 3), (gated, 1)):
        s.passed(k)


def retrieval(core, a):
    nc = core.nc
    with ExitStack() as ctx:
        sb = lambda name, shape, dt=F32: core.sb(ctx, name, shape, dt)
        y = sb("y", [P, C, N])
        with ExitStack() as cg:
            picked = core.sb(cg, "picked", [P, 3, N])
            with ExitStack() as c1:
                xc = core.sb(c1, "xc2", [P, C, N])
                sq = core.sb(c1, "sq2", [P, C, N])
                norm(core, core.x1, N, core.h, True, [(0, N, core.mod[:, 32:40, 0], core.mod[:, 24:32, 0])], xc, sq)
                qt = core.sb(c1, "qt", [P, 16, N])

                def to_q(dve, t, u):
                    return nc.vector.tensor_copy(qt[:, bass.ds(t, 1), :], core.bank[u][:, 0:N].rearrange("p (o n) -> p o n", o=1))

                def first(u):
                    return [a["peer_u"][0], a["peer_u"][1], a["peer_v"][0], a["peer_u"][2]][u]

                project(core, lambda t: a["w_query"][t], 16, feature_products(core, core.h, 0, N), to_q, first)
                for tt in range(2):
                    choose(core, a, qt, tt, picked)
            weights = core.sb(cg, "weights", [P, N, P])
            with ExitStack() as c2:
                spread_weights(core, c2, picked, weights)
            experts(core, cg, a, weights, y)
        pre = sb("pre2", [P, C, N])
        xc = sb("xc3", [P, C, N])
        own = core.count("retrieved")
        with nc.Block() as block:

            @block.vector
            def _(dve):
                for c in range(C):
                    nc.vector.tensor_scalar(y[:, c, :], y[:, c, :], core.mod[:, 40 + c, 0:1], None, ALU.mult).then_inc(own.sem, 1)
                dve.wait_ge(own.sem, own.at(C))
                nc.vector.scalar_tensor_tensor(pre[:], core.x1[:], ALPHA, y[:], ALU.mult, ALU.add).then_inc(own.sem, 1)
        own.passed(C + 1)
        norm(core, pre, N, core.x1, True, [(0, N, core.vcols("ln_gamma1"), core.vcols("ln_beta1"))], xc, y)


def choose(core, a, qt, tt, picked):
    nc = core.nc
    with ExitStack() as ctx:
        sb = lambda name, shape, dt=F32: core.sb(ctx, f"{name}_{tt}", shape, dt)
        keys = sb("keys", [P, 2, P])
        s = sb("s", [P, 16, P])
        s2 = sb("s_rest", [P, 16, P])
        v = sb("v", [P, HEADS, 2, TOPK])
        vi = sb("vi", [P, HEADS, 2, TOPK], U32)
        vif = sb("vif", [P, HEADS, 2, TOPK])
        cand = sb("cand", [P, HEADS, TOPK, TOPK])
        cand2 = sb("cand_rest", [P, HEADS, TOPK, TOPK])
        top = sb("top", [P, HEADS, TOPK])
        pos = sb("pos", [P, HEADS, TOPK], U32)
        ab = sb("ab", [P, 2, HEADS, TOPK], U32)
        abf = sb("abf", [P, 2, HEADS * TOPK])
        hit = sb("hit", [P, HEADS * TOPK, TOPK])
        out = sb("out", [P, 3, HEADS, TOPK])
        tot = sb("tot", [P, HEADS])
        loaded, scored, own, expd, ready, turned, kept = (
            core.count(x) for x in ("keys_loaded", "keys_scored", "choose_vector_steps", "choice_exp", "choice_ready",
                                    "choice_turned", "choice_kept"))
        with nc.Block() as block:

            @block.sync
            def _(sp):
                sp.dma_start(keys[:], a["keys"]).then_inc(loaded.sem, 16)
                sp.wait_ge(loaded.sem, loaded.at(16))

            @block.tensor
            def _(pe):
                pe.wait_ge(loaded.sem, loaded.at(16))
                for g in range(4):
                    for j in range(4):
                        t = 4 * g + j
                        last = nc.tensor.matmul(core.bank[4 + g][:, j * P:j * P + P], qt[:, t, tt * P:tt * P + P], keys[:, t % 2, :],
                                                start=True, stop=True)
                    last.then_inc(scored.sem, 1)
                pe.wait_ge(ready.sem, ready.at(2))
                for j in range(3):
                    last = nc.tensor.transpose(core.bank[4][:, j * P:j * P + P], out[:, j, :, :].rearrange("p h k -> p (h k)"), core.ident)
                last.then_inc(turned.sem, 1)

            @block.vector
            def _(dve):
                steps = Steps(dve, own)
                for g in range(4):
                    dve.wait_ge(scored.sem, scored.at(g + 1))
                    ins = nc.vector.tensor_copy(s[:, 4 * g:4 * g + 4, :], core.bank[4 + g][:, :].rearrange("p (j n) -> p j n", n=P))
                steps.then(ins)

                def best(vals, rest, n, outs, idxs):
                    for j in range(n):
                        ins = nc.vector.max(outs(j)[:, 0:8], vals(j))
                    steps.then(ins)
                    for j in range(n):
                        nc.vector.max_index(idxs(j)[:, 0:8], outs(j)[:, 0:8], vals(j))
                        ins = nc.vector.match_replace(rest(j), outs(j)[:, 0:8], vals(j), NEG)
                    steps.then(ins)
                    for j in range(n):
                        ins = nc.vector.max(outs(j)[:, 8:16], rest(j))
                    steps.then(ins)
                    for j in range(n):
                        ins = nc.vector.max_index(idxs(j)[:, 8:16], outs(j)[:, 8:16], rest(j))
                    steps.then(ins)

                best(lambda j: s[:, j, :], lambda j: s2[:, j, :], 16, lambda j: v[:, j // 2, j % 2, :], lambda j: vi[:, j // 2, j % 2, :])
                nc.vector.tensor_copy(vif[:], vi[:])
                steps.then(nc.vector.tensor_tensor(cand[:], v[:, :, 0, :].rearrange("p h (k o) -> p h k o", o=1).broadcast_to([P, HEADS, TOPK, TOPK]),
                                                   v[:, :, 1:2, :].broadcast_to([P, HEADS, TOPK, TOPK]), ALU.add))
                flat = lambda t: (lambda j: t[:, j].rearrange("p a b -> p (a b)"))
                best(flat(cand), flat(cand2), HEADS, lambda j: top[:, j, :], lambda j: pos[:, j, :])
                nc.vector.tensor_scalar(ab[:, 0], pos[:], 4, None, ALU.logical_shift_right)
                nc.vector.tensor_scalar(ab[:, 1], pos[:], 15, None, ALU.bitwise_and)
                nc.vector.tensor_tensor(out[:, 2], top[:], top[:, :, 0:1].broadcast_to([P, HEADS, TOPK]), ALU.subtract).then_inc(ready.sem, 1)
                steps.then(nc.vector.tensor_copy(tot[:], top[:, :, 0]))
                steps.then(nc.vector.tensor_copy(abf[:], ab[:].rearrange("p w h k -> p w (h k)")))
                for w in range(2):
                    steps.then(nc.vector.tensor_tensor(hit[:], abf[:, w, :].rearrange("p (m o) -> p m o", o=1).broadcast_to([P, HEADS * TOPK, TOPK]),
                                                       core.iota[:, 0:TOPK].rearrange("p (o n) -> p o n", o=1).broadcast_to([P, HEADS * TOPK, TOPK]),
                                                       ALU.is_equal))
                    h4 = hit[:].rearrange("p (h k) n -> p h k n", k=TOPK)
                    steps.then(nc.vector.tensor_tensor(h4, h4, vif[:, :, w:w + 1, :].broadcast_to([P, HEADS, TOPK, TOPK]), ALU.mult))
                    steps.then(nc.vector.tensor_reduce(out[:, w].rearrange("p h k -> p (h k)"), hit[:], AX.X, ALU.add))
                dve.wait_ge(expd.sem, expd.at(1))
                steps.then(nc.vector.tensor_reduce(tot[:], out[:, 2], AX.X, ALU.add))
                steps.then(nc.vector.reciprocal(tot[:], tot[:]))
                nc.vector.tensor_tensor(out[:, 2], out[:, 2], tot[:].rearrange("p (h o) -> p h o", o=1).broadcast_to([P, HEADS, TOPK]), ALU.mult)\
                    .then_inc(ready.sem, 1)
                dve.wait_ge(turned.sem, turned.at(1))
                nc.vector.tensor_copy(picked[:, :, tt * P:tt * P + P], core.bank[4][:, 0:3 * P].rearrange("p (j n) -> p j n", n=P))\
                    .then_inc(kept.sem, 1)
                n_own.append(steps.k)

            @block.scalar
            def _(act):
                act.wait_ge(ready.sem, ready.at(1))
                nc.scalar.activation(out[:, 2], out[:, 2], ACT.Exp).then_inc(expd.sem, 1)
        loaded.passed(16)
        scored.passed(4)
        own.passed(n_own.pop())
        expd.passed(1)
        ready.passed(2)
        turned.passed(1)
        kept.passed(1)


n_own = []


def spread_weights(core, ctx, picked, weights):
    nc = core.nc
    B = 4
    one_a = core.sb(ctx, "one_a", [P, 2, B, P])
    one_b = core.sb(ctx, "one_b", [P, 2, B, P])
    marked, made, kept = core.count("keys_marked"), core.count("weights_made"), core.count("weights_kept")
    rounds = N // (2 * B)
    iota_b = core.iota.rearrange("p (o n) -> p o n", o=1).broadcast_to([P, B, P])
    with nc.Block() as block:

        @block.vector
        def _(dve):
            dve.sem_inc(made.sem, 2)
            with dve.Fori(0, rounds) as i:
                for w in range(2):
                    t0 = i * (2 * B) + w * B
                    dve.wait_ge(made.sem, made.at(w + 1) + i * 2)
                    for j in range(B):
                        nc.vector.tensor_scalar(one_a[:, w, j, :], core.iota, picked[:, 0, bass.ds(t0 + j, 1)], None, ALU.is_equal)\
                            .then_inc(marked.sem, 1)
                        nc.vector.tensor_scalar(one_b[:, w, j, :], core.iota, picked[:, 1, bass.ds(t0 + j, 1)],
                                                picked[:, 2, bass.ds(t0 + j, 1)], ALU.is_equal, ALU.mult).then_inc(marked.sem, 1)

        @block.scalar
        def _(act):
            with act.Fori(0, rounds) as i:
                for w in range(2):
                    act.wait_ge(made.sem, made.at(2 + w + 1) + i * 2)
                    nc.scalar.activation(weights[:, bass.ds(i * (2 * B) + w * B, B), :], core.bank[w][:, :].rearrange("p (b n) -> p b n", n=P),
                                         ACT.Copy).then_inc(kept.sem, 1)

        @block.tensor
        def _(pe):
            pe.sem_inc(kept.sem, 2)
            with pe.Fori(0, rounds) as i:
                for w in range(2):
                    pe.wait_ge(marked.sem, marked.at(2 * B * (w + 1)) + i * (4 * B))
                    pe.wait_ge(kept.sem, kept.at(w + 1) + i * 2)
                    for j in range(B):
                        last = nc.tensor.matmul(core.bank[w][:, j * P:j * P + P], one_b[:, w, j, :], one_a[:, w, j, :], start=True, stop=True)
                    last.then_inc(made.sem, 1)
    marked.passed(2 * N)
    made.passed(2 * rounds + 2)
    kept.passed(2 * rounds + 2)


def zero_banks(core, pe, banks):
    for b in banks:
        core.nc.tensor.matmul(core.bank[b][:, :], core.zeros[:, 0:P], core.zeros[:, :], start=True, stop=False, skip_group_check=True)


def add_products(core, slot, moving, stop=False):
    for m in range(C):
        last = core.nc.tensor.matmul(core.bank[4 + m // 2][:, (m % 2) * N:(m % 2) * N + N], core.slot[slot][:, m, :], moving,
                                     start=False, stop=stop, skip_group_check=True)
    return last


def experts(core, ctx, a, weights, y):
    nc = core.nc
    T = P
    act_g = core.sb(ctx, "act_g", [P, 2, N])
    act_w = core.sb(ctx, "act_w", [P, 2, N])
    side = core.sb(ctx, "side", [P, 2, C, P])
    used = core.tiles_used
    geled, weighed, read = core.count("expert_gelu"), core.count("expert_weighed"), core.count("expert_sums")
    side_landed = [core.count(f"ada_landed_{w}") for w in range(2)]
    side_used, side_added = core.count("ada_used"), core.count("ada_added")
    pairs = T // 2
    SIDE = DEPTH_2 * 48
    side_rounds = SIDE // 2
    ada = a["ada_w_2"]

    def wait_landed(pe, u, k):
        pe.wait_ge(core.landed[u].sem, core.landed[u].at(16) + k * 16)

    def load_side(sp, w, tile):
        sp.dma_start(side[:, w].rearrange("p c m -> p (c m)"), tile).then_inc(side_landed[w].sem, 16)

    with nc.Block() as block:

        @block.sync
        def _(sp):
            def refill(i, last, with_side):
                order = (a["peer_v"][i * 2 - 1], a["peer_u"][i * 2 + 1], a["peer_v"][i * 2],
                         a["peer_v"][i * 2 + 1] if last else a["peer_u"][i * 2 + 2])
                for u, tile in enumerate(order):
                    sp.wait_ge(used.sem, used.at(u - 3) + i * 4)
                    core.load_tile(sp, u, tile)
                    if with_side and u % 2:
                        sp.wait_ge(side_used.sem, side_used.at(u // 2 - 1) + i * 2)
                        load_side(sp, u // 2, ada[i * 2 + u // 2])

            for w in range(2):
                load_side(sp, w, ada[w])
            with sp.Fori(1, side_rounds) as i:
                refill(i, False, True)
            with sp.Fori(side_rounds, pairs - 1) as i:
                refill(i, False, False)
            refill(pairs - 1, True, False)
            sp.wait_ge(used.sem, used.at(2 * T))
            for u in range(U):
                core.load_tile(sp, u, a["w_in_2"][u])

        @block.tensor
        def _(pe):
            def dot(u, w):
                for c in range(C):
                    last = nc.tensor.matmul(core.bank[w][:, 0:N], core.slot[u][:, c, :], core.h[:, c, :], start=(c == 0), stop=(c == C - 1))
                last.then_inc(used.sem, 1)

            def round_(i, with_side):
                for w, (su, sv) in enumerate(((1, 2), (3, 0))):
                    wait_landed(pe, su, i)
                    pe.wait_ge(geled.sem, geled.at(w + 1) + i * 2)
                    dot(su, 1 - w)
                    if with_side:
                        pe.wait_ge(side_landed[w].sem, side_landed[w].at(16) + i * 16)
                        for c in range(C):
                            last = nc.tensor.matmul(core.bank[2][:, bass.ds(i * 2 + w, 1)], side[:, w, c, :], core.c2s[:, c, :],
                                                    start=(c == 0), stop=(c == C - 1))
                        last.then_inc(side_used.sem, 1)
                    wait_landed(pe, sv, i + (1 if sv == 0 else 0))
                    pe.wait_ge(weighed.sem, weighed.at(w + 1) + i * 2)
                    add_products(core, sv, act_w[:, w, :]).then_inc(used.sem, 1)

            zero_banks(core, pe, range(4, 8))
            wait_landed(pe, 0, 0)
            dot(0, 0)
            with pe.Fori(0, side_rounds) as i:
                round_(i, True)
            with pe.Fori(side_rounds, pairs - 1) as i:
                round_(i, False)
            k = pairs - 1
            wait_landed(pe, 1, k)
            pe.wait_ge(geled.sem, geled.at(2 * k + 1))
            dot(1, 1)
            wait_landed(pe, 2, k)
            pe.wait_ge(weighed.sem, weighed.at(2 * k + 1))
            add_products(core, 2, act_w[:, 0, :]).then_inc(used.sem, 1)
            wait_landed(pe, 3, k)
            pe.wait_ge(weighed.sem, weighed.at(2 * k + 2))
            add_products(core, 3, act_w[:, 1, :], stop=True).then_inc(used.sem, 1)

        @block.scalar
        def _(act):
            act.sem_inc(geled.sem, 1)
            act.wait_ge(used.sem, used.at(1))
            nc.scalar.activation(act_g[:, 0, :], core.bank[0][:, 0:N], ACT.Gelu_apprx_tanh).then_inc(geled.sem, 1)
            act.wait_ge(used.sem, used.at(2))
            nc.scalar.activation(act_g[:, 1, :], core.bank[1][:, 0:N], ACT.Gelu_apprx_tanh).then_inc(geled.sem, 1)
            with act.Fori(1, pairs) as i:
                for w in range(2):
                    act.wait_ge(used.sem, used.at(2 * w) + i * 4)
                    act.wait_ge(weighed.sem, weighed.at(w - 1) + i * 2)
                    nc.scalar.activation(act_g[:, w, :], core.bank[w][:, 0:N], ACT.Gelu_apprx_tanh).then_inc(geled.sem, 1)

        @block.vector
        def _(dve):
            def weigh(i, w):
                nc.vector.tensor_tensor(act_w[:, w, :], act_g[:, w, :],
                                        weights[:, :, bass.ds(i * 2 + w, 1)].rearrange("p t o -> p (t o)"), ALU.mult).then_inc(weighed.sem, 1)

            for w in range(2):
                dve.wait_ge(geled.sem, geled.at(w + 2))
                weigh(0, w)
            with dve.Fori(1, pairs) as i:
                for w in range(2):
                    dve.wait_ge(geled.sem, geled.at(w + 2) + i * 2)
                    dve.wait_ge(used.sem, used.at(2 * w - 1) + i * 4)
                    weigh(i, w)
            dve.wait_ge(side_used.sem, side_used.at(SIDE))
            for l in range(DEPTH_2):
                nc.vector.tensor_tensor(core.mod2[:, 48 * l:48 * l + 48, 0], core.bank[2][:, 48 * l:48 * l + 48], core.vcols(f"ada_b{l}"), ALU.add)\
                    .then_inc(side_added.sem, 1)
            dve.wait_ge(used.sem, used.at(2 * T))
            for b in range(4):
                nc.vector.tensor_copy(y[:, 2 * b:2 * b + 2, :], core.bank[4 + b][:, :].rearrange("p (m n) -> p m n", n=N))\
                    .then_inc(read.sem, 1)
    used.passed(2 * T)
    for u in range(U):
        core.landed[u].passed(16 * (2 * T // U))
    for w in range(2):
        side_landed[w].passed(16 * side_rounds)
    for s, k in ((geled, T + 1), (weighed, T), (read, 4), (side_used, SIDE), (side_added, DEPTH_2)):
        s.passed(k)


def second_block(core, a):
    nc = core.nc
    with ExitStack() as ctx:
        sb = lambda name, shape, dt=F32: core.sb(ctx, name, shape, dt)
        cos = sb("cos", [P, N])
        sin = sb("sin", [P, N])
        hide = sb("hide", [P, 2, N])
        lam = sb("lam", [P, DEPTH_2, 1])
        gain = sb("gain", [P, DEPTH_2, 2, C])
        positions(core, a, cos, sin, hide, lam, gain)
        x = core.x1
        for l in range(DEPTH_2):
            m = lambda s, l=l: core.mod2[:, 48 * l + 8 * s:48 * l + 8 * s + 8, 0]
            moe = l % 2 == 1
            with ExitStack() as c1:
                z = core.sb(c1, f"z{l}", [P, 16, N])
                v = core.sb(c1, f"v{l}", [P, 2, 512])
                mix = core.sb(c1, f"mix{l}", [P, C, N])
                sq = core.sb(c1, f"sq_{l}", [P, C, N])
                norm(core, x, N, core.h, False, [(0, N, gain[:, l, 0], m(0))], None, sq)

                def to_z(dve, t, u):
                    return nc.vector.tensor_copy(z[:, bass.ds(t, 1), :], core.bank[u][:, 0:N].rearrange("p (o n) -> p o n", o=1))

                project(core, lambda t: a["w_in_2"][t + 20 * l], 16, feature_products(core, core.h, 0, N), to_z,
                        lambda u: a["w_in_2"][20 * l + 16 + u])

                def token_products(pe, t, u):
                    for tt in range(2):
                        for c in range(C):
                            last = nc.tensor.matmul(core.bank[u][:, tt * P:tt * P + P], core.h[:, c, tt * P:tt * P + P],
                                                    core.slot[u][:, c, :], start=(c == 0), stop=(c == C - 1))
                    return last

                def to_v(dve, t, u):
                    return nc.vector.tensor_copy(v[:, :, bass.ds(t * P, P)], core.bank[u][:, 0:N].rearrange("p (t n) -> p t n", t=2))

                project(core, lambda t: a["w_in_2"][t + 20 * l + 16], 4, token_products, to_v, lambda u: a["w_out_2"][8 * l + u])
                with ExitStack() as c2:
                    linear_recurrence(core, c2, a, l, z, mix)
                with ExitStack() as c2:
                    attention(core, c2, a, l, z, v, mix, cos, sin, hide, lam)
                tmp = core.sb(c1, f"tmp{l}", [P, U, N])
                if moe:
                    first = lambda u: a["moe_gu"][u % 2, u // 2]
                else:
                    first = lambda u: a["ffn_gu"][u % 2, u // 2]
                add_residual_2(core, a, l, mix, x, m(2), first)
                norm(core, x, N, core.h, False, [(0, N, gain[:, l, 1], m(3))], None, sq)
            with ExitStack() as c1:
                if moe:
                    routed_feed_forward(core, c1, a, x, m(5))
                else:
                    hid = core.sb(c1, "hid", [P, FT, N])
                    feed_forward(core, c1, a["ffn_gu"], a["ffn_d"], hid, lambda u: a["w_in_2"][20 + u], x, m(5))
        sq = sb("sq_end", [P, C, N])
        norm(core, x, N, core.h, False, [(0, N, core.vcols("final_g"), None)], None, sq)
        stored = core.count("stored")
        with nc.Block() as block:

            @block.sync
            def _(sp):
                sp.dma_start(a["out"], core.h[:]).then_inc(stored.sem, 16)
                sp.wait_ge(stored.sem, 16)


def add_residual_2(core, a, l, moving, x, gate, next_tiles):
    nc = core.nc

    def evacuate(dve, t, u):
        return nc.vector.scalar_tensor_tensor(x[:, bass.ds(t, 1), :], core.bank[u][:, 0:N].rearrange("p (o n) -> p o n", o=1),
                                              gate[:, bass.ds(t, 1)], x[:, bass.ds(t, 1), :], ALU.mult, ALU.add)

    project(core, lambda t: a["w_out_2"][t + 8 * l], C, feature_products(core, moving, 0, N), evacuate, next_tiles)


def positions(core, a, cos, sin, hide, lam, gain):
    nc = core.nc
    with ExitStack() as ctx:
        sb = lambda name, shape, dt=F32: core.sb(ctx, name, shape, dt)
        row = sb("pos_row", [P, N], I32)
        col = sb("pos_col", [P, 2], I32)
        rowc = sb("chunk_row", [P, N], I32)
        colc = sb("chunk_col", [P, 2], I32)
        rowf = sb("pos_f", [P, N])
        rowcf = sb("chunk_row_f", [P, N])
        colcf = sb("chunk_col_f", [P, 2])
        turns = sb("turns", [P, N])
        ang = sb("ang", [P, N])
        lv = sb("lv", [P, DEPTH_2, 4, DH])
        lp = sb("lp", [P, DEPTH_2 * 2, DH])
        ls = sb("ls", [P, DEPTH_2 * 2])
        loaded, own, angle, done = core.count("positions_loaded"), core.count("positions_vector_steps"), core.count("angles_ready"), core.count("sines_ready")
        with nc.Block() as block:

            @block.sync
            def _(sp):
                sp.dma_start(row[:], a["pos"].rearrange("(o n) -> o n", o=1).broadcast_to([P, N])).then_inc(loaded.sem, 16)
                sp.dma_start(col[:], a["pos_cols"]).then_inc(loaded.sem, 16)
                sp.dma_start(lv[:], a["lam_rows"].broadcast_to([P, DEPTH_2, 4, DH])).then_inc(loaded.sem, 16)
                sp.wait_ge(loaded.sem, loaded.at(48))

            @block.vector
            def _(dve):
                steps = Steps(dve, own)
                dve.wait_ge(loaded.sem, loaded.at(48))
                nc.vector.tensor_copy(rowf[:], row[:])
                nc.vector.tensor_scalar(rowc[:], row[:], 6, None, ALU.arith_shift_right)
                steps.then(nc.vector.tensor_scalar(colc[:], col[:], 6, None, ALU.arith_shift_right))
                nc.vector.tensor_copy(rowcf[:], rowc[:])
                nc.vector.tensor_copy(colcf[:], colc[:])
                steps.then(nc.vector.tensor_scalar(ang[:], rowf[:], core.col("inv_freq", 0), None, ALU.mult))
                steps.then(nc.vector.tensor_scalar(turns[:], ang[:], 1.0 / TWO_PI, None, ALU.mult))
                steps.then(nc.vector.tensor_scalar(turns[:], turns[:], ROUND, None, ALU.add))
                steps.then(nc.vector.tensor_scalar(turns[:], turns[:], ROUND, None, ALU.subtract))
                for part in (PI_A, PI_B, PI_C):
                    steps.then(nc.vector.scalar_tensor_tensor(ang[:], turns[:], -part, ang[:], ALU.mult, ALU.add))
                nc.vector.tensor_scalar(ang[:], ang[:], -3.1415925, 3.1415925, ALU.max, ALU.min).then_inc(angle.sem, 1)
                for tt in range(2):
                    ins = nc.vector.tensor_scalar(hide[:, tt, :], rowcf[:], colcf[:, tt:tt + 1], None, ALU.is_le)
                steps.then(ins)
                steps.then(nc.vector.tensor_scalar(hide[:], hide[:], 1.0, 1e30, ALU.subtract, ALU.mult))
                for l in range(DEPTH_2):
                    pairs = lv[:, l].rearrange("p (k two) d -> p k two d", two=2)
                    ins = nc.vector.tensor_tensor(lp[:, 2 * l:2 * l + 2, :], pairs[:, :, 0, :], pairs[:, :, 1, :], ALU.mult)
                steps.then(ins)
                nc.vector.tensor_reduce(ls[:], lp[:], AX.X, ALU.add).then_inc(angle.sem, 1)
                for l in range(DEPTH_2):
                    for j in range(2):
                        s = 48 * l + 8 * (1 + 3 * j)
                        ins = nc.vector.scalar_tensor_tensor(gain[:, l, j], core.mod2[:, s:s + 8, 0], 1.0,
                                                             core.vcols(f"ln{j + 1}_g{l}"), ALU.add, ALU.mult)
                steps.then(ins)
                dve.wait_ge(done.sem, done.at(3))
                for l in range(DEPTH_2):
                    ins = nc.vector.scalar_tensor_tensor(lam[:, l], ls[:, 2 * l:2 * l + 1], lambda_init(l), ls[:, 2 * l + 1:2 * l + 2],
                                                         ALU.add, ALU.subtract)
                steps.then(ins)

            @block.scalar
            def _(act):
                act.wait_ge(angle.sem, angle.at(1))
                nc.scalar.activation(sin[:], ang[:], ACT.Sin).then_inc(done.sem, 1)
                nc.scalar.activation(turns[:], ang[:], ACT.Abs).then_inc(done.sem, 1)
                act.wait_ge(done.sem, done.at(2))
                act.wait_ge(angle.sem, angle.at(2))
                nc.scalar.activation(ls[:], ls[:], ACT.Exp).then_inc(done.sem, 1)
                nc.scalar.activation(cos[:], turns[:], ACT.Sin, scale=-1.0, bias=core.col("halfpi", 0)).then_inc(done.sem, 1)
        loaded.passed(48)
        own.passed(13)
        angle.passed(2)
        done.passed(4)


def lambda_init(l):
    return 0.8 - 0.6 * float(np.exp(-0.3 * l))


def linear_recurrence(core, ctx, a, l, z, mix):
    nc = core.nc
    sb = lambda name, shape, dt=F32: core.sb(ctx, f"{name}_{l}", shape, dt)
    T = 4
    wg = sb("gate_w", [P, 2, T, P])
    conv = sb("conv", [P, T, N])
    r = sb("lru_r", [P, T, N])
    i_ = sb("lru_i", [P, T, N])
    av = sb("lru_a", [P, T, N])
    th = sb("lru_th", [P, T, N])
    gy = sb("lru_gy", [P, T, N])
    sp8 = sb("lru_rate", [P, 3, T])
    loaded, conved, made, gated, own, act_s, v_s = (core.count(x) for x in (
        "lru_loaded", "conv_ready", "lru_products", "lru_gates", "lru_vector_steps", "lru_scalar_steps", "lru_logs_ready"))
    lamc = core.vcols(f"lru_lambda{l}")
    with nc.Block() as block:

        @block.sync
        def _(sp):
            sp.dma_start(wg[:], a["lru_gates"][l]).then_inc(loaded.sem, 16)
            sp.wait_ge(loaded.sem, loaded.at(16))

        @block.vector
        def _(dve):
            steps = Steps(dve, own)
            for t in range(T):
                ins = nc.vector.tensor_scalar(conv[:, t, :], z[:, t, :], core.col(f"conv_w{l}", 12 + t), core.col(f"conv_b{l}", t), ALU.mult, ALU.add)
            steps.then(ins)
            for j in range(1, 4):
                for t in range(T):
                    ins = nc.vector.scalar_tensor_tensor(conv[:, t, j:N], z[:, t, 0:N - j], core.col(f"conv_w{l}", 4 * (3 - j) + t),
                                                         conv[:, t, j:N], ALU.mult, ALU.add)
                steps.then(ins)
            nc.vector.tensor_copy(sp8[:, 2, :], lamc).then_inc(conved.sem, 1)
            dve.wait_ge(act_s.sem, act_s.at(3))
            steps.then(nc.vector.scalar_tensor_tensor(sp8[:, 0, :], lamc, 0.0, sp8[:, 1, :], ALU.min, ALU.subtract))
            steps.then(nc.vector.tensor_scalar(sp8[:, 0, :], sp8[:, 0, :], 8.0, None, ALU.mult))
            dve.wait_ge(gated.sem, gated.at(8))
            for t in range(T):
                nc.vector.tensor_tensor(i_[:, t, :], i_[:, t, :], conv[:, t, :], ALU.mult)
                ins = nc.vector.tensor_scalar(r[:, t, :], r[:, t, :], sp8[:, 0, t:t + 1], None, ALU.mult)
            ins.then_inc(v_s.sem, 1)
            dve.wait_ge(act_s.sem, act_s.at(5))
            steps.then(nc.vector.tensor_scalar(r[:], th[:], 1.0, None, ALU.add))
            steps.then(nc.vector.reciprocal(r[:], r[:]))
            nc.vector.scalar_tensor_tensor(r[:], th[:], 2.0, r[:], ALU.mult, ALU.mult).then_inc(v_s.sem, 1)
            dve.wait_ge(act_s.sem, act_s.at(6))
            steps.then(nc.vector.tensor_tensor(i_[:], i_[:], r[:], ALU.mult))
            for t in range(T):
                ins = nc.vector.tensor_tensor_scan(conv[:, t, :], av[:, t, :], i_[:, t, :], 0.0, ALU.mult, ALU.add)
            steps.then(ins)
            dve.wait_ge(act_s.sem, act_s.at(7))
            steps.then(nc.vector.tensor_tensor(mix[:, 0:T, :], conv[:], gy[:], ALU.mult))

        @block.tensor
        def _(pe):
            pe.wait_ge(loaded.sem, loaded.at(16))
            pe.wait_ge(conved.sem, conved.at(1))
            for w in range(2):
                for t in range(T):
                    nc.tensor.matmul(core.bank[2 * w + t // 2][:, (t % 2) * N:(t % 2) * N + N], wg[:, w, t, :], conv[:, t, :],
                                     start=True, stop=True).then_inc(made.sem, 1)

        @block.scalar
        def _(act):
            steps = Steps(act, act_s)
            steps.then(nc.scalar.activation(sp8[:, 1, :], lamc, ACT.Abs))
            steps.then(nc.scalar.activation(sp8[:, 1, :], sp8[:, 1, :], ACT.Exp, scale=-1.0))
            steps.then(nc.scalar.activation(sp8[:, 1, :], sp8[:, 1, :], ACT.Ln, bias=core.col("one", 0)))
            for w, (out, bias) in enumerate(((r, f"gate_a_b{l}"), (i_, f"gate_x_b{l}"))):
                for t in range(T):
                    act.wait_ge(made.sem, made.at(4 * w + t // 2 * 2 + 2))
                    nc.scalar.activation(out[:, t, :], core.bank[2 * w + t // 2][:, (t % 2) * N:(t % 2) * N + N], ACT.Sigmoid,
                                         bias=core.col(bias, t)).then_inc(gated.sem, 1)
            act.wait_ge(v_s.sem, v_s.at(1))
            steps.then(nc.scalar.activation(av[:], r[:], ACT.Exp))
            steps.then(nc.scalar.activation(th[:], r[:], ACT.Tanh, scale=-1.0))
            act.wait_ge(v_s.sem, v_s.at(2))
            steps.then(nc.scalar.activation(r[:], r[:], ACT.Sqrt))
            steps.then(nc.scalar.activation(gy[:], z[:, 4:8, :], ACT.Gelu_apprx_tanh))
    for s, k in ((loaded, 16), (conved, 1), (made, 8), (gated, 8), (own, 11), (act_s, 7), (v_s, 2)):
        s.passed(k)


def attention(core, ctx, a, l, z, v, mix, cos, sin, hide, lam):
    nc = core.nc
    sb = lambda name, shape, dt=F32: core.sb(ctx, f"{name}_{l}", shape, dt)
    H = 4
    qk = sb("qk", [P, 8, N])
    s = sb("att", [P, 16, N])
    mx = sb("att_max", [P, 16])
    tot = sb("att_tot", [P, 16])
    pt = sb("att_t", [P, 2, H, N])
    o = sb("att_o", [P, H, N])
    sq = sb("att_sq", [P, H, N])
    own, turned, roped, scored, shifted, expd, mixed, flipped, flip_kept, made, copied, squared, meant, rooted = (
        core.count(x) for x in ("att_vector_steps", "half_turned", "roped", "att_scored", "att_shifted", "att_exp", "att_mixed",
                                "att_flipped", "flip_kept", "att_made", "att_copied", "att_squared", "att_mean", "att_root"))
    with nc.Block() as block:

        @block.tensor
        def _(pe):
            for t in range(8):
                last = nc.tensor.matmul(core.bank[t // 2][:, (t % 2) * N:(t % 2) * N + N], core.rot, z[:, 8 + t, :], start=True, stop=True)
                if t % 2:
                    last.then_inc(turned.sem, 1)
            pe.wait_ge(roped.sem, roped.at(1))
            for h in range(H):
                for c in range(2):
                    rows = slice(DH * c, DH * c + DH)
                    for tt in range(2):
                        last = nc.tensor.matmul(core.bank[2 * h + c][:, tt * N:tt * N + N], qk[rows, h, tt * P:tt * P + P], qk[rows, 4 + h, :],
                                                start=True, stop=True)
                    last.then_inc(scored.sem, 1)
            for h in range(H):
                pe.wait_ge(mixed.sem, mixed.at(2 * h + 2))
                for kt in range(2):
                    for tt in range(2):
                        last = nc.tensor.transpose(core.bank[h][:, kt * N + tt * P:kt * N + tt * P + P],
                                                   s[:, 4 * h + tt, kt * P:kt * P + P], core.ident)
                last.then_inc(flipped.sem, 1)
            for h in range(H):
                pe.wait_ge(flip_kept.sem, flip_kept.at(h + 1))
                for kt in range(2):
                    last = nc.tensor.matmul(core.bank[4 + h // 2][:, (h % 2) * N:(h % 2) * N + N], v[:, kt, h * P:h * P + P], pt[:, kt, h, :],
                                            start=(kt == 0), stop=(kt == 1))
                if h % 2:
                    last.then_inc(made.sem, 1)
            for g in range(2):
                pe.wait_ge(squared.sem, squared.at(g + 1))
                nc.tensor.matmul(core.bank[6 + g][:, :], core.avg_head[:], sq[:, 2 * g:2 * g + 2, :].rearrange("p h n -> p (h n)"),
                                 start=True, stop=True).then_inc(meant.sem, 1)

        @block.vector
        def _(dve):
            steps = Steps(dve, own)
            cosb = cos[:].rearrange("p (o n) -> p o n", o=1)
            sinb = sin[:].rearrange("p (o n) -> p o n", o=1)
            nc.vector.tensor_tensor(qk[:], z[:, 8:16, :], cosb.broadcast_to([P, 8, N]), ALU.mult)
            for g in range(4):
                dve.wait_ge(turned.sem, turned.at(g + 1))
                ins = nc.vector.tensor_tensor(s[:, 2 * g:2 * g + 2, :], core.bank[g][:, :].rearrange("p (t n) -> p t n", n=N),
                                              sinb.broadcast_to([P, 2, N]), ALU.mult)
            steps.then(ins)
            nc.vector.tensor_tensor(qk[:], qk[:], s[:, 0:8, :], ALU.add).then_inc(roped.sem, 1)
            dve.wait_ge(roped.sem, roped.at(1))
            for j in range(8):
                dve.wait_ge(scored.sem, scored.at(j + 1))
                ins = nc.vector.scalar_tensor_tensor(s[:, 2 * j:2 * j + 2, :], core.bank[j][:, :].rearrange("p (t n) -> p t n", n=N),
                                                     DH ** -0.5, hide[:], ALU.mult, ALU.add)
            steps.then(ins)
            steps.then(nc.vector.tensor_reduce(mx[:], s[:], AX.X, ALU.max))
            nc.vector.tensor_scalar(mx[:], mx[:], -1.0, None, ALU.mult).then_inc(shifted.sem, 1)
            dve.wait_ge(expd.sem, expd.at(16))
            steps.then(nc.vector.reciprocal(tot[:], tot[:]))
            t4 = tot[:].rearrange("p (h c t) -> p h c t", c=2, t=2)
            steps.then(nc.vector.tensor_scalar(t4[:, :, 1, :], t4[:, :, 1, :], lam[:, l], None, ALU.mult))
            for h in range(H):
                for tt in range(2):
                    j = 4 * h + tt
                    steps.then(nc.vector.tensor_scalar(s[:, j + 2, :], s[:, j + 2, :], tot[:, j + 2:j + 3], None, ALU.mult))
                    nc.vector.scalar_tensor_tensor(s[:, j, :], s[:, j, :], tot[:, j:j + 1], s[:, j + 2, :], ALU.mult, ALU.subtract)                        .then_inc(mixed.sem, 1)
            for h in range(H):
                dve.wait_ge(flipped.sem, flipped.at(h + 1))
                nc.vector.tensor_copy(pt[:, :, h, :], core.bank[h][:, :].rearrange("p (k n) -> p k n", n=N)).then_inc(flip_kept.sem, 1)
            for g in range(2):
                dve.wait_ge(made.sem, made.at(g + 1))
                nc.vector.tensor_copy(o[:, 2 * g:2 * g + 2, :], core.bank[4 + g][:, :].rearrange("p (h n) -> p h n", n=N)).then_inc(copied.sem, 1)
            dve.wait_ge(rooted.sem, rooted.at(2))
            steps.then(nc.vector.reciprocal(sq[:], sq[:]))
            steps.then(nc.vector.scalar_tensor_tensor(o[:], o[:], core.col(f"subln_g{l}", 0), sq[:], ALU.mult, ALU.mult))
            steps.then(nc.vector.tensor_scalar(mix[:, 4:8, :], o[:], 1.0 - lambda_init(l), None, ALU.mult))

        @block.scalar
        def _(act):
            act.wait_ge(shifted.sem, shifted.at(1))
            for j in range(16):
                nc.scalar.activation(s[:, j, :], s[:, j, :], ACT.Exp, bias=mx[:, j:j + 1], accum_out=tot[:, j:j + 1]).then_inc(expd.sem, 1)
            for g in range(2):
                act.wait_ge(copied.sem, copied.at(g + 1))
                nc.scalar.activation(sq[:, 2 * g:2 * g + 2, :], o[:, 2 * g:2 * g + 2, :], ACT.Square).then_inc(squared.sem, 1)
            for g in range(2):
                act.wait_ge(meant.sem, meant.at(g + 1))
                nc.scalar.activation(sq[:, 2 * g:2 * g + 2, :], core.bank[6 + g][:, :].rearrange("p (h n) -> p h n", n=N), ACT.Sqrt,
                                     bias=core.col("eps", 0)).then_inc(rooted.sem, 1)
    for c, k in ((own, 16), (turned, 4), (roped, 1), (scored, 8), (shifted, 1), (expd, 16), (mixed, 8), (flipped, 4),
                 (flip_kept, 4), (made, 2), (copied, 2), (squared, 2), (meant, 2), (rooted, 2)):
        c.passed(k)


def route(core, a, r):
    nc = core.nc
    with ExitStack() as ctx:
        sb = lambda name, shape, dt=F32: core.sb(ctx, name, shape, dt)
        rw = sb("router_w", [P, C, EXPERTS])
        lg = sb("logits", [P, 2, EXPERTS])
        top = sb("route_top", [P, 2, 8])
        idx = sb("route_idx", [P, 2, 8], U32)
        idf = sb("route_idf", [P, 2, 8])
        e = sb("route_e", [P, 2, 1])
        w = sb("route_w", [P, 2, 2])
        hot = sb("route_hot", [P, 2, 2, EXPERTS])
        g = sb("route_g", [P, 2, EXPERTS])
        chosen = sb("route_chosen", [P, 2, EXPERTS])
        gt = sb("route_gt", [EXPERTS, 2, N])
        more = sb("route_more", [P, EXPERTS])
        rank = sb("route_rank", [P, EXPERTS])
        which = sb("route_which", [P, MORE, EXPERTS])
        named = sb("route_named", [P, MORE, EXPERTS])
        tab = sb("route_tab", [P, ROUNDS + 2])
        ones = sb("route_ones", [P, P])
        shares, place_rows, place_cols, first, table, ht = (r[k] for k in ("shares", "place_rows", "place_cols", "first", "table", "ht"))
        loaded, scored, own, expd, ready, turned, kept, spread, copied, ranked, flipped, flips = (core.count(x) for x in (
            "router_loaded", "routed", "route_vector_steps", "route_exp", "route_ready", "route_turned", "route_kept",
            "route_spread", "route_copied", "route_ranked", "tokens_turned", "tokens_copied"))
        with nc.Block() as block:

            @block.sync
            def _(sp):
                sp.dma_start(rw[:], a["router"]).then_inc(loaded.sem, 16)
                sp.wait_ge(loaded.sem, loaded.at(16))

            @block.tensor
            def _(pe):
                pe.wait_ge(loaded.sem, loaded.at(16))
                for tt in range(2):
                    for c in range(C):
                        last = nc.tensor.matmul(core.bank[0][:, tt * EXPERTS:tt * EXPERTS + EXPERTS], core.h[:, c, tt * P:tt * P + P],
                                                rw[:, c, :], start=(c == 0), stop=(c == C - 1))
                last.then_inc(scored.sem, 1)
                for q in range(4):
                    for j in range(4):
                        tt, c = q // 2, 4 * (q % 2) + j
                        last = nc.tensor.transpose(core.bank[4 + q][:, j * P:j * P + P], core.h[:, c, tt * P:tt * P + P], core.ident)
                    last.then_inc(flipped.sem, 1)
                pe.wait_ge(ready.sem, ready.at(2))
                nc.tensor.matmul(core.bank[2][:, 0:EXPERTS], core.before, chosen[:, 0, :], start=True, stop=True)
                nc.tensor.matmul(core.bank[2][:, EXPERTS:2 * EXPERTS], ones[:], chosen[:, 0, :], start=True, stop=False)
                nc.tensor.matmul(core.bank[2][:, EXPERTS:2 * EXPERTS], core.before, chosen[:, 1, :], start=False, stop=True)
                nc.tensor.matmul(core.bank[2][:, 2 * EXPERTS:3 * EXPERTS], ones[:], chosen[:, 0, :], start=True, stop=False)
                nc.tensor.matmul(core.bank[2][:, 2 * EXPERTS:3 * EXPERTS], ones[:], chosen[:, 1, :], start=False, stop=True)\
                    .then_inc(ranked.sem, 1)
                pe.wait_ge(ready.sem, ready.at(3))
                for k, src in enumerate((g, place_cols)):
                    for tt in range(2):
                        last = nc.tensor.transpose(core.bank[1][0:EXPERTS, k * N + tt * P:k * N + tt * P + P], src[:, tt, :], core.ident)
                last.then_inc(turned.sem, 1)
                pe.wait_ge(kept.sem, kept.at(1))
                pe.wait_ge(flips.sem, flips.at(4))
                for k in range(2):
                    if k:
                        pe.wait_ge(copied.sem, copied.at(4))
                    for x in range(EXPERTS):
                        last = nc.tensor.matmul(core.bank[4 + x // 2][:, (x % 2) * N:(x % 2) * N + N], core.sel[0:EXPERTS, x, :], gt[:, k, :],
                                                start=True, stop=True)
                    last.then_inc(spread.sem, 1)

            @block.vector
            def _(dve):
                steps = Steps(dve, own)
                nc.vector.memset(ones[:], 1.0)
                nc.vector.memset(tab[:], 0.0)
                nc.vector.memset(first[:], 0.0)
                dve.wait_ge(scored.sem, scored.at(1))
                steps.then(nc.vector.tensor_copy(lg[:], core.bank[0][:, 0:2 * EXPERTS].rearrange("p (t e) -> p t e", t=2)))
                for tt in range(2):
                    ins = nc.vector.max(top[:, tt, :], lg[:, tt, :])
                steps.then(ins)
                for tt in range(2):
                    ins = nc.vector.max_index(idx[:, tt, :], top[:, tt, :], lg[:, tt, :])
                steps.then(ins)
                nc.vector.tensor_copy(idf[:], idx[:])
                nc.vector.tensor_tensor(e[:], top[:, :, 1:2], top[:, :, 0:1], ALU.subtract).then_inc(ready.sem, 1)
                dve.wait_ge(expd.sem, expd.at(1))
                steps.then(nc.vector.tensor_scalar(w[:, :, 0:1], e[:], 1.0, None, ALU.add))
                steps.then(nc.vector.reciprocal(w[:, :, 0:1], w[:, :, 0:1]))
                steps.then(nc.vector.tensor_tensor(w[:, :, 1:2], w[:, :, 0:1], e[:], ALU.mult))
                for tt in range(2):
                    for k in range(2):
                        ins = nc.vector.tensor_scalar(hot[:, tt, k, :], core.iota[:, 0:EXPERTS], idf[:, tt, k:k + 1], w[:, tt, k:k + 1],
                                                      ALU.is_equal, ALU.mult)
                steps.then(ins)
                steps.then(nc.vector.tensor_tensor(g[:], hot[:, :, 0, :], hot[:, :, 1, :], ALU.add))
                nc.vector.tensor_scalar(chosen[:], g[:], 0.0, None, ALU.is_gt).then_inc(ready.sem, 1)
                dve.wait_ge(ranked.sem, ranked.at(1))
                steps.then(nc.vector.scalar_tensor_tensor(place_cols[:], core.bank[2][:, 0:2 * EXPERTS].rearrange("p (t e) -> p t e", t=2), 1.0,
                                                          chosen[:], ALU.add, ALU.mult))
                nc.vector.tensor_scalar(place_cols[:], place_cols[:], 1.0, None, ALU.subtract).then_inc(ready.sem, 1)
                steps.then(nc.vector.tensor_scalar(more[:], core.bank[2][:, 2 * EXPERTS:3 * EXPERTS], float(P), None, ALU.is_gt))
                steps.then(nc.vector.tensor_tensor_scan(rank[:], more[:], more[:], 0.0, ALU.add, ALU.bypass))
                for j in range(MORE):
                    ins = nc.vector.scalar_tensor_tensor(which[:, j, :], rank[:], float(j + 1), more[:], ALU.is_equal, ALU.mult)
                steps.then(ins)
                for j in range(MORE):
                    ins = nc.vector.tensor_tensor(named[:, j, :], which[:, j, :], core.iota[:, 0:EXPERTS], ALU.mult)
                steps.then(ins)
                nc.vector.tensor_copy(tab[:, 0:EXPERTS], core.iota[:, 0:EXPERTS])
                nc.vector.tensor_reduce(tab[:, EXPERTS:ROUNDS], named[:], AX.X, ALU.add)
                steps.then(nc.vector.tensor_reduce(first[:, EXPERTS:ROUNDS], which[:], AX.X, ALU.add))
                steps.then(nc.vector.tensor_scalar(first[:, EXPERTS:ROUNDS], first[:, EXPERTS:ROUNDS], float(P) - FAR, FAR, ALU.mult, ALU.add))
                steps.then(nc.vector.memset(first[:, ROUNDS:ROUNDS + 1], FAR))
                steps.then(nc.vector.tensor_scalar(tab[:, ROUNDS + 1:ROUNDS + 2], rank[:, EXPERTS - 1:EXPERTS], float(EXPERTS), None, ALU.add))
                steps.then(nc.vector.tensor_copy(table[0:1, :], tab[0:1, :]))
                dve.wait_ge(turned.sem, turned.at(1))
                nc.vector.tensor_copy(gt[:, :, :], core.bank[1][0:EXPERTS, :].rearrange("p (k n) -> p k n", k=2)).then_inc(kept.sem, 1)
                for k, dst in enumerate((shares, place_rows)):
                    dve.wait_ge(spread.sem, spread.at(k + 1))
                    for b in range(4):
                        nc.vector.tensor_copy(dst[:, 2 * b:2 * b + 2, :], core.bank[4 + b][:, :].rearrange("p (e n) -> p e n", n=N))\
                            .then_inc(copied.sem, 1)
                n_own.append(steps.k)

            @block.scalar
            def _(act):
                for q in range(4):
                    act.wait_ge(flipped.sem, flipped.at(q + 1))
                    nc.scalar.activation(ht[:, q // 2, 512 * (q % 2):512 * (q % 2) + 512], core.bank[4 + q][:, :], ACT.Copy).then_inc(flips.sem, 1)
                act.wait_ge(ready.sem, ready.at(1))
                nc.scalar.activation(e[:], e[:], ACT.Exp).then_inc(expd.sem, 1)
        for c, k in ((loaded, 16), (scored, 1), (own, n_own.pop()), (expd, 1), (ready, 3), (turned, 1), (kept, 1), (spread, 2),
                     (copied, 8), (ranked, 1), (flipped, 4), (flips, 4)):
            c.passed(k)


def feed_forward(core, ctx, gu, down, hid, next_tiles, x, gate):
    nc = core.nc
    sg = core.sb(ctx, "silu", [P, 2, N])
    used, free = core.tiles_used, core.pair_free
    silued, ready, read = core.count("ffn_silu"), core.count("ffn_hidden"), core.count("ffn_read")
    R1, R2 = 2 * FT // U, FT // U
    R = R1 + R2
    with nc.Block() as block:

        @block.sync
        def _(sp):
            with sp.Fori(1, R1) as i:
                for u in range(U):
                    sp.wait_ge(used.sem, used.at(u + 1 - U) + i * U)
                    core.load_tile(sp, u, gu[u % 2, i * 2 + u // 2])
            with sp.Fori(0, R2) as i:
                for u in range(U):
                    sp.wait_ge(used.sem, used.at(U * R1 + u + 1 - U) + i * U)
                    core.load_tile(sp, u, down[i * U + u])
            for u in range(U):
                sp.wait_ge(used.sem, used.at(U * R - U + u + 1))
                core.load_tile(sp, u, next_tiles(u))

        @block.tensor
        def _(pe):
            zero_banks(core, pe, range(4, 8))
            with pe.Fori(0, R1) as i:
                for u in range(U):
                    pe.wait_ge(core.landed[u].sem, core.landed[u].at(16) + i * 16)
                    if u % 2 == 0:
                        pe.wait_ge(free.sem, free.at(u // 2 + 1) + i * 2)
                    for c in range(C):
                        last = nc.tensor.matmul(core.bank[u][:, 0:N], core.slot[u][:, c, :], core.h[:, c, :], start=(c == 0), stop=(c == C - 1))
                    last.then_inc(used.sem, 1)
            with pe.Fori(0, R2) as i:
                for u in range(U):
                    pe.wait_ge(core.landed[u].sem, core.landed[u].at(16 * R1 + 16) + i * 16)
                    pe.wait_ge(ready.sem, ready.at(u + 1) + i * U)
                    add_products(core, u, hid[:, bass.ds(i * U + u, 1), :].rearrange("p o n -> p (o n)")).then_inc(used.sem, 1)
            for b in range(4, 8):
                last = nc.tensor.matmul(core.bank[b][:, :], core.zeros[:, 0:P], core.zeros[:, :], start=False, stop=True, skip_group_check=True)
            last.then_inc(read.sem, 1)

        @block.scalar
        def _(act):
            with act.Fori(0, R1) as i:
                for w in range(2):
                    act.wait_ge(used.sem, used.at(2 * w + 1) + i * U)
                    nc.scalar.activation(sg[:, w, :], core.bank[2 * w][:, 0:N], ACT.Silu).then_inc(silued.sem, 1)

        @block.vector
        def _(dve):
            with dve.Fori(0, R1) as i:
                for w in range(2):
                    dve.wait_ge(silued.sem, silued.at(w + 1) + i * 2)
                    dve.wait_ge(used.sem, used.at(2 * w + 2) + i * U)
                    out = hid[:, bass.ds(i * 2 + w, 1), :].rearrange("p o n -> p (o n)")
                    nc.vector.tensor_tensor(out, sg[:, w, :], core.bank[2 * w + 1][:, 0:N], ALU.mult).then_inc(free.sem, 1)
                    dve.wait_ge(free.sem, free.at(2 + w + 1) + i * 2)
                    dve.sem_inc(ready.sem, 1)
            dve.wait_ge(read.sem, read.at(1))
            for m in range(C):
                nc.vector.scalar_tensor_tensor(x[:, m, :], core.bank[4 + m // 2][:, (m % 2) * N:(m % 2) * N + N], gate[:, m:m + 1], x[:, m, :],
                                               ALU.mult, ALU.add).then_inc(read.sem, 1)
    used.passed(U * R)
    free.passed(FT)
    silued.passed(FT)
    ready.passed(FT)
    read.passed(1 + C)
    for u in range(U):
        core.landed[u].passed(16 * R)


def routed_feed_forward(core, ctx, a, x, gate):
    nc = core.nc
    sb = lambda name, shape, dt=F32: core.sb(ctx, name, shape, dt)
    r = dict(shares=sb("shares", [P, EXPERTS, N]), place_rows=sb("place_rows", [P, EXPERTS, N]),
             place_cols=sb("place_cols", [P, 2, EXPERTS]), first=sb("first", [P, ROUNDS + 1]),
             table=sb("round_table", [1, ROUNDS + 2], I32), ht=sb("h_tokens", [P, 2, D]))
    route(core, a, r)
    shares, place_rows, place_cols, first, table, ht = (r[k] for k in ("shares", "place_rows", "place_cols", "first", "table", "ht"))
    M = P
    hid = sb("hid_r", [P, FT, M])
    xg = sb("xg", [P, C, M])
    yg = sb("yg", [P, D])
    pick = sb("pick", [P, 2, M])
    back = sb("back", [P, N])
    sg = sb("silu_r", [P, 2, M])
    used, free = core.tiles_used, core.pair_free
    silued, ready = core.count("ffn_silu"), core.count("ffn_hidden")
    picks, gathered, xg_ready, backs, y_kept, scattered, added, offs = (core.count(n) for n in (
        "picks_ready", "tokens_gathered", "gathered_copied", "backs_ready", "outputs_kept", "outputs_scattered", "outputs_added",
        "place_offset"))
    own = core.count("round_vector_steps")
    off = sb("offset", [P, 1])
    R1, R2 = 2 * FT // U, FT // U
    R = R1 + R2
    T = U * R
    gu, down = a["moe_gu"], a["moe_d"]

    def n_rounds(eng):
        return eng.value_load(table[0:1, ROUNDS + 1:ROUNDS + 2], min_val=EXPERTS, max_val=ROUNDS)

    def expert_of(eng, k):
        return eng.value_load(table[0:1, bass.ds(k, 1)], min_val=0, max_val=EXPERTS - 1)

    with nc.Block() as block:

        @block.sync
        def _(sp):
            def load(k, e, start):
                with sp.Fori(start, R1) as i:
                    for u in range(U):
                        sp.wait_ge(used.sem, used.at(u + 1 - U) + k * T + i * U)
                        core.load_tile(sp, u, gu[u % 2, e * FT + i * 2 + u // 2])
                with sp.Fori(0, R2) as i:
                    for u in range(U):
                        sp.wait_ge(used.sem, used.at(U * R1 + u + 1 - U) + k * T + i * U)
                        core.load_tile(sp, u, down[e * FT + i * U + u])

            load(0, 0, 1)
            with sp.Fori(1, n_rounds(sp)) as k:
                load(k, expert_of(sp, k), 0)

        @block.tensor
        def _(pe):
            def gather(k):
                pe.wait_ge(picks.sem, picks.at(1) + k)
                for b in range(2):
                    for j in range(4):
                        for tt in range(2):
                            c = 4 * b + j
                            last = nc.tensor.matmul(core.bank[6 + b][:, j * M:j * M + M], ht[:, tt, c * P:c * P + P], pick[:, tt, :],
                                                    start=(tt == 0), stop=(tt == 1))
                    last.then_inc(gathered.sem, 1)

            gather(0)
            with pe.Fori(0, n_rounds(pe)) as k:
                with pe.Fori(0, R1) as i:
                    pe.wait_ge(xg_ready.sem, xg_ready.at(2) + k * 2)
                    for u in range(U):
                        pe.wait_ge(core.landed[u].sem, core.landed[u].at(16) + k * (16 * R) + i * 16)
                        if u % 2 == 0:
                            pe.wait_ge(free.sem, free.at(u // 2 + 1) + k * FT + i * 2)
                        for c in range(C):
                            last = nc.tensor.matmul(core.bank[u][:, 0:M], core.slot[u][:, c, :], xg[:, c, :], start=(c == 0), stop=(c == C - 1))
                        last.then_inc(used.sem, 1)
                for t in range(FT):
                    u = t % U
                    pe.wait_ge(core.landed[u].sem, core.landed[u].at(16 * (R1 + t // U + 1)) + k * (16 * R))
                    pe.wait_ge(ready.sem, ready.at(t + 1) + k * FT)
                    for b in range(2):
                        last = nc.tensor.matmul(core.bank[4 + b][:, :], hid[:, t, :], core.slot[u][:, 4 * b:4 * b + 4, :].rearrange("p c m -> p (c m)"),
                                                start=(t == 0), stop=(t == FT - 1))
                    last.then_inc(used.sem, 1)
                gather(k + 1)
                pe.wait_ge(backs.sem, backs.at(1) + k)
                pe.wait_ge(y_kept.sem, y_kept.at(2) + k * 2)
                for s in range(4):
                    if s < 2:
                        pe.wait_ge(xg_ready.sem, xg_ready.at(2 + s + 1) + k * 2)
                    else:
                        pe.wait_ge(added.sem, added.at(2 * (s - 1)) + k * C)
                    for j in range(2):
                        m = 2 * s + j
                        last = nc.tensor.matmul(core.bank[6 + s % 2][:, j * N:j * N + N], yg[:, m * P:m * P + P], back[:, :], start=True, stop=True)
                    last.then_inc(scattered.sem, 1)

        @block.scalar
        def _(act):
            def copy_gathered(k):
                for b in range(2):
                    act.wait_ge(gathered.sem, gathered.at(b + 1) + k * 2)
                    nc.scalar.activation(xg[:, 4 * b:4 * b + 4, :], core.bank[6 + b][:, :].rearrange("p (c m) -> p c m", m=M), ACT.Copy)\
                        .then_inc(xg_ready.sem, 1)

            copy_gathered(0)
            with act.Fori(0, n_rounds(act)) as k:
                with act.Fori(0, R1) as i:
                    for w in range(2):
                        act.wait_ge(used.sem, used.at(2 * w + 1) + k * T + i * U)
                        nc.scalar.activation(sg[:, w, :], core.bank[2 * w][:, 0:M], ACT.Silu).then_inc(silued.sem, 1)
                act.wait_ge(used.sem, used.at(T) + k * T)
                for b in range(2):
                    nc.scalar.activation(yg[:, 512 * b:512 * b + 512], core.bank[4 + b][:, :], ACT.Copy).then_inc(y_kept.sem, 1)
                copy_gathered(k + 1)

        @block.vector
        def _(dve):
            def make_pick(k):
                e = expert_of(dve, k)
                for tt in range(2):
                    ins = nc.vector.tensor_scalar(pick[:, tt, :], core.iota, first[:, bass.ds(k, 1)], place_cols[:, tt, bass.ds(e, 1)],
                                                  ALU.add, ALU.is_equal)
                ins.then_inc(picks.sem, 1)

            make_pick(0)
            with dve.Fori(0, n_rounds(dve)) as k:
                dve.wait_ge(gathered.sem, gathered.at(2) + k * 2)
                make_pick(k + 1)
                e = expert_of(dve, k)
                nc.vector.tensor_tensor(off[:], core.col("partition", 0), first[:, bass.ds(k, 1)], ALU.add).then_inc(offs.sem, 1)
                dve.wait_ge(offs.sem, offs.at(1) + k)
                nc.vector.scalar_tensor_tensor(back[:, :], place_rows[:, bass.ds(e, 1), :].rearrange("p o n -> p (o n)"), off[:, 0:1],
                                               shares[:, bass.ds(e, 1), :].rearrange("p o n -> p (o n)"), ALU.is_equal, ALU.mult)\
                    .then_inc(backs.sem, 1)
                with dve.Fori(0, R1) as i:
                    for w in range(2):
                        dve.wait_ge(silued.sem, silued.at(w + 1) + k * FT + i * 2)
                        dve.wait_ge(used.sem, used.at(2 * w + 2) + k * T + i * U)
                        out = hid[:, bass.ds(i * 2 + w, 1), :].rearrange("p o n -> p (o n)")
                        nc.vector.tensor_tensor(out, sg[:, w, :], core.bank[2 * w + 1][:, 0:M], ALU.mult).then_inc(free.sem, 1)
                        dve.wait_ge(free.sem, free.at(2 + w + 1) + k * FT + i * 2)
                        dve.sem_inc(ready.sem, 1)
                for s in range(4):
                    dve.wait_ge(scattered.sem, scattered.at(s + 1) + k * 4)
                    for j in range(2):
                        m = 2 * s + j
                        nc.vector.scalar_tensor_tensor(x[:, m, :], core.bank[6 + s % 2][:, j * N:j * N + N], gate[:, m:m + 1], x[:, m, :],
                                                       ALU.mult, ALU.add).then_inc(added.sem, 1)



def as_columns(v):
    return np.ascontiguousarray(v.reshape(-1, P).T)


def as_tiles(w):
    k, m = w.shape
    return np.ascontiguousarray(w.reshape(k // P, P, m // P, P).transpose(2, 1, 0, 3)).reshape(m // P, P, k)


def constants():
    const = np.zeros((N_CONST, P, P), np.float32)
    const[0] = np.eye(P)
    for d in range(P):
        h = d % DH
        if h < DH // 2:
            const[1, d + DH // 2, d] = -1.0
        else:
            const[1, d - DH // 2, d] = 1.0
    const[2] = np.arange(P)[None, :]
    for e in range(EXPERTS):
        const[3 + e, e, :] = 1.0
    const[3 + EXPERTS] = np.triu(np.ones((P, P)), 1)
    i = np.arange(P)
    mask = np.zeros((LEVELS + 1, P, P), np.int32)
    for l in range(LEVELS):
        same = (i[:, None] >> (l + 1)) == (i[None, :] >> (l + 1))
        mask[l] = same & ((i[:, None] >> l) != (i[None, :] >> l))
    mask[LEVELS] = np.eye(P)
    return const, mask


def lay_out(x, c, ctx, c_ctx, w_ada, b_ada, w_in, w_gk2, b_gk, hg_lower_bounds, hg_norm, gla_norm,
            w_out, ln_gamma, ln_beta, peer_w_query, peer_sub_keys, peer_u, peer_v, c_2, positions_2,
            ada_w_2, ada_b_2, ln1_g_2, ln2_g_2, w_in_2, conv_w_2, conv_b_2, gate_a_w_2, gate_a_b_2,
            gate_x_w_2, gate_x_b_2, lru_lambda_2, lam_q1_2, lam_k1_2, lam_q2_2, lam_k2_2, subln_g_2,
            w_out_2, ffn_w_gate_2, ffn_w_up_2, ffn_w_down_2, moe_router_2, moe_w_gate_2, moe_w_up_2,
            moe_w_down_2, final_g_2):
    a = {}
    tokens = np.concatenate([ctx[0], x[0]], axis=0)
    a["x"] = np.ascontiguousarray(tokens.reshape(L, C, P).transpose(2, 1, 0))
    vec = np.zeros((P, NVEC), np.float32)

    def put(name, block):
        at, n = COLS[name]
        vec[:, at:at + n] = block

    cc = np.stack([c[0], c_ctx]).reshape(2, C, P).transpose(2, 1, 0).reshape(P, 2 * C)
    put("c", cc)
    put("b_ada", as_columns(b_ada))
    put("lb", as_columns(hg_lower_bounds))
    put("b_gk", as_columns(b_gk))
    put("hg_norm", as_columns(hg_norm))
    put("gla_norm", as_columns(gla_norm))
    for j in range(2):
        put(f"ln_gamma{j}", as_columns(ln_gamma[0, j]))
        put(f"ln_beta{j}", as_columns(ln_beta[0, j]))
    put("c_2", as_columns(c_2))
    put("final_g", as_columns(final_g_2))
    half = np.arange(P) % (DH // 2)
    put("inv_freq", (np.float32(10000.0) ** (-(2 * half).astype(np.float32) / np.float32(DH)))[:, None])
    put("one", 1.0)
    put("eps", EPS)
    put("halfpi", TWO_PI / 4)
    put("partition", np.arange(P, dtype=np.float32)[:, None])
    for l in range(DEPTH_2):
        for name, v in (("ada_b", ada_b_2), ("ln1_g", ln1_g_2), ("ln2_g", ln2_g_2), ("conv_w", conv_w_2), ("conv_b", conv_b_2),
                        ("gate_a_b", gate_a_b_2), ("gate_x_b", gate_x_b_2), ("lru_lambda", lru_lambda_2), ("subln_g", subln_g_2)):
            put(f"{name}{l}", as_columns(v[l]))
    a["vec"] = vec
    a["const"], a["mask"] = constants()
    a["w_ada"] = np.ascontiguousarray(w_ada[0].reshape(C, P, 6, D).transpose(2, 0, 1, 3)).reshape(6 * C, P, D)
    a["ada_w_2"] = np.concatenate([as_tiles(ada_w_2[l]) for l in range(DEPTH_2)])
    w = w_in[0]
    at = np.cumsum([0, 512, 512, 512, 512, 512, 256, 256, 512, 512, 16, 16])
    hq, hff, hfb, hi, hg, gq, gk, gv, gg = (w[:, at[i]:at[i + 1]] for i in range(9))
    a["w_in"] = as_tiles(np.concatenate([hff, hfb, gk, gq, hq, hg, gg, hi, gv], axis=1))
    a["w_rank"] = np.ascontiguousarray(w[:, at[9]:at[11]].reshape(C, P, 32).transpose(1, 0, 2))
    a["w_gk2"] = np.ascontiguousarray(w_gk2[0].transpose(1, 0, 2))
    a["w_out"] = as_tiles(w_out[0])
    a["w_query"] = as_tiles(peer_w_query[0])
    a["keys"] = np.ascontiguousarray(peer_sub_keys[0].transpose(2, 0, 1))
    a["peer_u"] = np.ascontiguousarray(peer_u[0].reshape(P, P, C, P).transpose(0, 3, 2, 1)).reshape(P, P, D)
    a["peer_v"] = peer_v[0].reshape(P, P, D)
    a["w_in_2"] = np.concatenate([as_tiles(w_in_2[l]) for l in range(DEPTH_2)])
    a["w_out_2"] = np.concatenate([as_tiles(w_out_2[l]) for l in range(DEPTH_2)])
    gates_w = np.zeros((DEPTH_2, P, 2, 4, P), np.float32)
    for l in range(DEPTH_2):
        for w_, src in enumerate((gate_a_w_2, gate_x_w_2)):
            for n in range(8):
                r = 64 * (n % 2)
                gates_w[l, r:r + 64, w_, n // 2, r:r + 64] = src[l, n]
    a["lru_gates"] = gates_w
    a["pos"] = positions_2[0]
    a["pos_cols"] = np.ascontiguousarray(positions_2[0].reshape(2, P).T)
    a["lam_rows"] = np.stack([lam_q1_2, lam_k1_2, lam_q2_2, lam_k2_2], axis=1)[None]
    a["ffn_gu"] = np.stack([as_tiles(ffn_w_gate_2[0]), as_tiles(ffn_w_up_2[0])])
    a["ffn_d"] = ffn_w_down_2[0].reshape(FT, P, D)
    a["moe_gu"] = np.stack([np.concatenate([as_tiles(w_[0, e]) for e in range(EXPERTS)]) for w_ in (moe_w_gate_2, moe_w_up_2)])
    a["moe_d"] = moe_w_down_2[0].reshape(EXPERTS * FT, P, D)
    a["router"] = np.ascontiguousarray(moe_router_2[0].reshape(C, P, EXPERTS).transpose(1, 0, 2))
    return a


def kernel(**inputs):
    import concourse.bacc as bacc
    from concourse.bass_utils import run_bass_kernel_spmd

    arrays = lay_out(**{k: np.asarray(v) for k, v in inputs.items()})
    nc = bacc.Bacc("TRN2", target_bir_lowering=False, num_devices=1)
    a = {}
    for name, v in arrays.items():
        a[name] = nc.dram_tensor(f"in_{name}", v.shape, mybir.dt.from_np(v.dtype), kind="ExternalInput").ap()
    a["out"] = nc.dram_tensor("out", [P, C, N], F32, kind="ExternalOutput").ap()
    kernel_program(nc, a)
    r = run_bass_kernel_spmd(nc, [{f"in_{k}": v for k, v in arrays.items()}], core_ids=[0])
    out = r.results[0]["out"]
    return np.ascontiguousarray(out.transpose(2, 1, 0)).reshape(1, N, D)
```

```python
from contextlib import ExitStack

import numpy as np

import concourse.bass as bass
from concourse import mybir

F32 = mybir.dt.float32
F32R = mybir.dt.float32r
I32 = mybir.dt.int32
U32 = mybir.dt.uint32
ALU = mybir.AluOpType
ACT = mybir.ActivationFunctionType
AX = mybir.AxisListType

P = 128
D = 1024
C = D // P
N = 256
NC = 256
L = N + NC
U = 4
EPS = 1e-6
ALPHA = 2.0 ** 0.25
LB_FLOOR = 1e-30
GRID_W = 64
ROWS = N // GRID_W
CH = 128
LEVELS = 7
TOPK = 16
HEADS = 8
LN2 = 0.6931471805599453
NEG = -3.0e38
PLACED = (0, 1, 2, 3, 4, 6, 5, 7)
TWO_PI = 6.283185307179586
PI_A = 6.28125
PI_B = 0.0019350051879882812
PI_C = TWO_PI - PI_A - PI_B
ROUND = 12582912.0
DEPTH_2 = 2
D_FF = 3072
FT = D_FF // P
EXPERTS = 8
MORE = 3
ROUNDS = EXPERTS + MORE
FAR = 1.0e6
DH = 64


def column_map():
    sizes = [("c", 16), ("b_ada", 48), ("lb", 8), ("b_gk", 4), ("hg_norm", 1), ("gla_norm", 1),
             ("ln_gamma0", 8), ("ln_gamma1", 8), ("ln_beta0", 8), ("ln_beta1", 8), ("c_2", 8),
             ("final_g", 8), ("inv_freq", 1), ("one", 1), ("eps", 1), ("halfpi", 1),
             ("partition", 1)]
    for l in range(DEPTH_2):
        sizes += [(f"ada_b{l}", 48), (f"ln1_g{l}", 8), (f"ln2_g{l}", 8), (f"conv_w{l}", 16), (f"conv_b{l}", 4),
                  (f"gate_a_b{l}", 4), (f"gate_x_b{l}", 4), (f"lru_lambda{l}", 4), (f"subln_g{l}", 1)]
    at, out = 0, {}
    for name, n in sizes:
        out[name] = (at, n)
        at += n
    return out, at


COLS, NVEC = column_map()
N_CONST = 4 + EXPERTS


class Count:

    def __init__(self, sem):
        self.sem = sem
        self.base = 0

    def at(self, k):
        return self.base + k

    def passed(self, k):
        self.base += k


class Steps:

    def __init__(self, eng, count, start=0):
        self.eng, self.count, self.k, self.start = eng, count, 0, start

    def then(self, ins):
        ins.then_inc(self.count.sem, 1)
        self.k += 1
        self.eng.wait_ge(self.count.sem, self.start + self.count.at(self.k))


class Core:

    def __init__(self, nc, ctx):
        self.nc, self.ctx = nc, ctx
        self.counts = {}
        self.norms = 0
        self.bank = [ctx.enter_context(nc.psum_tensor(f"bank{i}", [P, 512], F32)) for i in range(8)]
        self.slot = [ctx.enter_context(nc.sbuf_tensor(f"slot{u}", [P, C, P], F32)) for u in range(U)]
        self.landed = [self.count(f"tile_landed_{u}") for u in range(U)]
        self.tiles_used = self.count("tiles_used")
        self.bank_free = self.count("bank_free")
        self.pair_free = self.count("pair_free")

    def sb(self, ctx, name, shape, dt=F32):
        return ctx.enter_context(self.nc.sbuf_tensor(name, shape, dt))

    def count(self, name):
        if name not in self.counts:
            self.counts[name] = Count(self.ctx.enter_context(self.nc.semaphore(name)))
        return self.counts[name]

    def load_tile(self, sp, u, tile):
        sp.dma_start(self.slot[u][:].rearrange("p c m -> p (c m)"), tile).then_inc(self.landed[u].sem, 16)


def project(core, tiles, T, products, evacuate, next_tiles):
    nc = core.nc
    used, free = core.tiles_used, core.bank_free
    rounds = T // U
    with nc.Block() as block:

        @block.sync
        def _(sp):
            if rounds > 1:
                with sp.Fori(1, rounds) as i:
                    for u in range(U):
                        sp.wait_ge(used.sem, used.at(1 - U) + i * U + u)
                        core.load_tile(sp, u, tiles(i * U + u))
            for u in range(U):
                sp.wait_ge(used.sem, used.at(T - U + u + 1))
                if next_tiles is not None:
                    core.load_tile(sp, u, next_tiles(u))

        @block.tensor
        def _(pe):
            with pe.Fori(0, rounds) as i:
                for u in range(U):
                    pe.wait_ge(core.landed[u].sem, core.landed[u].at(16) + i * 16)
                    pe.wait_ge(free.sem, free.at(u + 1) + i * U)
                    products(pe, i * U + u, u).then_inc(used.sem, 1)

        @block.vector
        def _(dve):
            with dve.Fori(0, rounds) as i:
                for u in range(U):
                    dve.wait_ge(used.sem, used.at(u + 1) + i * U)
                    evacuate(dve, i * U + u, u).then_inc(free.sem, 1)

    used.passed(T)
    free.passed(T)
    for u in range(U):
        core.landed[u].passed(16 * rounds)


class Split:

    def __init__(self, core, ctx, name, source, n):
        self.source = source
        self.high, self.low = (core.sb(ctx, f"{name}_{part}", [P, C, n], F32R) for part in ("high", "low"))
        self.made = False


class Halver:

    def __init__(self, core, ctx, name):
        self.core = core
        self.tile_hi, self.tile_lo = (core.sb(ctx, f"{name}_tile_{part}", [P, 2, C, P], F32R) for part in ("high", "low"))
        self.hi_ready, self.lo_ready, self.hi_used, self.moving_split, self.low_split = (
            core.count(n) for n in ("tile_high_ready", "tile_low_ready", "tile_high_used", "moving_high", "moving_low"))

    def credit(self, act):
        act.sem_inc(self.hi_used.sem, 2)
        act.sem_inc(self.lo_ready.sem, 2)

    def high(self, act, place, i):
        core, u = self.core, place % U
        act.wait_ge(core.landed[u].sem, core.landed[u].at(16 * (place // U + 1)) + i * 16)
        act.wait_ge(self.hi_used.sem, self.hi_used.at(place + 1) + i * 4)
        act.wait_ge(self.lo_ready.sem, self.lo_ready.at(place + 1) + i * 4)
        core.nc.scalar.activation(self.tile_hi[:, place % 2], core.slot[u][:], ACT.Copy).then_inc(self.hi_ready.sem, 1)

    def lower(self, dve, place, i):
        core, slot = self.core, self.core.slot[place % U]
        if not isinstance(i, int) or place + 4 * i >= 2:
            dve.wait_ge(core.tiles_used.sem, core.tiles_used.at(place - 1) + i * 4)
        dve.wait_ge(self.hi_ready.sem, self.hi_ready.at(place + 1) + i * 4)
        core.nc.vector.tensor_tensor(self.tile_lo[:, place % 2], slot[:], self.tile_hi[:, place % 2].bitcast(F32), ALU.subtract)\
            .then_inc(self.lo_ready.sem, 1)

    def products(self, pe, place, i, out, high, low, opens, closes):
        core, nc, skip = self.core, self.core.nc, not (opens and closes)
        pe.wait_ge(self.hi_ready.sem, self.hi_ready.at(place + 1) + i * 4)
        for c in range(C):
            nc.tensor.matmul(out(c), self.tile_hi[:, place % 2, c, :], high(c), start=(opens and c == 0), stop=False, skip_group_check=skip)
            last = nc.tensor.matmul(out(c), self.tile_hi[:, place % 2, c, :], low(c), start=False, stop=False, skip_group_check=skip)
        last.then_inc(self.hi_used.sem, 1)
        pe.wait_ge(self.lo_ready.sem, self.lo_ready.at(place + 3) + i * 4)
        for c in range(C):
            last = nc.tensor.matmul(out(c), self.tile_lo[:, place % 2, c, :], high(c), start=False,
                                    stop=(closes and c == C - 1), skip_group_check=skip)
        last.then_inc(core.tiles_used.sem, 1)

    def reload(self, sp, place, i, tile):
        sp.wait_ge(self.lo_ready.sem, self.lo_ready.at(place - 1) + i * 4)
        self.core.load_tile(sp, place % U, tile)

    def split_high(self, act, split):
        for c in range(C):
            self.core.nc.scalar.activation(split.high[:, c, :], split.source[:, c, :], ACT.Copy).then_inc(self.moving_split.sem, 1)

    def split_low(self, dve, split):
        for c in range(C):
            dve.wait_ge(self.moving_split.sem, self.moving_split.at(c + 1))
            self.core.nc.vector.tensor_tensor(split.low[:, c, :], split.source[:, c, :], split.high[:, c, :].bitcast(F32), ALU.subtract)\
                .then_inc(self.low_split.sem, 1)

    def passed(self, tiles, split_moving):
        self.hi_ready.passed(tiles)
        self.hi_used.passed(tiles + 2)
        self.lo_ready.passed(tiles + 2)
        self.moving_split.passed(C if split_moving else 0)
        self.low_split.passed(C if split_moving else 0)


def project_split(core, halver, tiles, T, split, lo, n, evacuate, next_tiles):
    used, free = core.tiles_used, core.bank_free
    rounds = T // U
    fresh = not split.made
    split.made = True
    cut = lambda t: (lambda c: t[:, c, lo:lo + n])
    with core.nc.Block() as block:

        @block.sync
        def _(sp):
            if rounds > 1:
                with sp.Fori(1, rounds) as i:
                    for u in range(U):
                        halver.reload(sp, u, i, tiles(i * U + u))
            for u in range(U):
                halver.reload(sp, T + u, 0, next_tiles(u))

        @block.scalar
        def _(act):
            halver.credit(act)
            if fresh:
                halver.split_high(act, split)
            with act.Fori(0, rounds) as i:
                for u in range(U):
                    halver.high(act, u, i)

        @block.tensor
        def _(pe):
            if fresh:
                pe.wait_ge(halver.low_split.sem, halver.low_split.at(C))
            with pe.Fori(0, rounds) as i:
                for u in range(U):
                    pe.wait_ge(free.sem, free.at(u + 1) + i * U)
                    halver.products(pe, u, i, lambda c: core.bank[u][:, 0:n], cut(split.high), cut(split.low), True, True)

        @block.vector
        def _(dve):
            def empty(t, u, i):
                dve.wait_ge(used.sem, used.at(u + 1) + i * U)
                evacuate(dve, t, u).then_inc(free.sem, 1)

            if fresh:
                halver.split_low(dve, split)
            for u in range(U):
                halver.lower(dve, u, 0)
                if u >= 2:
                    empty(u - 2, u - 2, 0)
            if rounds > 1:
                with dve.Fori(1, rounds) as i:
                    for u in range(U):
                        halver.lower(dve, u, i)
                        if u < 2:
                            empty(i * U + u - 2, u + 2, i - 1)
                        else:
                            empty(i * U + u - 2, u - 2, i)
            for u in (2, 3):
                empty(T - U + u, u, rounds - 1)
    used.passed(T)
    free.passed(T)
    halver.passed(T, fresh)
    for u in range(U):
        core.landed[u].passed(16 * rounds)


def norm(core, x, n, out, centre, groups, xc, sq):
    core.norms += 1
    with ExitStack() as ctx:
        norm_in(core, x, n, out, centre, groups, xc, sq, core.sb(ctx, f"deviation{core.norms}", [P, 2, n]))


def norm_in(core, x, n, out, centre, groups, xc, sq, work):
    nc = core.nc
    mean_ready, centred, squared = core.count("mean_ready"), core.count("centred"), core.count("squared")
    var_ready, std_ready = core.count("var_ready"), core.count("std_ready")
    scaled, shifted, own = core.count("scaled"), core.count("shifted"), core.count("norm_vector_steps")
    mean, var, std, rstd = core.bank[4], core.bank[5], work[:, 0], work[:, 1]
    src = xc if centre else x
    n_scaled = C * len(groups)
    with nc.Block() as block:

        @block.tensor
        def _(pe):
            if centre:
                for c in range(C):
                    last = nc.tensor.matmul(mean[:, 0:n], core.avg[:], x[:, c, 0:n], start=(c == 0), stop=(c == C - 1))
                last.then_inc(mean_ready.sem, 1)
            for c in range(C):
                pe.wait_ge(squared.sem, squared.at(c + 1))
                last = nc.tensor.matmul(var[:, 0:n], core.avg[:], sq[:, c, 0:n], start=(c == 0), stop=(c == C - 1))
            last.then_inc(var_ready.sem, 1)

        @block.vector
        def _(dve):
            steps = Steps(dve, own)
            if centre:
                dve.wait_ge(mean_ready.sem, mean_ready.at(1))
                for c in range(C):
                    nc.vector.tensor_tensor(xc[:, c, 0:n], x[:, c, 0:n], mean[:, 0:n], ALU.subtract)\
                        .then_inc(centred.sem, 1)
            dve.wait_ge(std_ready.sem, std_ready.at(1))
            if centre:
                dve.wait_ge(centred.sem, centred.at(C))
            steps.then(nc.vector.reciprocal(rstd[:, 0:n], std[:, 0:n]))
            for lo, hi, gain, shift in groups:
                for c in range(C):
                    nc.vector.scalar_tensor_tensor(out[:, c, lo:hi], src[:, c, lo:hi], gain[:, c:c + 1],
                                                   rstd[:, lo:hi], ALU.mult, ALU.mult).then_inc(scaled.sem, 1)

        @block.scalar
        def _(act):
            for c in range(C):
                if centre:
                    act.wait_ge(centred.sem, centred.at(c + 1))
                nc.scalar.activation(sq[:, c, 0:n], src[:, c, 0:n], ACT.Square).then_inc(squared.sem, 1)
            act.wait_ge(var_ready.sem, var_ready.at(1))
            nc.scalar.activation(std[:, 0:n], var[:, 0:n], ACT.Sqrt, bias=core.col("eps", 0)).then_inc(std_ready.sem, 1)
            k = 0
            for lo, hi, gain, shift in groups:
                for c in range(C):
                    k += 1
                    if shift is not None:
                        act.wait_ge(scaled.sem, scaled.at(k))
                        nc.scalar.activation(out[:, c, lo:hi], out[:, c, lo:hi], ACT.Identity, bias=shift[:, c:c + 1])\
                            .then_inc(shifted.sem, 1)

    mean_ready.passed(1 if centre else 0)
    centred.passed(C if centre else 0)
    squared.passed(C)
    var_ready.passed(1)
    std_ready.passed(1)
    own.passed(1)
    scaled.passed(n_scaled)
    shifted.passed(sum(C for g in groups if g[3] is not None))


def modulation(core, a):
    nc = core.nc
    used = core.tiles_used
    S = 6
    summed, column, added, silued, own = (core.count(n) for n in ("mod_rows_summed", "mod_columns_made", "mod_added", "vector_silu", "mod_vector_steps"))
    with ExitStack() as ctx:
        cs = core.sb(ctx, "cs", [P, C, 2])
        acc = core.sb(ctx, "acc", [P, 2, 2, D])
        ones = core.sb(ctx, "ones_col", [P, 2])
        with nc.Block() as block:

            @block.sync
            def _(sp):
                with sp.Fori(1, S * C // U) as i:
                    for u in range(U):
                        sp.wait_ge(used.sem, used.at(1 - U) + i * U + u)
                        core.load_tile(sp, u, a["w_ada"][i * U + u])
                for u in range(U):
                    sp.wait_ge(used.sem, used.at(S * C - U + u + 1))
                    core.load_tile(sp, u, a["w_in"][u])

            @block.scalar
            def _(act):
                nc.scalar.activation(cs[:].rearrange("p c n -> p (c n)"), core.vcols("c"), ACT.Silu).then_inc(silued.sem, 1)
                nc.scalar.activation(core.c2s[:].rearrange("p c n -> p (c n)"), core.vcols("c_2"), ACT.Silu).then_inc(silued.sem, 1)

            def round_(dve, i, vectors, s0):
                k = 0
                for w in range(2):
                    if not isinstance(i, int):
                        dve.wait_ge(column.sem, column.at(w + 1) + i * 2 - 2)
                    for c in range(C):
                        t = w * C + c
                        dve.wait_ge(core.landed[t % U].sem, core.landed[t % U].at(16 * (t // U + 1)) + i * (16 * 4))
                        src = core.slot[t % U][:].rearrange("p c m -> p (c m)")
                        for j in range(vectors):
                            if c > 0:
                                dve.wait_ge(own.sem, own.at(s0 + k - vectors + 1) + i * (16 * vectors))
                            if c == 0:
                                ins = nc.vector.tensor_scalar(acc[:, w, j, :], src, cs[:, c, j:j + 1], None, ALU.mult)
                            else:
                                ins = nc.vector.scalar_tensor_tensor(acc[:, w, j, :], src, cs[:, c, j:j + 1], acc[:, w, j, :], ALU.mult, ALU.add)
                            ins.then_inc(own.sem, 1)
                            k += 1
                        dve.wait_ge(own.sem, own.at(s0 + k) + i * (16 * vectors))
                        dve.sem_inc(used.sem, 1)
                    dve.sem_inc(summed.sem, 1)

            @block.vector
            def _(dve):
                nc.vector.memset(ones[:], 1.0).then_inc(added.sem, 1)
                dve.wait_ge(silued.sem, silued.at(1))
                round_(dve, 0, 2, 0)
                with dve.Fori(1, S // 2) as i:
                    round_(dve, i, 1, 16)
                dve.wait_ge(column.sem, column.at(S))
                nc.vector.tensor_tensor(core.mod[:, 0:16, :], core.bank[0][:, 0:32].rearrange("p (t n) -> p t n", n=2),
                                        core.vcols("b_ada")[:, 0:16].rearrange("p (t n) -> p t n", n=1).broadcast_to([P, 16, 2]), ALU.add)\
                    .then_inc(added.sem, 1)
                nc.vector.tensor_tensor(core.mod[:, 16:48, 0], core.bank[1][:, 0:32], core.vcols("b_ada")[:, 16:48], ALU.add)\
                    .then_inc(added.sem, 1)
                dve.wait_ge(added.sem, added.at(3))
                nc.vector.tensor_scalar(core.mod[:, 8:16, :], core.mod[:, 8:16, :], 1.0, None, ALU.add).then_inc(added.sem, 1)
                nc.vector.tensor_scalar(core.mod[:, 32:40, 0], core.mod[:, 32:40, 0], 1.0, None, ALU.add).then_inc(added.sem, 1)

            @block.tensor
            def _(pe):
                pe.wait_ge(added.sem, added.at(1))
                for w in range(2):
                    pe.wait_ge(summed.sem, summed.at(w + 1))
                    for m in range(C):
                        for j in range(2):
                            t = 2 * (w * C + m) + j
                            last = nc.tensor.matmul(core.bank[0][:, t:t + 1], acc[:, w, j, m * P:m * P + P], ones[:, 0:1], start=True, stop=True)
                    last.then_inc(column.sem, 1)
                with pe.Fori(1, S // 2) as i:
                    for w in range(2):
                        pe.wait_ge(summed.sem, summed.at(w + 1) + i * 2)
                        for m in range(C):
                            last = nc.tensor.matmul(core.bank[1][:, bass.ds((i - 1) * (2 * C) + w * C + m, 1)], acc[:, w, 0, m * P:m * P + P], ones[:, 0:1],
                                                    start=True, stop=True)
                        last.then_inc(column.sem, 1)
    used.passed(S * C)
    silued.passed(2)
    summed.passed(S)
    column.passed(S)
    added.passed(5)
    own.passed(32 + 32)
    for u in range(U):
        core.landed[u].passed(16 * S * C // U)


def gates(core, z, la, k_f, k_b, zt, lb):
    nc = core.nc
    own_a, own_v = core.count("gates_scalar_steps"), core.count("gates_vector_steps")
    soft, ls_ready, diff, keyed = (core.count(x) for x in ("softplus_ready", "log_sigmoid_ready", "key_log_ready", "keys_ready"))
    bound, lse = core.count("bounds_ready"), core.count("excess_ready")
    zf, tf, lf = ([t[:, s].rearrange("p t n -> p (t n)") for s in range(2)] for t in (z, zt, la))
    groups = ((0, 4), (6, 10))
    one = core.col("one", 0)
    hg = (0, 1, 2, 3, 6, 7, 8, 9)
    lbv, lbe, log_lb, log_1mlb, lb_gap, lbt = (lb[:, 8 * i:8 * i + 8] for i in range(6))
    landed, turn = core.count("gate_parts_landed"), core.count("gate_scalar_turns")
    with nc.Block() as block:

        @block.vector
        def _(dve):
            steps = Steps(dve, own_v)
            steps.then(nc.vector.tensor_tensor(lbv, core.vcols("lb"), core.vcols("lb"), ALU.subtract))
            nc.vector.tensor_copy(lbt, lbv).then_inc(bound.sem, 1)
            dve.wait_ge(own_a.sem, own_a.at(1))
            steps.then(nc.vector.reciprocal(lbv, lbe))
            steps.then(nc.vector.tensor_tensor(lbv, lbv, lbe, ALU.mult))
            steps.then(nc.vector.tensor_tensor(lbv, lbv, lbv, ALU.subtract))
            steps.then(nc.vector.tensor_scalar(lbv, lbv, 0.0, 1.0 - 1e-6, ALU.max, ALU.min))
            nc.vector.tensor_scalar(lbt, lbv, LB_FLOOR, None, ALU.max).then_inc(bound.sem, 1)
            dve.wait_ge(own_a.sem, own_a.at(3))
            steps.then(nc.vector.tensor_scalar(log_lb, log_lb, 60.0 * LN2, None, ALU.subtract))
            nc.vector.tensor_tensor(lb_gap, log_1mlb, log_lb, ALU.subtract).then_inc(bound.sem, 1)
            for s in range(2):
                dve.wait_ge(soft.sem, soft.at(s + 1))
                nc.vector.scalar_tensor_tensor(lf[s], zf[s], 0.0, tf[s], ALU.min, ALU.subtract).then_inc(ls_ready.sem, 1)
                dve.wait_ge(ls_ready.sem, ls_ready.at(s + 1))
                nc.vector.tensor_tensor(zf[s], lf[s], zf[s], ALU.subtract).then_inc(diff.sem, 1)
            dve.wait_ge(diff.sem, diff.at(2))
            for s in range(2):
                for lo, hi in groups:
                    nc.vector.tensor_scalar(la[:, s, hi:hi + 2, :], la[:, s, hi:hi + 2, :], 1.0 / 16.0, None, ALU.mult).then_inc(landed.sem, 1)
                dve.wait_ge(keyed.sem, keyed.at(8 * s + 8))
                for j, t in enumerate(hg):
                    nc.vector.tensor_scalar(la[:, s, t, :], la[:, s, t, :], log_1mlb[:, j:j + 1], log_lb[:, j:j + 1],
                                            ALU.add, ALU.max).then_inc(landed.sem, 1)
            for s in range(2):
                dve.wait_ge(lse.sem, lse.at(s + 1))
                dve.wait_ge(landed.sem, landed.at(20))
                for lo, hi in groups:
                    nc.vector.tensor_tensor(la[:, s, lo:hi, :], la[:, s, lo:hi, :], zt[:, s, lo:hi, :], ALU.add).then_inc(landed.sem, 1)

        @block.scalar
        def _(act):
            steps = Steps(act, own_a)
            act.wait_ge(bound.sem, bound.at(1))
            steps.then(nc.scalar.activation(lbe, lbt, ACT.Exp))
            act.wait_ge(bound.sem, bound.at(2))
            steps.then(nc.scalar.activation(log_lb, lbt, ACT.Ln, scale=2.0 ** 60))
            steps.then(nc.scalar.activation(log_1mlb, lbv, ACT.Ln, scale=-1.0, bias=one))
            for s in range(2):
                nc.scalar.activation(tf[s], zf[s], ACT.Abs).then_inc(turn.sem, 1)
            for s in range(2):
                act.wait_ge(turn.sem, turn.at(s + 1))
                nc.scalar.activation(tf[s], tf[s], ACT.Exp, scale=-1.0).then_inc(turn.sem, 1)
            for s in range(2):
                act.wait_ge(turn.sem, turn.at(s + 3))
                nc.scalar.activation(tf[s], tf[s], ACT.Ln, bias=one).then_inc(soft.sem, 1)
            act.wait_ge(bound.sem, bound.at(3))
            for s in range(2):
                act.wait_ge(diff.sem, diff.at(s + 1))
                for j, t in enumerate(hg):
                    nc.scalar.activation(zt[:, s, t, :], la[:, s, t, :], ACT.Abs, bias=lb_gap[:, j:j + 1])
                    keys = k_f if t < 6 else k_b
                    nc.scalar.activation(keys[:, s, t % 6, :], z[:, s, t, :], ACT.Exp, bias=log_1mlb[:, j:j + 1])\
                        .then_inc(keyed.sem, 1)
            act.wait_ge(keyed.sem, keyed.at(16))
            for s in range(2):
                for lo, hi in groups:
                    nc.scalar.activation(zt[:, s, lo:hi, :], zt[:, s, lo:hi, :], ACT.Exp, scale=-1.0).then_inc(turn.sem, 1)
            for s in range(2):
                act.wait_ge(turn.sem, turn.at(6 + 2 * s))
                for lo, hi in groups:
                    ins = nc.scalar.activation(zt[:, s, lo:hi, :], zt[:, s, lo:hi, :], ACT.Ln, bias=one)
                ins.then_inc(lse.sem, 1)
    own_a.passed(3)
    own_v.passed(6)
    for s, k in ((soft, 2), (ls_ready, 2), (diff, 2), (keyed, 16), (bound, 3), (lse, 2), (landed, 24), (turn, 8)):
        s.passed(k)


def kernel_program(nc, a):
    with ExitStack() as ctx:
        core = Core(nc, ctx)
        vec = core.sb(ctx, "vec", [P, NVEC])
        const = core.sb(ctx, "const", [P, N_CONST, P])
        core.avg = core.sb(ctx, "avg", [P, P])
        core.avg_head = core.sb(ctx, "avg_head", [P, P])
        core.zeros = core.sb(ctx, "zeros", [P, P])
        core.vcols = lambda name: vec[:, COLS[name][0]:COLS[name][0] + COLS[name][1]]
        core.col = lambda name, j: vec[:, COLS[name][0] + j:COLS[name][0] + j + 1]
        core.ident = const[:, 0, :]
        core.rot = const[:, 1, :]
        core.iota = const[:, 2, :]
        core.sel = const[:, 3:3 + EXPERTS, :]
        core.before = const[:, 3 + EXPERTS, :]
        core.x1 = core.sb(ctx, "x1", [P, C, N])
        core.mod = core.sb(ctx, "mod", [P, 48, 2])
        core.mod2 = core.sb(ctx, "mod2", [P, DEPTH_2 * 48, 1])
        core.c2s = core.sb(ctx, "c2s", [P, C, 1])
        start(core, a, vec, const)
        modulation(core, a)
        first_mixer(core, a)
        retrieval(core, a)
        core.h = core.sb(ctx, "h", [P, C, N])
        second_block(core, a)


def start(core, a, vec, const):
    nc = core.nc
    loaded, filled = core.count("start_loaded"), core.count("start_filled")
    with nc.Block() as block:

        @block.sync
        def _(sp):
            sp.dma_start(vec[:], a["vec"]).then_inc(loaded.sem, 16)
            for u in range(U):
                core.load_tile(sp, u, a["w_ada"][u])
            sp.dma_start(const[:], a["const"].rearrange("b p n -> p b n")).then_inc(loaded.sem, 16)
            sp.wait_ge(loaded.sem, 32)

        @block.vector
        def _(dve):
            nc.vector.memset(core.avg[:], 1.0 / D).then_inc(filled.sem, 1)
            nc.vector.memset(core.avg_head[:], 1.0 / P).then_inc(filled.sem, 1)
            nc.vector.memset(core.zeros[:], 0.0).then_inc(filled.sem, 1)
            dve.wait_ge(filled.sem, 3)
            dve.sem_inc(core.bank_free.sem, U)
            dve.sem_inc(core.pair_free.sem, 2)
    loaded.passed(32)
    filled.passed(3)


def swap_grid(ap):
    return ap.rearrange("p t (r c) -> p t c r", c=GRID_W)


def as_grid(ap):
    return ap.rearrange("p t (c r) -> p t c r", r=ROWS)


def first_mixer(core, a):
    nc = core.nc
    with ExitStack() as ctx:
        sb = lambda name, shape, dt=F32: core.sb(ctx, name, shape, dt)
        v_a = sb("v_a", [P, 4, 512])
        v_b = sb("v_b", [P, 4, 512])
        lat = sb("lat", [P, 12, N])
        k_f = sb("k_f", [P, 2, 6, N])
        k_b = sb("k_b", [P, 2, 6, N])
        q = sb("q", [P, 6, N])
        z = sb("z", [P, 2, 12, N])
        with ExitStack() as c2:
            x = core.sb(c2, "x", [P, C, L])
            s2 = core.sb(c2, "s2", [P, C, L])
            mixer_inputs(core, a, x, s2, z, v_a, v_b, lat, k_f, k_b, q)
        la = sb("la", [P, 2, 12, N])
        with ExitStack() as c3:
            zt = core.sb(c3, "zt", [P, 2, 12, N])
            lb = core.sb(c3, "lb_cols", [P, 48])
            gates(core, z, la, k_f, k_b, zt, lb)
        b = z
        o = core.x1
        st = sb("state", [P, 2, 2, 6, P])
        running_sums(core, la, b)
        with ExitStack() as c4:
            states(core, c4, a, k_f, k_b, b, v_a, v_b, st, la)
        with ExitStack() as c5:
            scores = core.sb(c5, "scores", [P, 16, P])
            chunk_scores(core, c5, a, q, k_f, k_b, b, scores, la)
            mixer_outputs(core, q, b, st, v_a, v_b, scores, o, la)
        mix = core.x1
        with ExitStack() as c6:
            head_norms(core, c6, o, lat, mix)
    with ExitStack() as ctx:
        xl, pre, xc = (core.sb(ctx, name, [P, C, N]) for name in ("xl", "pre", "xc1"))
        tmp = core.sb(ctx, "tmp", [P, U, N])
        add_residual(core, a, "w_out", mix, xl, pre, tmp, lambda t: core.mod[:, bass.ds(t + 16, 1), 0],
                     lambda u: a["w_query"][u], load_x=a["x"][:, :, NC:L], alpha=ALPHA)
        norm(core, pre, N, core.x1, True, [(0, N, core.vcols("ln_gamma0"), core.vcols("ln_beta0"))], xc, pre)


def add_residual(core, a, w, moving, x, out, tmp, gate, next_tiles, load_x=None, alpha=None):
    nc = core.nc
    own = core.count("residual_gated")
    base = own.base
    if load_x is not None:
        loaded = core.count("residual_loaded")
        with nc.Block() as block:

            @block.sync
            def _(sp):
                sp.dma_start(x[:], load_x).then_inc(loaded.sem, 16)
                sp.wait_ge(loaded.sem, loaded.at(16))
        loaded.passed(16)

    def evacuate(dve, t, u):
        nc.vector.tensor_scalar(tmp[:, u, :], core.bank[u][:, 0:N], gate(t), None, ALU.mult).then_inc(own.sem, 1)
        dve.wait_ge(own.sem, base + t + 1)
        return nc.vector.scalar_tensor_tensor(out[:, bass.ds(t, 1), :], x[:, bass.ds(t, 1), :],
                                              1.0 if alpha is None else alpha,
                                              tmp[:, u:u + 1, :], ALU.mult, ALU.add)

    with ExitStack() as ctx:
        project_split(core, Halver(core, ctx, w), lambda t: a[w][t], C, Split(core, ctx, w, moving, N), 0, N, evacuate, next_tiles)
    own.passed(C)


def mixer_inputs(core, a, x, s2, z, v_a, v_b, lat, k_f, k_b, q):
    nc = core.nc
    with ExitStack() as ctx:
        sb = lambda name, shape, dt=F32: core.sb(ctx, name, shape, dt)
        rank_w = sb("rank_w", [P, C, 32])
        gk2 = sb("gk2", [16, 2, 256])
        rank = sb("rank", [16, 2, L])
        loaded = core.count("mixer_loaded")
        with nc.Block() as block:

            @block.sync
            def _(sp):
                sp.dma_start(x[:], a["x"]).then_inc(loaded.sem, 16)
                sp.dma_start(rank_w[:], a["w_rank"]).then_inc(loaded.sem, 16)
                sp.dma_start(gk2[:], a["w_gk2"]).then_inc(loaded.sem, 16)
                sp.wait_ge(loaded.sem, loaded.at(48))

        loaded.passed(48)
        gain = [core.mod[:, 8:16, j] for j in range(2)]
        shift = [core.mod[:, 0:8, j] for j in range(2)]
        norm(core, x, L, x, True, [(0, NC, gain[1], shift[1]), (NC, L, gain[0], shift[0])], x, s2)
        h = x
        parts = ctx.enter_context(ExitStack())
        split = Split(core, parts, "mixer_h", h, L)
        halver = Halver(core, parts, "mixer")

        def to_z(dve, t, u):
            return nc.vector.tensor_copy(s2[:, bass.ds(t, 1), :], core.bank[u][:, :].rearrange("p (o n) -> p o n", o=1))

        zz = s2
        project_split(core, halver, lambda t: a["w_in"][t], 8, split, 0, L, to_z, lambda u: a["w_in"][8 + u])
        own = core.count("inputs_spread")
        with nc.Block() as block:

            @block.vector
            def _(dve):
                for d in range(2):
                    for s in range(2):
                        nc.vector.tensor_copy(z[:, s, 6 * d:6 * d + 4, :], zz[:, 4 * d:4 * d + 4, s * NC:s * NC + N])\
                            .then_inc(own.sem, 1)
        own.passed(4)

        def to_kq(dve, t, u):
            return nc.vector.tensor_copy(s2[:, bass.ds(t, 1), :], core.bank[u][:, :].rearrange("p (o n) -> p o n", o=1))

        project_split(core, halver, lambda t: a["w_in"][t + 8], 4, split, 0, L, to_kq, lambda u: a["w_in"][12 + u])
        with nc.Block() as block:

            @block.vector
            def _(dve):
                for k in (k_f, k_b):
                    nc.vector.tensor_copy(k[:, 0, 4:6, :], s2[:, 0:2, 0:NC]).then_inc(own.sem, 1)
                    for j in range(2):
                        nc.vector.tensor_copy(as_grid(k[:, 1, 4 + j:5 + j, :]), swap_grid(s2[:, j:j + 1, NC:L])).then_inc(own.sem, 1)
                for j in range(2):
                    nc.vector.tensor_scalar(as_grid(q[:, 4 + j:5 + j, :]), swap_grid(s2[:, 2 + j:3 + j, NC:L]), 0.125, None, ALU.mult)\
                        .then_inc(own.sem, 1)
        own.passed(8)

        def to_lat(dve, t, u):
            return nc.vector.tensor_copy(lat[:, bass.ds(t, 1), :], core.bank[u][:, 0:N].rearrange("p (o n) -> p o n", o=1))

        project_split(core, halver, lambda t: a["w_in"][t + 12], 12, split, NC, N, to_lat, lambda u: a["w_in"][24 + u])

        parts.close()

        def token_products(src):
            def products(pe, t, u):
                for tt in range(4):
                    for c in range(C):
                        last = nc.tensor.matmul(core.bank[u][:, tt * P:tt * P + P], src[:, c, tt * P:tt * P + P],
                                                core.slot[u][:, c, :], start=(c == 0), stop=(c == C - 1))
                return last
            return products

        def to_values(v):
            def evacuate(dve, t, u):
                return nc.vector.tensor_copy(v[:, :, bass.ds(t * P, P)], core.bank[u][:, :].rearrange("p (t n) -> p t n", t=4))
            return evacuate

        project(core, lambda t: a["w_in"][t + 24], 4, token_products(h), to_values(v_a), lambda u: a["w_in"][28 + u])

        rank_ready, spread = core.count("rank_ready"), core.count("rank_spread")
        gated = core.count("gate_inputs")
        with nc.Block() as block:

            @block.tensor
            def _(pe):
                for d in range(2):
                    for c in range(C):
                        last = nc.tensor.matmul(core.bank[4 + d][0:16, :], rank_w[:, c, 16 * d:16 * d + 16], h[:, c, :],
                                                start=(c == 0), stop=(c == C - 1))
                    last.then_inc(rank_ready.sem, 1)
                pe.wait_ge(spread.sem, spread.at(4))
                for d in range(2):
                    for j in range(2):
                        nc.tensor.matmul(core.bank[4 + 2 * d + j][:, :], gk2[:, d, j * P:j * P + P], rank[:, d, :],
                                         start=True, stop=True).then_inc(gated.sem, 1)

            @block.vector
            def _(dve):
                for d in range(2):
                    dve.wait_ge(rank_ready.sem, rank_ready.at(d + 1))
                    nc.vector.tensor_copy(rank[:, d, 0:NC], core.bank[4 + d][0:16, 0:NC]).then_inc(spread.sem, 1)
                    nc.vector.tensor_copy(as_grid(rank[:, d:d + 1, NC:L]),
                                          swap_grid(core.bank[4 + d][0:16, NC:L].rearrange("p (o n) -> p o n", o=1)))\
                        .then_inc(spread.sem, 1)
                for d in range(2):
                    for j in range(2):
                        dve.wait_ge(gated.sem, gated.at(2 * d + j + 1))
                        for s in range(2):
                            nc.vector.tensor_scalar(z[:, s, 6 * d + 4 + j, :], core.bank[4 + 2 * d + j][:, s * NC:s * NC + N],
                                                    core.col("b_gk", 2 * d + j), None, ALU.add).then_inc(own.sem, 1)
                nc.vector.tensor_copy(s2[:, :, 0:NC], h[:, :, 0:NC]).then_inc(own.sem, 1)
                for c in range(C):
                    nc.vector.tensor_copy(as_grid(s2[:, c:c + 1, NC:L]), swap_grid(h[:, c:c + 1, NC:L])).then_inc(own.sem, 1)

            @block.scalar
            def _(act):
                nc.scalar.activation(q[:, 0:4, :], lat[:, 0:4, :], ACT.Copy).then_inc(core.count("queries_copied").sem, 1)
        core.count("queries_copied").passed(1)
        rank_ready.passed(2)
        spread.passed(4)
        gated.passed(4)
        own.passed(17)
        project(core, lambda t: a["w_in"][t + 28], 4, token_products(s2), to_values(v_b), lambda u: a["w_out"][u])


def running_sums(core, la, b):
    nc = core.nc
    with ExitStack() as ctx:
        keep = core.sb(ctx, "keep", [P, 6 * N])
        filled, summed = core.count("keep_filled"), core.count("sums_ready")
        with nc.Block() as block:

            @block.vector
            def _(dve):
                nc.vector.memset(keep[:], 1.0).then_inc(filled.sem, 1)
                dve.wait_ge(filled.sem, filled.at(1))
                nc.vector.memset(keep[:].rearrange("p (k n) -> p k n", n=CH)[:, :, 0:1], 0.0).then_inc(filled.sem, 1)
                dve.wait_ge(filled.sem, filled.at(2))
                for s in range(2):
                    src = la[:, s, 0:6, :].rearrange("p t n -> p (t n)")
                    dst = b[:, s, 0:6, :].rearrange("p t n -> p (t n)")
                    nc.vector.tensor_tensor_scan(dst, keep[:], src, 0.0, ALU.mult, ALU.add).then_inc(summed.sem, 1)
                    src = la[:, s, 6:12, :].rearrange("p t n -> p (t n)")
                    dst = b[:, s, 6:12, :].rearrange("p t n -> p (t n)")
                    nc.vector.tensor_tensor_scan(dst[:, ::-1], keep[:], src[:, ::-1], 0.0, ALU.mult, ALU.add).then_inc(summed.sem, 1)
        filled.passed(2)
        summed.passed(4)


def states(core, ctx, a, k_f, k_b, b, v_a, v_b, st, kd):
    nc = core.nc
    sb = lambda name, shape, dt=F32: core.sb(ctx, name, shape, dt)
    kt = sb("kt", [P, 2, 3, 6, P])
    end = sb("end", [P, 2, 2, 6, 2])
    work = sb("state_work", [P, 2, 6, P])
    gaps, decays, keyed = core.count("gaps_ready"), core.count("end_decays_ready"), core.count("decayed_keys")
    turned, kt_ready, grown = core.count("keys_turned"), core.count("turned_keys_ready"), core.count("growth_ready")
    stepped = core.count("states_stepped")
    keys = (k_f, k_b)
    met = (((0, 0), (0, 1), (1, 0)), ((0, 1), (0, 0), (1, 1)))

    def by_chunk(t, s, d):
        return t[:, s, 6 * d:6 * d + 6, :].rearrange("p t (c n) -> p (t c) n", n=CH)

    with nc.Block() as block:

        @block.vector
        def _(dve):
            for d in range(2):
                e = CH - 1 if d == 0 else 0
                for s in range(2):
                    last = by_chunk(b, s, d)[:, :, e:e + 1]
                    nc.vector.tensor_copy(end[:, s, d, :, :].rearrange("p t c -> p (t c)"), last).then_inc(gaps.sem, 1)
                    nc.vector.tensor_tensor(by_chunk(kd, s, d), last.broadcast_to([P, 12, CH]), by_chunk(b, s, d), ALU.subtract)\
                        .then_inc(gaps.sem, 1)
            for d in range(2):
                for s in range(2):
                    dve.wait_ge(decays.sem, decays.at(2 * d + s + 1))
                    nc.vector.tensor_tensor(kd[:, s, 6 * d:6 * d + 6, :], kd[:, s, 6 * d:6 * d + 6, :], keys[d][:, s, :, :], ALU.mult)\
                        .then_inc(keyed.sem, 1)
            n = 0
            for i in range(3):
                for d in range(2):
                    for half in range(2):
                        n += 1
                        dve.wait_ge(turned.sem, turned.at(n))
                        nc.vector.tensor_copy(kt[:, d, i, 3 * half:3 * half + 3, :],
                                              core.bank[(n - 1) % 4][:, 0:3 * P].rearrange("p (t n) -> p t n", n=P))\
                            .then_inc(kt_ready.sem, 1)
            k = 0
            for i in range(3):
                for d in range(2):
                    dve.wait_ge(grown.sem, grown.at(2 * i + d + 1))
                    if i > 0:
                        dve.wait_ge(stepped.sem, stepped.at(k))
                    s, c = met[d][i]
                    x, y = core.bank[4 + 2 * d], core.bank[5 + 2 * d]
                    before = work[:, d] if i == 1 else st[:, d, 0]
                    after = work[:, d] if i == 0 else st[:, d, i - 1]
                    parts = [(slice(0, P), t, x[:, t * P:t * P + P]) for t in range(4)]
                    parts += [(slice(64 * r, 64 * r + 64), 4 + j, y[64 * r:64 * r + 64, 256 * j + 128 * r:256 * j + 128 * r + 128])
                              for j in range(2) for r in range(2)]
                    for rows, t, new in parts:
                        if i == 0:
                            ins = nc.vector.tensor_copy(after[rows, t, :], new)
                        else:
                            ins = nc.vector.scalar_tensor_tensor(after[rows, t, :], before[rows, t, :], end[rows, s, d, t, c:c + 1],
                                                                 new, ALU.mult, ALU.add)
                        ins.then_inc(stepped.sem, 1)
                        k += 1

        @block.scalar
        def _(act):
            for d in range(2):
                for s in range(2):
                    act.wait_ge(gaps.sem, gaps.at(4 * d + 2 * s + 2))
                    nc.scalar.activation(end[:, s, d, :, :], end[:, s, d, :, :], ACT.Exp)
                    nc.scalar.activation(kd[:, s, 6 * d:6 * d + 6, :], kd[:, s, 6 * d:6 * d + 6, :], ACT.Exp).then_inc(decays.sem, 1)

        @block.tensor
        def _(pe):
            pe.wait_ge(keyed.sem, keyed.at(4))
            n = 0
            for i in range(3):
                for d in range(2):
                    s, c = met[d][i]
                    for half in range(2):
                        if n >= 4:
                            pe.wait_ge(kt_ready.sem, kt_ready.at(n - 3))
                        for j in range(3):
                            t = 3 * half + j
                            last = nc.tensor.transpose(core.bank[n % 4][:, j * P:j * P + P],
                                                       kd[:, s, 6 * d + t, c * CH:c * CH + CH], core.ident)
                        last.then_inc(turned.sem, 1)
                        n += 1
            for i in range(3):
                for d in range(2):
                    s, c = met[d][i]
                    tt = 2 * s + c
                    pe.wait_ge(kt_ready.sem, kt_ready.at(4 * i + 2 * d + 2))
                    if i > 0:
                        pe.wait_ge(stepped.sem, stepped.at(8 * (2 * (i - 1) + d + 1)))
                    for t in range(4):
                        nc.tensor.matmul(core.bank[4 + 2 * d][:, t * P:t * P + P], kt[:, d, i, t, :], v_a[:, tt, t * P:t * P + P],
                                         start=True, stop=True)
                    for j in range(2):
                        last = nc.tensor.matmul(core.bank[5 + 2 * d][:, 256 * j:256 * j + 256], kt[:, d, i, 4 + j, :],
                                                v_b[:, tt, 256 * j:256 * j + 256], start=True, stop=True)
                    last.then_inc(grown.sem, 1)
    for s, k in ((gaps, 8), (decays, 4), (keyed, 4), (turned, 12), (kt_ready, 12), (grown, 6), (stepped, 48)):
        s.passed(k)


def chunk_scores(core, ctx, a, q, k_f, k_b, b, scores, la):
    nc = core.nc
    sb = lambda name, shape, dt=F32: core.sb(ctx, name, shape, dt)
    mask = sb("mask", [P, LEVELS + 1, P], I32)
    df, db = (la[:, s].rearrange("p (w t) n -> p w (t n)", w=2) for s in range(2))
    ql = sb("ql", [P, 2, 6, N])
    kl = sb("kl", [P, 2, 6, N])
    loaded = core.count("mask_loaded")
    gaps, gaps_b = core.count("level_gaps_forward"), core.count("level_gaps_backward")
    factors, sided = core.count("level_factors"), core.count("level_sided")
    made, kept = core.count("level_products"), core.count("level_kept")
    bf = b[:, 1, 0:6, :].rearrange("p t n -> p (t n)")
    bb = b[:, 1, 6:12, :].rearrange("p t n -> p (t n)")
    qf = q[:].rearrange("p t n -> p (t n)")
    kf = k_f[:, 1].rearrange("p t n -> p (t n)")
    kb = k_b[:, 1].rearrange("p t n -> p (t n)")
    flat = lambda t, w: t[:, w].rearrange("p t n -> p (t n)")

    def halves(ap, h):
        return ap.rearrange("p (n two h) -> p n two h", two=2, h=h)

    with nc.Block() as block:

        @block.sync
        def _(sp):
            sp.dma_start(mask[:], a["mask"].rearrange("l p n -> p l n")).then_inc(loaded.sem, 16)
            sp.wait_ge(loaded.sem, loaded.at(16))

        def keep(dve, l):
            if l == 0:
                dve.wait_ge(loaded.sem, loaded.at(16))
            else:
                dve.wait_ge(kept.sem, kept.at(4 * l))
            dve.wait_ge(made.sem, made.at(l + 1))
            for g in range(4):
                nc.vector.copy_predicated(scores[:, 4 * g:4 * g + 4, :],
                                          mask[:, l:l + 1, :].broadcast_to([P, 4, P]),
                                          core.bank[4 * (l % 2) + g][:, :].rearrange("p (g n) -> p g n", n=P))\
                    .then_inc(kept.sem, 1)

        def blocks(ap, h):
            return ap.rearrange("p (n m) -> p n m", m=2 * h)

        @block.gpsimd
        def _(pool):
            for l in range(LEVELS):
                h = 1 << l
                if l >= 2:
                    pool.wait_ge(sided.sem, sided.at(4 * (l - 1)))
                mid = blocks(bb, h)[:, :, h:h + 1].broadcast_to([P, 6 * N // (2 * h), 2 * h])
                nc.gpsimd.tensor_tensor(blocks(db[:, l % 2], h), blocks(bb, h), mid, ALU.subtract).then_inc(gaps_b.sem, 1)

        @block.vector
        def _(dve):
            def gap(l):
                h = 1 << l
                mid = blocks(bf, h)[:, :, h - 1:h].broadcast_to([P, 6 * N // (2 * h), 2 * h])
                nc.vector.tensor_tensor(blocks(df[:, l % 2], h), blocks(bf, h), mid, ALU.subtract).then_inc(gaps.sem, 1)

            gap(0)
            for l in range(LEVELS + 1):
                w = l % 2
                if l + 1 < LEVELS:
                    if l >= 1:
                        dve.wait_ge(sided.sem, sided.at(4 * l))
                    gap(l + 1)
                if l >= 2:
                    dve.wait_ge(made.sem, made.at(l - 1))
                if l < LEVELS:
                    h = 1 << l
                    dve.wait_ge(factors.sem, factors.at(4 * l + 4))
                    for out, x, f, side in ((ql, qf, df, 1), (ql, qf, db, 0), (kl, kf, df, 0), (kl, kb, db, 1)):
                        nc.vector.tensor_tensor(halves(flat(out, w), h)[:, :, side, :], halves(x, h)[:, :, side, :],
                                                halves(f[:, w], h)[:, :, side, :], ALU.mult).then_inc(sided.sem, 1)
                else:
                    nc.vector.tensor_copy(flat(ql, w), qf).then_inc(sided.sem, 1)
                    nc.vector.tensor_tensor(flat(kl, w), kf, kb, ALU.add).then_inc(sided.sem, 1)
                if l >= 1:
                    keep(dve, l - 1)
            keep(dve, LEVELS)

        @block.scalar
        def _(act):
            for l in range(LEVELS):
                h, w = 1 << l, l % 2
                for k, (f, side, sign) in enumerate(((df, 1, 1.0), (df, 0, -1.0), (db, 0, 1.0), (db, 1, -1.0))):
                    if k % 2 == 0:
                        ready = gaps_b if k else gaps
                        act.wait_ge(ready.sem, ready.at(l + 1))
                    v = halves(f[:, w], h)[:, :, side, :]
                    nc.scalar.activation(v, v, ACT.Exp, scale=sign).then_inc(factors.sem, 1)

        @block.tensor
        def _(pe):
            for l in range(LEVELS + 1):
                w = l % 2
                pe.wait_ge(sided.sem, sided.at(4 * l + (4 if l < LEVELS else 2)))
                if l >= 2:
                    pe.wait_ge(kept.sem, kept.at(4 * (l - 1)))
                for place, head in enumerate(PLACED):
                    rows = slice(0, P) if head < 4 else slice(64 * (head % 2), 64 * (head % 2) + 64)
                    t = head if head < 4 else 4 + (head - 4) // 2
                    for c in range(2):
                        j = 2 * place + c
                        last = nc.tensor.matmul(core.bank[4 * w + j // 4][:, (j % 4) * P:(j % 4) * P + P],
                                                kl[rows, w, t, c * CH:c * CH + CH], ql[rows, w, t, c * CH:c * CH + CH],
                                                start=True, stop=True)
                last.then_inc(made.sem, 1)
    loaded.passed(16)
    for s, k in ((gaps, LEVELS), (gaps_b, LEVELS), (factors, 4 * LEVELS), (sided, 4 * LEVELS + 2), (made, LEVELS + 1), (kept, 4 * (LEVELS + 1))):
        s.passed(k)


def mixer_outputs(core, q, b, st, v_a, v_b, scores, o, la):
    nc = core.nc
    qd = la[:, 0].rearrange("p (d t) n -> p d t n", d=2)
    decay, ready, made, out = core.count("query_decay"), core.count("queries_decayed"), core.count("outputs_made"), core.count("outputs_copied")
    with nc.Block() as block:

        @block.scalar
        def _(act):
            for d in range(2):
                nc.scalar.activation(qd[:, d], b[:, 1, 6 * d:6 * d + 6, :], ACT.Exp).then_inc(decay.sem, 1)

        @block.vector
        def _(dve):
            for d in range(2):
                dve.wait_ge(decay.sem, decay.at(d + 1))
                nc.vector.tensor_tensor(qd[:, d], qd[:, d], q[:], ALU.mult).then_inc(ready.sem, 1)
            for g in range(4):
                dve.wait_ge(made.sem, made.at(g + 1))
                src = core.bank[g][:, :].rearrange("p (h n) -> p h n", n=N)
                if g < 2:
                    nc.vector.tensor_copy(o[:, 2 * g:2 * g + 2, :], src).then_inc(out.sem, 1)
                else:
                    for r in range(2):
                        head = PLACED[2 * g + r]
                        nc.vector.tensor_copy(swap_grid(o[:, head:head + 1, :]), as_grid(src[:, r:r + 1, :])).then_inc(out.sem, 1)

        @block.tensor
        def _(pe):
            pe.wait_ge(ready.sem, ready.at(2))
            for place, head in enumerate(PLACED):
                rows = slice(0, P) if head < 4 else slice(64 * (head % 2), 64 * (head % 2) + 64)
                t = head if head < 4 else 4 + (head - 4) // 2
                v = v_a if head < 4 else v_b
                for c in range(2):
                    dst = core.bank[place // 2][:, (place % 2) * N + c * CH:(place % 2) * N + c * CH + CH]
                    nc.tensor.matmul(dst, v[:, 2 + c, (head % 4) * P:(head % 4) * P + P], scores[:, 2 * place + c, :], start=True, stop=False)
                    for d in range(2):
                        step = c if d == 0 else 1 - c
                        last = nc.tensor.matmul(dst, st[rows, d, step, t, :], qd[rows, d, t, c * CH:c * CH + CH],
                                                start=False, stop=(d == 1))
                if place % 2:
                    last.then_inc(made.sem, 1)
    decay.passed(2)
    ready.passed(2)
    made.passed(4)
    out.passed(6)


def head_norms(core, ctx, o, lat, mix):
    nc = core.nc
    sq = core.sb(ctx, "head_sq", [P, 8, N])
    sg = core.sb(ctx, "head_gate", [P, 8, N])
    squared, meant, rooted, own, gated = (core.count(x) for x in ("head_squared", "head_mean", "head_root", "head_vector_steps", "head_gates"))
    with nc.Block() as block:

        @block.scalar
        def _(act):
            nc.scalar.activation(sg[:], lat[:, 4:12, :], ACT.Silu).then_inc(gated.sem, 1)
            for g in range(4):
                nc.scalar.activation(sq[:, 2 * g:2 * g + 2, :], o[:, 2 * g:2 * g + 2, :], ACT.Square).then_inc(squared.sem, 1)
            for g in range(4):
                act.wait_ge(meant.sem, meant.at(g + 1))
                nc.scalar.activation(sq[:, 2 * g:2 * g + 2, :], core.bank[g][:, :].rearrange("p (h n) -> p h n", n=N), ACT.Sqrt,
                                     bias=core.col("eps", 0)).then_inc(rooted.sem, 1)

        @block.tensor
        def _(pe):
            for g in range(4):
                pe.wait_ge(squared.sem, squared.at(g + 1))
                nc.tensor.matmul(core.bank[g][:, :], core.avg_head[:], sq[:, 2 * g:2 * g + 2, :].rearrange("p h n -> p (h n)"),
                                 start=True, stop=True).then_inc(meant.sem, 1)

        @block.vector
        def _(dve):
            steps = Steps(dve, own)
            dve.wait_ge(gated.sem, gated.at(1))
            for g in range(4):
                two = slice(2 * g, 2 * g + 2)
                dve.wait_ge(rooted.sem, rooted.at(g + 1))
                steps.then(nc.vector.reciprocal(sq[:, two, :], sq[:, two, :]))
                steps.then(nc.vector.scalar_tensor_tensor(sq[:, two, :], o[:, two, :], core.col("hg_norm" if g < 2 else "gla_norm", 0),
                                                          sq[:, two, :], ALU.mult, ALU.mult))
                steps.then(nc.vector.tensor_tensor(mix[:, two, :], sq[:, two, :], sg[:, two, :], ALU.mult))
    for s, k in ((squared, 4), (meant, 4), (rooted, 4), (own, 12), (gated, 1)):
        s.passed(k)


def retrieval(core, a):
    nc = core.nc
    with ExitStack() as ctx:
        sb = lambda name, shape, dt=F32: core.sb(ctx, name, shape, dt)
        with ExitStack() as cg:
            side = core.sb(cg, "picked_or_ada", [P, D])
            picked = side[:, 0:3 * N].rearrange("p (j n) -> p j n", j=3)
            split = Split(core, cg, "h", None, N)
            with ExitStack() as c1:
                h = split.source = core.sb(c1, "h_whole", [P, C, N])
                xc = core.sb(c1, "xc2", [P, C, N])
                sq = core.sb(c1, "sq2", [P, C, N])
                norm(core, core.x1, N, h, True, [(0, N, core.mod[:, 32:40, 0], core.mod[:, 24:32, 0])], xc, sq)
                qt = core.sb(c1, "qt", [P, 16, N])

                def to_q(dve, t, u):
                    return nc.vector.tensor_copy(qt[:, bass.ds(t, 1), :], core.bank[u][:, 0:N].rearrange("p (o n) -> p o n", o=1))

                def first(u):
                    return [a["peer_u"][0], a["peer_u"][1], a["peer_v"][0], a["peer_u"][2]][u]

                with ExitStack() as c2:
                    project_split(core, Halver(core, c2, "w_query"), lambda t: a["w_query"][t], 16, split, 0, N, to_q, first)
                for tt in range(2):
                    choose(core, a, qt, tt, picked)
            weights = core.sb(cg, "weights", [P, N, P])
            with ExitStack() as c2:
                spread_weights(core, c2, picked, weights)
            experts(core, cg, a, weights, split, side)
        pre = sb("pre2", [P, C, N])
        y = sb("y", [P, C, N])
        xc = sb("xc3", [P, C, N])
        own = core.count("retrieved")
        with nc.Block() as block:

            @block.vector
            def _(dve):
                for c in range(C):
                    nc.vector.tensor_scalar(y[:, c, :], core.bank[4 + c // 2][:, (c % 2) * N:(c % 2) * N + N], core.mod[:, 40 + c, 0:1], None, ALU.mult)\
                        .then_inc(own.sem, 1)
                dve.wait_ge(own.sem, own.at(C))
                nc.vector.scalar_tensor_tensor(pre[:], core.x1[:], ALPHA, y[:], ALU.mult, ALU.add).then_inc(own.sem, 1)
        own.passed(C + 1)
        norm(core, pre, N, core.x1, True, [(0, N, core.vcols("ln_gamma1"), core.vcols("ln_beta1"))], xc, y)


def choose(core, a, qt, tt, picked):
    nc = core.nc
    with ExitStack() as ctx:
        sb = lambda name, shape, dt=F32: core.sb(ctx, f"{name}_{tt}", shape, dt)
        keys = sb("keys", [P, 2, P])
        s = sb("s", [P, 16, P])
        s2 = sb("s_rest", [P, 16, P])
        v = sb("v", [P, HEADS, 2, TOPK])
        vi = sb("vi", [P, HEADS, 2, TOPK], U32)
        vif = sb("vif", [P, HEADS, 2, TOPK])
        cand = sb("cand", [P, HEADS, TOPK, TOPK])
        cand2 = sb("cand_rest", [P, HEADS, TOPK, TOPK])
        top = sb("top", [P, HEADS, TOPK])
        pos = sb("pos", [P, HEADS, TOPK], U32)
        ab = sb("ab", [P, 2, HEADS, TOPK], U32)
        abf = sb("abf", [P, 2, HEADS * TOPK])
        hit = sb("hit", [P, HEADS * TOPK, TOPK])
        out = sb("out", [P, 3, HEADS, TOPK])
        tot = sb("tot", [P, HEADS])
        loaded, scored, own, expd, ready, turned, kept = (
            core.count(x) for x in ("keys_loaded", "keys_scored", "choose_vector_steps", "choice_exp", "choice_ready",
                                    "choice_turned", "choice_kept"))
        with nc.Block() as block:

            @block.sync
            def _(sp):
                sp.dma_start(keys[:], a["keys"]).then_inc(loaded.sem, 16)
                sp.wait_ge(loaded.sem, loaded.at(16))

            @block.tensor
            def _(pe):
                pe.wait_ge(loaded.sem, loaded.at(16))
                for g in range(4):
                    for j in range(4):
                        t = 4 * g + j
                        last = nc.tensor.matmul(core.bank[4 + g][:, j * P:j * P + P], qt[:, t, tt * P:tt * P + P], keys[:, t % 2, :],
                                                start=True, stop=True)
                    last.then_inc(scored.sem, 1)
                pe.wait_ge(ready.sem, ready.at(2))
                for j in range(3):
                    last = nc.tensor.transpose(core.bank[4][:, j * P:j * P + P], out[:, j, :, :].rearrange("p h k -> p (h k)"), core.ident)
                last.then_inc(turned.sem, 1)

            @block.vector
            def _(dve):
                steps = Steps(dve, own)
                for g in range(4):
                    dve.wait_ge(scored.sem, scored.at(g + 1))
                    ins = nc.vector.tensor_copy(s[:, 4 * g:4 * g + 4, :], core.bank[4 + g][:, :].rearrange("p (j n) -> p j n", n=P))
                steps.then(ins)

                def best(vals, rest, n, outs, idxs):
                    for j in range(n):
                        ins = nc.vector.max(outs(j)[:, 0:8], vals(j))
                    steps.then(ins)
                    for j in range(n):
                        nc.vector.max_index(idxs(j)[:, 0:8], outs(j)[:, 0:8], vals(j))
                        ins = nc.vector.match_replace(rest(j), outs(j)[:, 0:8], vals(j), NEG)
                    steps.then(ins)
                    for j in range(n):
                        ins = nc.vector.max(outs(j)[:, 8:16], rest(j))
                    steps.then(ins)
                    for j in range(n):
                        ins = nc.vector.max_index(idxs(j)[:, 8:16], outs(j)[:, 8:16], rest(j))
                    steps.then(ins)

                best(lambda j: s[:, j, :], lambda j: s2[:, j, :], 16, lambda j: v[:, j // 2, j % 2, :], lambda j: vi[:, j // 2, j % 2, :])
                nc.vector.tensor_copy(vif[:], vi[:])
                steps.then(nc.vector.tensor_tensor(cand[:], v[:, :, 0, :].rearrange("p h (k o) -> p h k o", o=1).broadcast_to([P, HEADS, TOPK, TOPK]),
                                                   v[:, :, 1:2, :].broadcast_to([P, HEADS, TOPK, TOPK]), ALU.add))
                flat = lambda t: (lambda j: t[:, j].rearrange("p a b -> p (a b)"))
                best(flat(cand), flat(cand2), HEADS, lambda j: top[:, j, :], lambda j: pos[:, j, :])
                nc.vector.tensor_scalar(ab[:, 0], pos[:], 4, None, ALU.logical_shift_right)
                nc.vector.tensor_scalar(ab[:, 1], pos[:], 15, None, ALU.bitwise_and)
                nc.vector.tensor_tensor(out[:, 2], top[:], top[:, :, 0:1].broadcast_to([P, HEADS, TOPK]), ALU.subtract).then_inc(ready.sem, 1)
                steps.then(nc.vector.tensor_copy(tot[:], top[:, :, 0]))
                steps.then(nc.vector.tensor_copy(abf[:], ab[:].rearrange("p w h k -> p w (h k)")))
                for w in range(2):
                    steps.then(nc.vector.tensor_tensor(hit[:], abf[:, w, :].rearrange("p (m o) -> p m o", o=1).broadcast_to([P, HEADS * TOPK, TOPK]),
                                                       core.iota[:, 0:TOPK].rearrange("p (o n) -> p o n", o=1).broadcast_to([P, HEADS * TOPK, TOPK]),
                                                       ALU.is_equal))
                    h4 = hit[:].rearrange("p (h k) n -> p h k n", k=TOPK)
                    steps.then(nc.vector.tensor_tensor(h4, h4, vif[:, :, w:w + 1, :].broadcast_to([P, HEADS, TOPK, TOPK]), ALU.mult))
                    steps.then(nc.vector.tensor_reduce(out[:, w].rearrange("p h k -> p (h k)"), hit[:], AX.X, ALU.add))
                dve.wait_ge(expd.sem, expd.at(1))
                steps.then(nc.vector.tensor_reduce(tot[:], out[:, 2], AX.X, ALU.add))
                steps.then(nc.vector.reciprocal(tot[:], tot[:]))
                nc.vector.tensor_tensor(out[:, 2], out[:, 2], tot[:].rearrange("p (h o) -> p h o", o=1).broadcast_to([P, HEADS, TOPK]), ALU.mult)\
                    .then_inc(ready.sem, 1)
                dve.wait_ge(turned.sem, turned.at(1))
                nc.vector.tensor_copy(picked[:, :, tt * P:tt * P + P], core.bank[4][:, 0:3 * P].rearrange("p (j n) -> p j n", n=P))\
                    .then_inc(kept.sem, 1)
                n_own.append(steps.k)

            @block.scalar
            def _(act):
                act.wait_ge(ready.sem, ready.at(1))
                nc.scalar.activation(out[:, 2], out[:, 2], ACT.Exp).then_inc(expd.sem, 1)
        loaded.passed(16)
        scored.passed(4)
        own.passed(n_own.pop())
        expd.passed(1)
        ready.passed(2)
        turned.passed(1)
        kept.passed(1)


n_own = []


def spread_weights(core, ctx, picked, weights):
    nc = core.nc
    B = 4
    W = 4
    one_a = core.sb(ctx, "one_a", [P, W, B, P])
    one_b = core.sb(ctx, "one_b", [P, W, B, P])
    marked, made, kept = core.count("keys_marked"), core.count("weights_made"), core.count("weights_kept")
    away, distance, marked_a = core.count("keys_away"), core.count("keys_distance"), core.count("first_keys_marked")
    rounds = N // (W * B)
    marks = W * B + W // 2
    iota_b = core.iota.rearrange("p (o n) -> p o n", o=1).broadcast_to([P, B, P])

    def first_keys(t0):
        return picked[:, 0:1, bass.ds(t0, B)].rearrange("p o b -> p b o").broadcast_to([P, B, P])

    with nc.Block() as block:

        @block.gpsimd
        def _(pool):
            with pool.Fori(0, rounds) as i:
                for w in range(0, W, 2):
                    pool.wait_ge(made.sem, made.at(w + 1) + i * W)
                    nc.gpsimd.tensor_tensor(one_a[:, w], iota_b, first_keys(i * (W * B) + w * B), ALU.subtract).then_inc(away.sem, 1)

        @block.vector
        def _(dve):
            dve.sem_inc(made.sem, W)
            with dve.Fori(0, rounds) as i:
                for w in range(W):
                    t0 = i * (W * B) + w * B
                    dve.wait_ge(made.sem, made.at(w + 1) + i * W)
                    if w % 2:
                        nc.vector.tensor_tensor(one_a[:, w], iota_b, first_keys(t0), ALU.is_equal).then_inc(marked.sem, 1)
                    for j in range(B):
                        nc.vector.tensor_scalar(one_b[:, w, j, :], core.iota, picked[:, 1, bass.ds(t0 + j, 1)],
                                                picked[:, 2, bass.ds(t0 + j, 1)], ALU.is_equal, ALU.mult).then_inc(marked.sem, 1)

        @block.scalar
        def _(act):
            def mark(i, w):
                k = w // 2 + 1
                act.wait_ge(away.sem, away.at(k) + i * (W // 2))
                nc.scalar.activation(one_a[:, w], one_a[:, w], ACT.Abs).then_inc(distance.sem, 1)
                act.wait_ge(distance.sem, distance.at(k) + i * (W // 2))
                nc.scalar.activation(one_a[:, w], one_a[:, w], ACT.Relu, scale=-1.0, bias=core.col("one", 0)).then_inc(marked_a.sem, 1)

            def keep(i, w):
                act.wait_ge(made.sem, made.at(W + w + 1) + i * W)
                nc.scalar.activation(weights[:, bass.ds(i * (W * B) + w * B, B), :], core.bank[w][:, :].rearrange("p (b n) -> p b n", n=P),
                                     ACT.Copy).then_inc(kept.sem, 1)

            for w in range(0, W, 2):
                mark(0, w)
            with act.Fori(0, rounds - 1) as i:
                for w in range(W):
                    keep(i, w)
                    if w % 2 == 0:
                        mark(i + 1, w)
            for w in range(W):
                keep(rounds - 1, w)

        @block.tensor
        def _(pe):
            pe.sem_inc(kept.sem, W)
            with pe.Fori(0, rounds) as i:
                for w in range(W):
                    if w % 2 == 0:
                        pe.wait_ge(marked_a.sem, marked_a.at(w // 2 + 1) + i * (W // 2))
                    pe.wait_ge(marked.sem, marked.at(B * (w + 1) + (w + 1) // 2) + i * marks)
                    pe.wait_ge(kept.sem, kept.at(w + 1) + i * W)
                    for j in range(B):
                        last = nc.tensor.matmul(core.bank[w][:, j * P:j * P + P], one_b[:, w, j, :], one_a[:, w, j, :], start=True, stop=True)
                    last.then_inc(made.sem, 1)
    for c, k in ((marked, marks * rounds), (made, W * (rounds + 1)), (kept, W * (rounds + 1)), (away, W // 2 * rounds),
                 (distance, W // 2 * rounds), (marked_a, W // 2 * rounds)):
        c.passed(k)


def zero_banks(core, pe, banks):
    for b in banks:
        core.nc.tensor.matmul(core.bank[b][:, :].rearrange("p (o n) -> p o n", o=4), core.zeros[:], core.zeros[:].rearrange("p (o n) -> p o n", o=1).broadcast_to([P, 4, P]), start=True, stop=False, skip_group_check=True)


def experts(core, ctx, a, weights, split, side):
    nc = core.nc
    T = P
    act_g = core.sb(ctx, "act_g", [P, 2, N])
    act_lo = core.sb(ctx, "act_lo", [P, 2, N], F32R)
    act_hi = core.sb(ctx, "act_hi", [P, 2, N], F32R)
    slots = (side, core.sb(ctx, "ada_slot", [P, D]))
    used = core.tiles_used
    geled, weighed, weigh_steps = core.count("expert_gelu"), core.count("expert_weighed"), core.count("weigh_steps")
    halver = Halver(core, ctx, "expert")
    side_landed = [core.count(f"ada_landed_{w}") for w in range(2)]
    summed, column, added = core.count("ada_rows_summed"), core.count("ada_columns_made"), core.count("ada_added")
    pairs = T // 2
    S = DEPTH_2 * 6
    SIDE = S * C
    per = C // 2
    side_rounds = SIDE // 2
    ada = a["ada_w_2"]

    def load_side(sp, w, tile):
        sp.dma_start(slots[w][:], tile).then_inc(side_landed[w].sem, 16)

    with nc.Block() as block:

        @block.sync
        def _(sp):
            def refill(i, last=False, section=None):
                order = (a["peer_v"][i * 2 - 1], a["peer_u"][i * 2 + 1], a["peer_v"][i * 2],
                         a["peer_v"][i * 2 + 1] if last else a["peer_u"][i * 2 + 2])
                for u, tile in enumerate(order):
                    halver.reload(sp, u, i, tile)
                    if section is not None and u == 1:
                        if not isinstance(i, int) or i > 1:
                            sp.wait_ge(summed.sem, summed.at(-2) + i * 2)
                        if section is not True:
                            sp.wait_ge(column.sem, column.at(0) + section)
                        load_side(sp, 1, ada[i * 2 - 1])
                    if section is not None and u == 3 and not (isinstance(i, int) and i == side_rounds):
                        sp.wait_ge(summed.sem, summed.at(-1) + i * 2)
                        load_side(sp, 0, ada[i * 2])

            load_side(sp, 0, ada[0])
            for i in range(1, per + 1):
                refill(i, False, True)
            with sp.Fori(1, S - 1) as g:
                for r in range(1, per + 1):
                    refill(g * per + r, False, g if r == 1 else True)
            for r in range(1, per + 1):
                refill(side_rounds - per + r, False, S - 1 if r == 1 else True)
            with sp.Fori(side_rounds + 1, pairs - 1) as i:
                refill(i)
            refill(pairs - 1, True)
            for u in range(U):
                halver.reload(sp, 2 * T + u, 0, a["w_in_2"][u])

        @block.tensor
        def _(pe):
            def dot(place, i, w):
                halver.products(pe, place, i, lambda c: core.bank[w][:, 0:N], lambda c: split.high[:, c, :], lambda c: split.low[:, c, :], True, True)

            def add(place, i, w, stop=False):
                halver.products(pe, place, i, lambda m: core.bank[4 + m // 2][:, (m % 2) * N:(m % 2) * N + N],
                                lambda m: act_hi[:, w, :], lambda m: act_lo[:, w, :], False, stop)

            def add_rows(g):
                pe.wait_ge(summed.sem, summed.at(C) + g * C)
                for m in range(C):
                    last = nc.tensor.matmul(core.bank[0][:, bass.ds(g * C + N + m, 1)], slots[1][:, m * P:m * P + P], core.col("one", 0),
                                            start=True, stop=True)
                last.then_inc(column.sem, 1)

            def round_(i, before=None):
                for w in range(2):
                    pe.wait_ge(geled.sem, geled.at(w + 1) + i * 2)
                    if before is not None and w == 1:
                        add_rows(before)
                    dot(1 + 2 * w, i, 1 - w)
                    pe.wait_ge(weighed.sem, weighed.at(w + 1) + i * 2)
                    add(2 + 2 * w, i, w)

            zero_banks(core, pe, range(4, 8))
            dot(0, 0, 0)
            with pe.Fori(0, per) as i:
                round_(i)
            with pe.Fori(1, S) as g:
                for r in range(per):
                    round_(g * per + r, g - 1 if r == 0 else None)
            round_(side_rounds, S - 1)
            with pe.Fori(side_rounds + 1, pairs - 1) as i:
                round_(i)
            k = pairs - 1
            pe.wait_ge(geled.sem, geled.at(2 * k + 1))
            dot(4 * k + 1, 0, 1)
            pe.wait_ge(weighed.sem, weighed.at(2 * k + 1))
            add(4 * k + 2, 0, 0)
            pe.wait_ge(weighed.sem, weighed.at(2 * k + 2))
            add(4 * k + 3, 0, 1, stop=True)

        @block.scalar
        def _(act):
            high = lambda place, i: halver.high(act, place, i)

            def gelu(w):
                nc.scalar.activation(act_g[:, w, :], core.bank[w][:, 0:N], ACT.Gelu_apprx_tanh).then_inc(geled.sem, 1)

            halver.credit(act)
            act.sem_inc(geled.sem, 1)
            high(0, 0)
            high(1, 0)
            for w in range(2):
                act.wait_ge(used.sem, used.at(w + 1))
                gelu(w)
                high(2 + 2 * w, 0)
                high(3 + 2 * w, 0)
            with act.Fori(1, pairs - 1) as i:
                for w in range(2):
                    act.wait_ge(used.sem, used.at(2 * w) + i * 4)
                    act.wait_ge(weighed.sem, weighed.at(w - 1) + i * 2)
                    gelu(w)
                    high(2 + 2 * w, i)
                    high(3 + 2 * w, i)
            k = pairs - 1
            for w in range(2):
                act.wait_ge(used.sem, used.at(2 * w + 4 * k))
                act.wait_ge(weighed.sem, weighed.at(w - 1 + 2 * k))
                gelu(w)
                if w == 0:
                    high(4 * k + 2, 0)
                    high(4 * k + 3, 0)

        @block.vector
        def _(dve):
            lower = lambda place, i: halver.lower(dve, place, i)

            def weigh(i, w):
                dve.wait_ge(geled.sem, geled.at(w + 2) + i * 2)
                row = weights[:, :, bass.ds(i * 2 + w, 1)].rearrange("p t o -> p (t o)")
                nc.vector.tensor_tensor(act_hi[:, w, :], act_g[:, w, :], row, ALU.mult).then_inc(weigh_steps.sem, 1)
                nc.vector.tensor_tensor(act_g[:, w, :], act_g[:, w, :], row, ALU.mult).then_inc(weigh_steps.sem, 1)
                dve.wait_ge(weigh_steps.sem, weigh_steps.at(2 * (w + 1)) + i * 4)
                nc.vector.tensor_tensor(act_lo[:, w, :], act_g[:, w, :], act_hi[:, w, :].bitcast(F32), ALU.subtract).then_inc(weighed.sem, 1)

            def add_tile(g, r, w):
                c = 2 * r + w
                dve.wait_ge(side_landed[w].sem, side_landed[w].at(16 * (r + 1)) + g * (16 * per))
                half = lambda t, b: t[:, b * 512:b * 512 + 512]
                if c > 0:
                    dve.wait_ge(summed.sem, summed.at(c) + g * C)
                for b in range(2):
                    row, sums = half(slots[w], b), core.bank[2 + b][:, :]
                    if c == 0:
                        ins = nc.vector.tensor_scalar(sums, row, core.c2s[:, c, :], None, ALU.mult)
                    else:
                        ins = nc.vector.scalar_tensor_tensor(row if c == C - 1 else sums, row, core.c2s[:, c, :], sums, ALU.mult, ALU.add)
                ins.then_inc(summed.sem, 1)

            def round_(i, g=None, r=None):
                for w in range(2):
                    if not isinstance(i, int) or i > 0:
                        dve.wait_ge(used.sem, used.at(2 * w - 1) + i * 4)
                    weigh(i, w)
                    lower(2 + 2 * w, i)
                    lower(3 + 2 * w, i)
                    if g is not None:
                        add_tile(g, r, w)

            lower(0, 0)
            lower(1, 0)
            for r in range(per):
                round_(r, 0, r)
            with dve.Fori(1, S) as g:
                for r in range(per):
                    round_(g * per + r, g, r)
            with dve.Fori(side_rounds, pairs - 1) as i:
                round_(i)
            k = pairs - 1
            for w in range(2):
                dve.wait_ge(used.sem, used.at(2 * w - 1 + 4 * k))
                weigh(k, w)
                if w == 0:
                    lower(4 * k + 2, 0)
                    lower(4 * k + 3, 0)
            dve.wait_ge(column.sem, column.at(S))
            for l in range(DEPTH_2):
                nc.vector.tensor_tensor(core.mod2[:, 48 * l:48 * l + 48, 0], core.bank[0][:, N + 48 * l:N + 48 * l + 48], core.vcols(f"ada_b{l}"), ALU.add)\
                    .then_inc(added.sem, 1)
    used.passed(2 * T)
    for u in range(U):
        core.landed[u].passed(16 * (2 * T // U))
    for w in range(2):
        side_landed[w].passed(16 * side_rounds)
    for s, k in ((geled, T + 1), (weighed, T), (weigh_steps, 2 * T), (summed, SIDE), (column, S), (added, DEPTH_2)):
        s.passed(k)
    halver.passed(2 * T, False)


def second_block(core, a):
    nc = core.nc
    with ExitStack() as ctx:
        sb = lambda name, shape, dt=F32: core.sb(ctx, name, shape, dt)
        cos = sb("cos", [P, N])
        sin = sb("sin", [P, N])
        hide = sb("hide", [P, 2, N])
        lam = sb("lam", [P, DEPTH_2, 1])
        gain = sb("gain", [P, DEPTH_2, 2, C])
        positions(core, a, cos, sin, hide, lam, gain)
        x = core.x1
        for l in range(DEPTH_2):
            m = lambda s, l=l: core.mod2[:, 48 * l + 8 * s:48 * l + 8 * s + 8, 0]
            moe = l % 2 == 1
            with ExitStack() as c1:
                z = core.sb(c1, f"z{l}", [P, 16, N])
                v = core.sb(c1, f"v{l}", [P, 2, 512])
                mix = core.sb(c1, f"mix{l}", [P, C, N])
                sq = core.sb(c1, f"sq_{l}", [P, C, N])
                norm(core, x, N, core.h, False, [(0, N, gain[:, l, 0], m(0))], None, sq)

                def to_z(dve, t, u):
                    return nc.vector.tensor_copy(z[:, bass.ds(t, 1), :], core.bank[u][:, 0:N].rearrange("p (o n) -> p o n", o=1))

                with ExitStack() as c2:
                    name = f"w_in_2_{l}"
                    project_split(core, Halver(core, c2, name), lambda t: a["w_in_2"][t + 20 * l], 16, Split(core, c2, name, core.h, N), 0, N, to_z,
                                  lambda u: a["w_in_2"][20 * l + 16 + u])

                def token_products(pe, t, u):
                    for tt in range(2):
                        for c in range(C):
                            last = nc.tensor.matmul(core.bank[u][:, tt * P:tt * P + P], core.h[:, c, tt * P:tt * P + P],
                                                    core.slot[u][:, c, :], start=(c == 0), stop=(c == C - 1))
                    return last

                def to_v(dve, t, u):
                    return nc.vector.tensor_copy(v[:, :, bass.ds(t * P, P)], core.bank[u][:, 0:N].rearrange("p (t n) -> p t n", t=2))

                project(core, lambda t: a["w_in_2"][t + 20 * l + 16], 4, token_products, to_v, lambda u: a["w_out_2"][8 * l + u])
                with ExitStack() as c2:
                    linear_recurrence(core, c2, a, l, z, mix)
                with ExitStack() as c2:
                    attention(core, c2, a, l, z, v, mix, cos, sin, hide, lam)
                tmp = core.sb(c1, f"tmp{l}", [P, U, N])
                if moe:
                    first = lambda u: a["moe_gu"][u % 2, u // 2]
                else:
                    first = lambda u: a["ffn_gu"][u % 2, u // 2]
                add_residual_2(core, a, l, mix, x, m(2), first)
                norm(core, x, N, core.h, False, [(0, N, gain[:, l, 1], m(3))], None, sq)
            with ExitStack() as c1:
                if moe:
                    routed_feed_forward(core, c1, a, x, m(5))
                else:
                    feed_forward(core, c1, a["ffn_gu"], a["ffn_d"], lambda u: a["w_in_2"][20 + u], x, m(5))
        sq = sb("sq_end", [P, C, N])
        norm(core, x, N, core.h, False, [(0, N, core.vcols("final_g"), None)], None, sq)
        stored = core.count("stored")
        with nc.Block() as block:

            @block.sync
            def _(sp):
                sp.dma_start(a["out"], core.h[:]).then_inc(stored.sem, 16)
                sp.wait_ge(stored.sem, 16)


def add_residual_2(core, a, l, moving, x, gate, next_tiles):
    nc = core.nc

    def evacuate(dve, t, u):
        return nc.vector.scalar_tensor_tensor(x[:, bass.ds(t, 1), :], core.bank[u][:, 0:N].rearrange("p (o n) -> p o n", o=1),
                                              gate[:, bass.ds(t, 1)], x[:, bass.ds(t, 1), :], ALU.mult, ALU.add)

    with ExitStack() as ctx:
        name = f"w_out_2_{l}"
        project_split(core, Halver(core, ctx, name), lambda t: a["w_out_2"][t + 8 * l], C, Split(core, ctx, name, moving, N), 0, N, evacuate, next_tiles)


def positions(core, a, cos, sin, hide, lam, gain):
    nc = core.nc
    with ExitStack() as ctx:
        sb = lambda name, shape, dt=F32: core.sb(ctx, name, shape, dt)
        row = sb("pos_row", [P, N], I32)
        col = sb("pos_col", [P, 2], I32)
        rowc = sb("chunk_row", [P, N], I32)
        colc = sb("chunk_col", [P, 2], I32)
        rowf = sb("pos_f", [P, N])
        rowcf = sb("chunk_row_f", [P, N])
        colcf = sb("chunk_col_f", [P, 2])
        turns = sb("turns", [P, N])
        ang = sb("ang", [P, N])
        lv = sb("lv", [P, DEPTH_2, 4, DH])
        lp = sb("lp", [P, DEPTH_2 * 2, DH])
        ls = sb("ls", [P, DEPTH_2 * 2])
        loaded, own, angle, done = core.count("positions_loaded"), core.count("positions_vector_steps"), core.count("angles_ready"), core.count("sines_ready")
        with nc.Block() as block:

            @block.sync
            def _(sp):
                sp.dma_start(row[:], a["pos"].rearrange("(o n) -> o n", o=1).broadcast_to([P, N])).then_inc(loaded.sem, 16)
                sp.dma_start(col[:], a["pos_cols"]).then_inc(loaded.sem, 16)
                sp.dma_start(lv[:], a["lam_rows"].broadcast_to([P, DEPTH_2, 4, DH])).then_inc(loaded.sem, 16)
                sp.wait_ge(loaded.sem, loaded.at(48))

            @block.vector
            def _(dve):
                steps = Steps(dve, own)
                dve.wait_ge(loaded.sem, loaded.at(48))
                nc.vector.tensor_copy(rowf[:], row[:])
                nc.vector.tensor_scalar(rowc[:], row[:], 6, None, ALU.arith_shift_right)
                steps.then(nc.vector.tensor_scalar(colc[:], col[:], 6, None, ALU.arith_shift_right))
                nc.vector.tensor_copy(rowcf[:], rowc[:])
                nc.vector.tensor_copy(colcf[:], colc[:])
                steps.then(nc.vector.tensor_scalar(ang[:], rowf[:], core.col("inv_freq", 0), None, ALU.mult))
                steps.then(nc.vector.tensor_scalar(turns[:], ang[:], 1.0 / TWO_PI, None, ALU.mult))
                steps.then(nc.vector.tensor_scalar(turns[:], turns[:], ROUND, None, ALU.add))
                steps.then(nc.vector.tensor_scalar(turns[:], turns[:], ROUND, None, ALU.subtract))
                for part in (PI_A, PI_B, PI_C):
                    steps.then(nc.vector.scalar_tensor_tensor(ang[:], turns[:], -part, ang[:], ALU.mult, ALU.add))
                nc.vector.tensor_scalar(ang[:], ang[:], -3.1415925, 3.1415925, ALU.max, ALU.min).then_inc(angle.sem, 1)
                for tt in range(2):
                    ins = nc.vector.tensor_scalar(hide[:, tt, :], rowcf[:], colcf[:, tt:tt + 1], None, ALU.is_le)
                steps.then(ins)
                steps.then(nc.vector.tensor_scalar(hide[:], hide[:], 1.0, 1e30, ALU.subtract, ALU.mult))
                for l in range(DEPTH_2):
                    pairs = lv[:, l].rearrange("p (k two) d -> p k two d", two=2)
                    ins = nc.vector.tensor_tensor(lp[:, 2 * l:2 * l + 2, :], pairs[:, :, 0, :], pairs[:, :, 1, :], ALU.mult)
                steps.then(ins)
                nc.vector.tensor_reduce(ls[:], lp[:], AX.X, ALU.add).then_inc(angle.sem, 1)
                for l in range(DEPTH_2):
                    for j in range(2):
                        s = 48 * l + 8 * (1 + 3 * j)
                        ins = nc.vector.scalar_tensor_tensor(gain[:, l, j], core.mod2[:, s:s + 8, 0], 1.0,
                                                             core.vcols(f"ln{j + 1}_g{l}"), ALU.add, ALU.mult)
                steps.then(ins)
                dve.wait_ge(done.sem, done.at(3))
                for l in range(DEPTH_2):
                    ins = nc.vector.scalar_tensor_tensor(lam[:, l], ls[:, 2 * l:2 * l + 1], lambda_init(l), ls[:, 2 * l + 1:2 * l + 2],
                                                         ALU.add, ALU.subtract)
                steps.then(ins)

            @block.scalar
            def _(act):
                act.wait_ge(angle.sem, angle.at(1))
                nc.scalar.activation(sin[:], ang[:], ACT.Sin).then_inc(done.sem, 1)
                nc.scalar.activation(turns[:], ang[:], ACT.Abs).then_inc(done.sem, 1)
                act.wait_ge(done.sem, done.at(2))
                act.wait_ge(angle.sem, angle.at(2))
                nc.scalar.activation(ls[:], ls[:], ACT.Exp).then_inc(done.sem, 1)
                nc.scalar.activation(cos[:], turns[:], ACT.Sin, scale=-1.0, bias=core.col("halfpi", 0)).then_inc(done.sem, 1)
        loaded.passed(48)
        own.passed(13)
        angle.passed(2)
        done.passed(4)


def lambda_init(l):
    return 0.8 - 0.6 * float(np.exp(-0.3 * l))


def linear_recurrence(core, ctx, a, l, z, mix):
    nc = core.nc
    sb = lambda name, shape, dt=F32: core.sb(ctx, f"{name}_{l}", shape, dt)
    T = 4
    wg = sb("gate_w", [P, 2, T, P])
    conv = sb("conv", [P, T, N])
    r = sb("lru_r", [P, T, N])
    i_ = sb("lru_i", [P, T, N])
    av = sb("lru_a", [P, T, N])
    th = sb("lru_th", [P, T, N])
    gy = sb("lru_gy", [P, T, N])
    sp8 = sb("lru_rate", [P, 3, T])
    loaded, conved, made, gated, own, act_s, v_s = (core.count(x) for x in (
        "lru_loaded", "conv_ready", "lru_products", "lru_gates", "lru_vector_steps", "lru_scalar_steps", "lru_logs_ready"))
    lamc = core.vcols(f"lru_lambda{l}")
    with nc.Block() as block:

        @block.sync
        def _(sp):
            sp.dma_start(wg[:], a["lru_gates"][l]).then_inc(loaded.sem, 16)
            sp.wait_ge(loaded.sem, loaded.at(16))

        @block.vector
        def _(dve):
            steps = Steps(dve, own)
            for t in range(T):
                ins = nc.vector.tensor_scalar(conv[:, t, :], z[:, t, :], core.col(f"conv_w{l}", 12 + t), core.col(f"conv_b{l}", t), ALU.mult, ALU.add)
            steps.then(ins)
            for j in range(1, 4):
                for t in range(T):
                    ins = nc.vector.scalar_tensor_tensor(conv[:, t, j:N], z[:, t, 0:N - j], core.col(f"conv_w{l}", 4 * (3 - j) + t),
                                                         conv[:, t, j:N], ALU.mult, ALU.add)
                steps.then(ins)
            nc.vector.tensor_copy(sp8[:, 2, :], lamc).then_inc(conved.sem, 1)
            dve.wait_ge(act_s.sem, act_s.at(3))
            steps.then(nc.vector.scalar_tensor_tensor(sp8[:, 0, :], lamc, 0.0, sp8[:, 1, :], ALU.min, ALU.subtract))
            steps.then(nc.vector.tensor_scalar(sp8[:, 0, :], sp8[:, 0, :], 8.0, None, ALU.mult))
            dve.wait_ge(gated.sem, gated.at(8))
            for t in range(T):
                nc.vector.tensor_tensor(i_[:, t, :], i_[:, t, :], conv[:, t, :], ALU.mult)
                ins = nc.vector.tensor_scalar(r[:, t, :], r[:, t, :], sp8[:, 0, t:t + 1], None, ALU.mult)
            ins.then_inc(v_s.sem, 1)
            dve.wait_ge(act_s.sem, act_s.at(5))
            steps.then(nc.vector.tensor_scalar(r[:], th[:], 1.0, None, ALU.add))
            steps.then(nc.vector.reciprocal(r[:], r[:]))
            nc.vector.scalar_tensor_tensor(r[:], th[:], 2.0, r[:], ALU.mult, ALU.mult).then_inc(v_s.sem, 1)
            dve.wait_ge(act_s.sem, act_s.at(6))
            steps.then(nc.vector.tensor_tensor(i_[:], i_[:], r[:], ALU.mult))
            for t in range(T):
                ins = nc.vector.tensor_tensor_scan(conv[:, t, :], av[:, t, :], i_[:, t, :], 0.0, ALU.mult, ALU.add)
            steps.then(ins)
            dve.wait_ge(act_s.sem, act_s.at(7))
            steps.then(nc.vector.tensor_tensor(mix[:, 0:T, :], conv[:], gy[:], ALU.mult))

        @block.tensor
        def _(pe):
            pe.wait_ge(loaded.sem, loaded.at(16))
            pe.wait_ge(conved.sem, conved.at(1))
            for w in range(2):
                for t in range(T):
                    nc.tensor.matmul(core.bank[2 * w + t // 2][:, (t % 2) * N:(t % 2) * N + N], wg[:, w, t, :], conv[:, t, :],
                                     start=True, stop=True).then_inc(made.sem, 1)

        @block.scalar
        def _(act):
            steps = Steps(act, act_s)
            steps.then(nc.scalar.activation(sp8[:, 1, :], lamc, ACT.Abs))
            steps.then(nc.scalar.activation(sp8[:, 1, :], sp8[:, 1, :], ACT.Exp, scale=-1.0))
            steps.then(nc.scalar.activation(sp8[:, 1, :], sp8[:, 1, :], ACT.Ln, bias=core.col("one", 0)))
            for w, (out, bias) in enumerate(((r, f"gate_a_b{l}"), (i_, f"gate_x_b{l}"))):
                for t in range(T):
                    act.wait_ge(made.sem, made.at(4 * w + t // 2 * 2 + 2))
                    nc.scalar.activation(out[:, t, :], core.bank[2 * w + t // 2][:, (t % 2) * N:(t % 2) * N + N], ACT.Sigmoid,
                                         bias=core.col(bias, t)).then_inc(gated.sem, 1)
            act.wait_ge(v_s.sem, v_s.at(1))
            steps.then(nc.scalar.activation(av[:], r[:], ACT.Exp))
            steps.then(nc.scalar.activation(th[:], r[:], ACT.Tanh, scale=-1.0))
            act.wait_ge(v_s.sem, v_s.at(2))
            steps.then(nc.scalar.activation(r[:], r[:], ACT.Sqrt))
            steps.then(nc.scalar.activation(gy[:], z[:, 4:8, :], ACT.Gelu_apprx_tanh))
    for s, k in ((loaded, 16), (conved, 1), (made, 8), (gated, 8), (own, 11), (act_s, 7), (v_s, 2)):
        s.passed(k)


def attention(core, ctx, a, l, z, v, mix, cos, sin, hide, lam):
    nc = core.nc
    sb = lambda name, shape, dt=F32: core.sb(ctx, f"{name}_{l}", shape, dt)
    H = 4
    qk = sb("qk", [P, 8, N])
    s = sb("att", [P, 16, N])
    mx = sb("att_max", [P, 16])
    tot = sb("att_tot", [P, 16])
    pt = sb("att_t", [P, 2, H, N])
    o = sb("att_o", [P, H, N])
    sq = sb("att_sq", [P, H, N])
    own, turned, roped, scored, shifted, expd, mixed, flipped, flip_kept, made, copied, squared, meant, rooted = (
        core.count(x) for x in ("att_vector_steps", "half_turned", "roped", "att_scored", "att_shifted", "att_exp", "att_mixed",
                                "att_flipped", "flip_kept", "att_made", "att_copied", "att_squared", "att_mean", "att_root"))
    with nc.Block() as block:

        @block.tensor
        def _(pe):
            for t in range(8):
                last = nc.tensor.matmul(core.bank[t // 2][:, (t % 2) * N:(t % 2) * N + N], core.rot, z[:, 8 + t, :], start=True, stop=True)
                if t % 2:
                    last.then_inc(turned.sem, 1)
            pe.wait_ge(roped.sem, roped.at(1))
            for h in range(H):
                for c in range(2):
                    rows = slice(DH * c, DH * c + DH)
                    for tt in range(2):
                        last = nc.tensor.matmul(core.bank[2 * h + c][:, tt * N:tt * N + N], qk[rows, h, tt * P:tt * P + P], qk[rows, 4 + h, :],
                                                start=True, stop=True)
                    last.then_inc(scored.sem, 1)
            for h in range(H):
                pe.wait_ge(mixed.sem, mixed.at(2 * h + 2))
                for kt in range(2):
                    for tt in range(2):
                        last = nc.tensor.transpose(core.bank[h][:, kt * N + tt * P:kt * N + tt * P + P],
                                                   s[:, 4 * h + tt, kt * P:kt * P + P], core.ident)
                last.then_inc(flipped.sem, 1)
            for h in range(H):
                pe.wait_ge(flip_kept.sem, flip_kept.at(h + 1))
                for kt in range(2):
                    last = nc.tensor.matmul(core.bank[4 + h // 2][:, (h % 2) * N:(h % 2) * N + N], v[:, kt, h * P:h * P + P], pt[:, kt, h, :],
                                            start=(kt == 0), stop=(kt == 1))
                if h % 2:
                    last.then_inc(made.sem, 1)
            for g in range(2):
                pe.wait_ge(squared.sem, squared.at(g + 1))
                nc.tensor.matmul(core.bank[6 + g][:, :], core.avg_head[:], sq[:, 2 * g:2 * g + 2, :].rearrange("p h n -> p (h n)"),
                                 start=True, stop=True).then_inc(meant.sem, 1)

        @block.vector
        def _(dve):
            steps = Steps(dve, own)
            cosb = cos[:].rearrange("p (o n) -> p o n", o=1)
            sinb = sin[:].rearrange("p (o n) -> p o n", o=1)
            nc.vector.tensor_tensor(qk[:], z[:, 8:16, :], cosb.broadcast_to([P, 8, N]), ALU.mult)
            for g in range(4):
                dve.wait_ge(turned.sem, turned.at(g + 1))
                ins = nc.vector.tensor_tensor(s[:, 2 * g:2 * g + 2, :], core.bank[g][:, :].rearrange("p (t n) -> p t n", n=N),
                                              sinb.broadcast_to([P, 2, N]), ALU.mult)
            steps.then(ins)
            nc.vector.tensor_tensor(qk[:], qk[:], s[:, 0:8, :], ALU.add).then_inc(roped.sem, 1)
            dve.wait_ge(roped.sem, roped.at(1))
            for j in range(8):
                dve.wait_ge(scored.sem, scored.at(j + 1))
                pair = slice(2 * j, 2 * j + 2)
                steps.then(nc.vector.scalar_tensor_tensor(s[:, pair, :], core.bank[j][:, :].rearrange("p (t n) -> p t n", n=N),
                                                          DH ** -0.5, hide[:], ALU.mult, ALU.add))
                steps.then(nc.vector.tensor_reduce(mx[:, pair], s[:, pair, :], AX.X, ALU.max))
                nc.vector.tensor_scalar(mx[:, pair], mx[:, pair], -1.0, None, ALU.mult).then_inc(shifted.sem, 1)
            dve.wait_ge(expd.sem, expd.at(16))
            steps.then(nc.vector.reciprocal(tot[:], tot[:]))
            t4 = tot[:].rearrange("p (h c t) -> p h c t", c=2, t=2)
            steps.then(nc.vector.tensor_scalar(t4[:, :, 1, :], t4[:, :, 1, :], lam[:, l], None, ALU.mult))
            for h in range(H):
                for tt in range(2):
                    ins = nc.vector.tensor_scalar(s[:, 4 * h + tt + 2, :], s[:, 4 * h + tt + 2, :], tot[:, 4 * h + tt + 2:4 * h + tt + 3], None, ALU.mult)
                steps.then(ins)
                for tt in range(2):
                    j = 4 * h + tt
                    nc.vector.scalar_tensor_tensor(s[:, j, :], s[:, j, :], tot[:, j:j + 1], s[:, j + 2, :], ALU.mult, ALU.subtract)                        .then_inc(mixed.sem, 1)
            for h in range(H):
                dve.wait_ge(flipped.sem, flipped.at(h + 1))
                nc.vector.tensor_copy(pt[:, :, h, :], core.bank[h][:, :].rearrange("p (k n) -> p k n", n=N)).then_inc(flip_kept.sem, 1)
            for g in range(2):
                dve.wait_ge(made.sem, made.at(g + 1))
                nc.vector.tensor_copy(o[:, 2 * g:2 * g + 2, :], core.bank[4 + g][:, :].rearrange("p (h n) -> p h n", n=N)).then_inc(copied.sem, 1)
            dve.wait_ge(rooted.sem, rooted.at(2))
            steps.then(nc.vector.reciprocal(sq[:], sq[:]))
            steps.then(nc.vector.scalar_tensor_tensor(o[:], o[:], core.col(f"subln_g{l}", 0), sq[:], ALU.mult, ALU.mult))
            steps.then(nc.vector.tensor_scalar(mix[:, 4:8, :], o[:], 1.0 - lambda_init(l), None, ALU.mult))

        @block.scalar
        def _(act):
            for j in range(16):
                if j % 2 == 0:
                    act.wait_ge(shifted.sem, shifted.at(j // 2 + 1))
                nc.scalar.activation(s[:, j, :], s[:, j, :], ACT.Exp, bias=mx[:, j:j + 1], accum_out=tot[:, j:j + 1]).then_inc(expd.sem, 1)
            for g in range(2):
                act.wait_ge(copied.sem, copied.at(g + 1))
                nc.scalar.activation(sq[:, 2 * g:2 * g + 2, :], o[:, 2 * g:2 * g + 2, :], ACT.Square).then_inc(squared.sem, 1)
            for g in range(2):
                act.wait_ge(meant.sem, meant.at(g + 1))
                nc.scalar.activation(sq[:, 2 * g:2 * g + 2, :], core.bank[6 + g][:, :].rearrange("p (h n) -> p h n", n=N), ACT.Sqrt,
                                     bias=core.col("eps", 0)).then_inc(rooted.sem, 1)
    for c, k in ((own, 26), (turned, 4), (roped, 1), (scored, 8), (shifted, 8), (expd, 16), (mixed, 8), (flipped, 4),
                 (flip_kept, 4), (made, 2), (copied, 2), (squared, 2), (meant, 2), (rooted, 2)):
        c.passed(k)


def route(core, a, r):
    nc = core.nc
    with ExitStack() as ctx:
        sb = lambda name, shape, dt=F32: core.sb(ctx, name, shape, dt)
        rw = sb("router_w", [P, C, EXPERTS])
        lg = sb("logits", [P, 2, EXPERTS])
        top = sb("route_top", [P, 2, 8])
        idx = sb("route_idx", [P, 2, 8], U32)
        idf = sb("route_idf", [P, 2, 8])
        e = sb("route_e", [P, 2, 1])
        w = sb("route_w", [P, 2, 2])
        hot = sb("route_hot", [P, 2, 2, EXPERTS])
        g = sb("route_g", [P, 2, EXPERTS])
        chosen = sb("route_chosen", [P, 2, EXPERTS])
        gt = sb("route_gt", [EXPERTS, 2, N])
        more = sb("route_more", [P, EXPERTS])
        rank = sb("route_rank", [P, EXPERTS])
        which = sb("route_which", [P, MORE, EXPERTS])
        named = sb("route_named", [P, MORE, EXPERTS])
        tab = sb("route_tab", [P, ROUNDS + 2])
        ones = sb("route_ones", [P, P])
        shares, place_rows, place_cols, first, table, ht = (r[k] for k in ("shares", "place_rows", "place_cols", "first", "table", "ht"))
        loaded, scored, own, expd, ready, turned, kept, spread, copied, ranked, flipped, flips = (core.count(x) for x in (
            "router_loaded", "routed", "route_vector_steps", "route_exp", "route_ready", "route_turned", "route_kept",
            "route_spread", "route_copied", "route_ranked", "tokens_turned", "tokens_copied"))
        with nc.Block() as block:

            @block.sync
            def _(sp):
                sp.dma_start(rw[:], a["router"]).then_inc(loaded.sem, 16)
                sp.wait_ge(loaded.sem, loaded.at(16))

            @block.tensor
            def _(pe):
                pe.wait_ge(loaded.sem, loaded.at(16))
                for tt in range(2):
                    for c in range(C):
                        last = nc.tensor.matmul(core.bank[0][:, tt * EXPERTS:tt * EXPERTS + EXPERTS], core.h[:, c, tt * P:tt * P + P],
                                                rw[:, c, :], start=(c == 0), stop=(c == C - 1))
                last.then_inc(scored.sem, 1)
                for q in range(4):
                    for j in range(4):
                        tt, c = q // 2, 4 * (q % 2) + j
                        last = nc.tensor.transpose(core.bank[4 + q][:, j * P:j * P + P], core.h[:, c, tt * P:tt * P + P], core.ident)
                    last.then_inc(flipped.sem, 1)
                pe.wait_ge(ready.sem, ready.at(2))
                nc.tensor.matmul(core.bank[2][:, 0:EXPERTS], core.before, chosen[:, 0, :], start=True, stop=True)
                nc.tensor.matmul(core.bank[2][:, EXPERTS:2 * EXPERTS], ones[:], chosen[:, 0, :], start=True, stop=False)
                nc.tensor.matmul(core.bank[2][:, EXPERTS:2 * EXPERTS], core.before, chosen[:, 1, :], start=False, stop=True)
                nc.tensor.matmul(core.bank[2][:, 2 * EXPERTS:3 * EXPERTS], ones[:], chosen[:, 0, :], start=True, stop=False)
                nc.tensor.matmul(core.bank[2][:, 2 * EXPERTS:3 * EXPERTS], ones[:], chosen[:, 1, :], start=False, stop=True)\
                    .then_inc(ranked.sem, 1)
                pe.wait_ge(ready.sem, ready.at(3))
                for k, src in enumerate((g, place_cols)):
                    for tt in range(2):
                        last = nc.tensor.transpose(core.bank[1][0:EXPERTS, k * N + tt * P:k * N + tt * P + P], src[:, tt, :], core.ident)
                last.then_inc(turned.sem, 1)
                pe.wait_ge(kept.sem, kept.at(1))
                pe.wait_ge(flips.sem, flips.at(4))
                for k in range(2):
                    if k:
                        pe.wait_ge(copied.sem, copied.at(4))
                    for x in range(EXPERTS):
                        last = nc.tensor.matmul(core.bank[4 + x // 2][:, (x % 2) * N:(x % 2) * N + N], core.sel[0:EXPERTS, x, :], gt[:, k, :],
                                                start=True, stop=True)
                    last.then_inc(spread.sem, 1)

            @block.vector
            def _(dve):
                steps = Steps(dve, own)
                nc.vector.memset(ones[:], 1.0)
                nc.vector.memset(tab[:], 0.0)
                nc.vector.memset(first[:], 0.0)
                dve.wait_ge(scored.sem, scored.at(1))
                steps.then(nc.vector.tensor_copy(lg[:], core.bank[0][:, 0:2 * EXPERTS].rearrange("p (t e) -> p t e", t=2)))
                for tt in range(2):
                    ins = nc.vector.max(top[:, tt, :], lg[:, tt, :])
                steps.then(ins)
                for tt in range(2):
                    ins = nc.vector.max_index(idx[:, tt, :], top[:, tt, :], lg[:, tt, :])
                steps.then(ins)
                nc.vector.tensor_copy(idf[:], idx[:])
                nc.vector.tensor_tensor(e[:], top[:, :, 1:2], top[:, :, 0:1], ALU.subtract).then_inc(ready.sem, 1)
                dve.wait_ge(expd.sem, expd.at(1))
                steps.then(nc.vector.tensor_scalar(w[:, :, 0:1], e[:], 1.0, None, ALU.add))
                steps.then(nc.vector.reciprocal(w[:, :, 0:1], w[:, :, 0:1]))
                steps.then(nc.vector.tensor_tensor(w[:, :, 1:2], w[:, :, 0:1], e[:], ALU.mult))
                for tt in range(2):
                    for k in range(2):
                        ins = nc.vector.tensor_scalar(hot[:, tt, k, :], core.iota[:, 0:EXPERTS], idf[:, tt, k:k + 1], w[:, tt, k:k + 1],
                                                      ALU.is_equal, ALU.mult)
                steps.then(ins)
                steps.then(nc.vector.tensor_tensor(g[:], hot[:, :, 0, :], hot[:, :, 1, :], ALU.add))
                nc.vector.tensor_scalar(chosen[:], g[:], 0.0, None, ALU.is_gt).then_inc(ready.sem, 1)
                dve.wait_ge(ranked.sem, ranked.at(1))
                steps.then(nc.vector.scalar_tensor_tensor(place_cols[:], core.bank[2][:, 0:2 * EXPERTS].rearrange("p (t e) -> p t e", t=2), 1.0,
                                                          chosen[:], ALU.add, ALU.mult))
                nc.vector.tensor_scalar(place_cols[:], place_cols[:], 1.0, None, ALU.subtract).then_inc(ready.sem, 1)
                steps.then(nc.vector.tensor_scalar(more[:], core.bank[2][:, 2 * EXPERTS:3 * EXPERTS], float(P), None, ALU.is_gt))
                steps.then(nc.vector.tensor_tensor_scan(rank[:], more[:], more[:], 0.0, ALU.add, ALU.bypass))
                for j in range(MORE):
                    ins = nc.vector.scalar_tensor_tensor(which[:, j, :], rank[:], float(j + 1), more[:], ALU.is_equal, ALU.mult)
                steps.then(ins)
                for j in range(MORE):
                    ins = nc.vector.tensor_tensor(named[:, j, :], which[:, j, :], core.iota[:, 0:EXPERTS], ALU.mult)
                steps.then(ins)
                nc.vector.tensor_copy(tab[:, 0:EXPERTS], core.iota[:, 0:EXPERTS])
                nc.vector.tensor_reduce(tab[:, EXPERTS:ROUNDS], named[:], AX.X, ALU.add)
                steps.then(nc.vector.tensor_reduce(first[:, EXPERTS:ROUNDS], which[:], AX.X, ALU.add))
                steps.then(nc.vector.tensor_scalar(first[:, EXPERTS:ROUNDS], first[:, EXPERTS:ROUNDS], float(P) - FAR, FAR, ALU.mult, ALU.add))
                steps.then(nc.vector.memset(first[:, ROUNDS:ROUNDS + 1], FAR))
                steps.then(nc.vector.tensor_scalar(tab[:, ROUNDS + 1:ROUNDS + 2], rank[:, EXPERTS - 1:EXPERTS], float(EXPERTS), None, ALU.add))
                steps.then(nc.vector.tensor_copy(table[0:1, :], tab[0:1, :]))
                dve.wait_ge(turned.sem, turned.at(1))
                nc.vector.tensor_copy(gt[:, :, :], core.bank[1][0:EXPERTS, :].rearrange("p (k n) -> p k n", k=2)).then_inc(kept.sem, 1)
                for k, dst in enumerate((shares, place_rows)):
                    dve.wait_ge(spread.sem, spread.at(k + 1))
                    for b in range(4):
                        nc.vector.tensor_copy(dst[:, 2 * b:2 * b + 2, :], core.bank[4 + b][:, :].rearrange("p (e n) -> p e n", n=N))\
                            .then_inc(copied.sem, 1)
                n_own.append(steps.k)

            @block.scalar
            def _(act):
                for q in range(4):
                    act.wait_ge(flipped.sem, flipped.at(q + 1))
                    nc.scalar.activation(ht[:, q // 2, 512 * (q % 2):512 * (q % 2) + 512], core.bank[4 + q][:, :], ACT.Copy).then_inc(flips.sem, 1)
                act.wait_ge(ready.sem, ready.at(1))
                nc.scalar.activation(e[:], e[:], ACT.Exp).then_inc(expd.sem, 1)
        for c, k in ((loaded, 16), (scored, 1), (own, n_own.pop()), (expd, 1), (ready, 3), (turned, 1), (kept, 1), (spread, 2),
                     (copied, 8), (ranked, 1), (flipped, 4), (flips, 4)):
            c.passed(k)


def feed_forward(core, ctx, gu, down, next_tiles, x, gate):
    nc = core.nc
    hid_hi = core.sb(ctx, "hid_high", [P, FT, N], F32R)
    hid_lo = core.sb(ctx, "hid_low", [P, FT, N], F32R)
    whole = core.sb(ctx, "hid_whole", [P, 2, N])
    split = Split(core, ctx, "ffn", core.h, N)
    halver = Halver(core, ctx, "ffn")
    sg = core.sb(ctx, "silu", [P, 2, N])
    used, free = core.tiles_used, core.pair_free
    silued, ready, read, own = core.count("ffn_silu"), core.count("ffn_hidden"), core.count("ffn_read"), core.count("ffn_vector_steps")
    R1, R2 = 2 * FT // U, FT // U
    R = R1 + R2
    with nc.Block() as block:

        @block.sync
        def _(sp):
            with sp.Fori(1, R1) as i:
                for u in range(U):
                    halver.reload(sp, u, i, gu[u % 2, i * 2 + u // 2])
            with sp.Fori(0, R2) as i:
                for u in range(U):
                    halver.reload(sp, U * R1 + u, i, down[i * U + u])
            for u in range(U):
                halver.reload(sp, U * R + u, 0, next_tiles(u))

        @block.tensor
        def _(pe):
            zero_banks(core, pe, range(4, 8))
            pe.wait_ge(halver.low_split.sem, halver.low_split.at(C))
            with pe.Fori(0, R1) as i:
                for u in range(U):
                    if u % 2 == 0:
                        pe.wait_ge(free.sem, free.at(u // 2 + 1) + i * 2)
                    halver.products(pe, u, i, lambda c: core.bank[u][:, 0:N], lambda c: split.high[:, c, :], lambda c: split.low[:, c, :],
                                    True, True)
            with pe.Fori(0, R2) as i:
                for u in range(U):
                    pe.wait_ge(ready.sem, ready.at(u + 1) + i * U)
                    part = lambda t: t[:, bass.ds(i * U + u, 1), :].rearrange("p o n -> p (o n)")
                    halver.products(pe, U * R1 + u, i, lambda m: core.bank[4 + m // 2][:, (m % 2) * N:(m % 2) * N + N],
                                    lambda m: part(hid_hi), lambda m: part(hid_lo), False, False)
            for b in range(4, 8):
                last = nc.tensor.matmul(core.bank[b][:, :].rearrange("p (o n) -> p o n", o=4), core.zeros[:], core.zeros[:].rearrange("p (o n) -> p o n", o=1).broadcast_to([P, 4, P]), start=False, stop=True, skip_group_check=True)
            last.then_inc(read.sem, 1)

        @block.scalar
        def _(act):
            def silu(w, i):
                act.wait_ge(used.sem, used.at(2 * w + 1) + i * U)
                nc.scalar.activation(sg[:, w, :], core.bank[2 * w][:, 0:N], ACT.Silu).then_inc(silued.sem, 1)

            def round_(place, i, before, here):
                for u in range(U):
                    halver.high(act, place + u, i)
                    if u == 1 and before is not None:
                        silu(1, before)
                    if u == 3 and here:
                        silu(0, i)

            halver.credit(act)
            halver.split_high(act, split)
            round_(0, 0, None, True)
            with act.Fori(1, R1) as i:
                round_(0, i, i - 1, True)
            round_(U * R1, 0, R1 - 1, False)
            with act.Fori(1, R2) as i:
                round_(U * R1, i, None, False)

        @block.vector
        def _(dve):
            def hidden(w, i):
                dve.wait_ge(silued.sem, silued.at(w + 1) + i * 2)
                dve.wait_ge(used.sem, used.at(2 * w + 2) + i * U)
                hi, lo = (t[:, bass.ds(i * 2 + w, 1), :].rearrange("p o n -> p (o n)") for t in (hid_hi, hid_lo))
                nc.vector.tensor_tensor(whole[:, w, :], sg[:, w, :], core.bank[2 * w + 1][:, 0:N], ALU.mult).then_inc(own.sem, 1)
                nc.vector.tensor_tensor(hi, sg[:, w, :], core.bank[2 * w + 1][:, 0:N], ALU.mult).then_inc(free.sem, 1)
                dve.wait_ge(own.sem, own.at(w + 1) + i * 2)
                dve.wait_ge(free.sem, free.at(2 + w + 1) + i * 2)
                nc.vector.tensor_tensor(lo, whole[:, w, :], hi.bitcast(F32), ALU.subtract).then_inc(ready.sem, 1)

            def round_(place, i, before, here):
                for u in range(U):
                    halver.lower(dve, place + u, i)
                    if u == 1 and before is not None:
                        hidden(1, before)
                    if u == 3 and here:
                        hidden(0, i)

            halver.split_low(dve, split)
            round_(0, 0, None, True)
            with dve.Fori(1, R1) as i:
                round_(0, i, i - 1, True)
            round_(U * R1, 0, R1 - 1, False)
            with dve.Fori(1, R2) as i:
                round_(U * R1, i, None, False)
            dve.wait_ge(read.sem, read.at(1))
            for m in range(C):
                nc.vector.scalar_tensor_tensor(x[:, m, :], core.bank[4 + m // 2][:, (m % 2) * N:(m % 2) * N + N], gate[:, m:m + 1], x[:, m, :],
                                               ALU.mult, ALU.add).then_inc(read.sem, 1)
    used.passed(U * R)
    free.passed(FT)
    silued.passed(FT)
    ready.passed(FT)
    own.passed(FT)
    read.passed(1 + C)
    halver.passed(U * R, True)
    for u in range(U):
        core.landed[u].passed(16 * R)


def routed_feed_forward(core, ctx, a, x, gate):
    nc = core.nc
    sb = lambda name, shape, dt=F32: core.sb(ctx, name, shape, dt)
    r = dict(shares=sb("shares", [P, EXPERTS, N]), place_rows=sb("place_rows", [P, EXPERTS, N]),
             place_cols=sb("place_cols", [P, 2, EXPERTS]), first=sb("first", [P, ROUNDS + 1]),
             table=sb("round_table", [1, ROUNDS + 2], I32), ht=sb("h_tokens", [P, 2, D]))
    route(core, a, r)
    shares, place_rows, place_cols, first, table, ht = (r[k] for k in ("shares", "place_rows", "place_cols", "first", "table", "ht"))
    M = P
    hid = sb("hid_r", [P, FT, M])
    xg = sb("xg", [P, C, M])
    yg = sb("yg", [P, D])
    pick = sb("pick", [P, 2, M])
    back = sb("back", [P, N])
    sg = sb("silu_r", [P, 2, M])
    used, free = core.tiles_used, core.pair_free
    silued, ready = core.count("ffn_silu"), core.count("ffn_hidden")
    picks, gathered, xg_ready, backs, y_kept, scattered, added, offs = (core.count(n) for n in (
        "picks_ready", "tokens_gathered", "gathered_copied", "backs_ready", "outputs_kept", "outputs_scattered", "outputs_added",
        "place_offset"))
    own = core.count("round_vector_steps")
    off = sb("offset", [P, 1])
    R1, R2 = 2 * FT // U, FT // U
    R = R1 + R2
    T = U * R
    gu, down = a["moe_gu"], a["moe_d"]

    def n_rounds(eng):
        return eng.value_load(table[0:1, ROUNDS + 1:ROUNDS + 2], min_val=EXPERTS, max_val=ROUNDS)

    def expert_of(eng, k):
        return eng.value_load(table[0:1, bass.ds(k, 1)], min_val=0, max_val=EXPERTS - 1)

    with nc.Block() as block:

        @block.sync
        def _(sp):
            def load(k, e, start):
                with sp.Fori(start, R1) as i:
                    for u in range(U):
                        sp.wait_ge(used.sem, used.at(u + 1 - U) + k * T + i * U)
                        core.load_tile(sp, u, gu[u % 2, e * FT + i * 2 + u // 2])
                with sp.Fori(0, R2) as i:
                    for u in range(U):
                        sp.wait_ge(used.sem, used.at(U * R1 + u + 1 - U) + k * T + i * U)
                        core.load_tile(sp, u, down[e * FT + i * U + u])

            load(0, 0, 1)
            with sp.Fori(1, n_rounds(sp)) as k:
                load(k, expert_of(sp, k), 0)

        @block.tensor
        def _(pe):
            def gather(k):
                pe.wait_ge(picks.sem, picks.at(1) + k)
                for b in range(2):
                    for j in range(4):
                        for tt in range(2):
                            c = 4 * b + j
                            last = nc.tensor.matmul(core.bank[6 + b][:, j * M:j * M + M], ht[:, tt, c * P:c * P + P], pick[:, tt, :],
                                                    start=(tt == 0), stop=(tt == 1))
                    last.then_inc(gathered.sem, 1)

            gather(0)
            with pe.Fori(0, n_rounds(pe)) as k:
                with pe.Fori(0, R1) as i:
                    pe.wait_ge(xg_ready.sem, xg_ready.at(2) + k * 2)
                    for u in range(U):
                        pe.wait_ge(core.landed[u].sem, core.landed[u].at(16) + k * (16 * R) + i * 16)
                        if u % 2 == 0:
                            pe.wait_ge(free.sem, free.at(u // 2 + 1) + k * FT + i * 2)
                        for c in range(C):
                            last = nc.tensor.matmul(core.bank[u][:, 0:M], core.slot[u][:, c, :], xg[:, c, :], start=(c == 0), stop=(c == C - 1))
                        last.then_inc(used.sem, 1)
                for t in range(FT):
                    u = t % U
                    pe.wait_ge(core.landed[u].sem, core.landed[u].at(16 * (R1 + t // U + 1)) + k * (16 * R))
                    pe.wait_ge(ready.sem, ready.at(t + 1) + k * FT)
                    for b in range(2):
                        last = nc.tensor.matmul(core.bank[4 + b][:, :], hid[:, t, :], core.slot[u][:, 4 * b:4 * b + 4, :].rearrange("p c m -> p (c m)"),
                                                start=(t == 0), stop=(t == FT - 1))
                    last.then_inc(used.sem, 1)
                gather(k + 1)
                pe.wait_ge(backs.sem, backs.at(1) + k)
                pe.wait_ge(y_kept.sem, y_kept.at(2) + k * 2)
                for s in range(4):
                    if s < 2:
                        pe.wait_ge(xg_ready.sem, xg_ready.at(2 + s + 1) + k * 2)
                    else:
                        pe.wait_ge(added.sem, added.at(2 * (s - 1)) + k * C)
                    for j in range(2):
                        m = 2 * s + j
                        last = nc.tensor.matmul(core.bank[6 + s % 2][:, j * N:j * N + N], yg[:, m * P:m * P + P], back[:, :], start=True, stop=True)
                    last.then_inc(scattered.sem, 1)

        @block.scalar
        def _(act):
            def copy_gathered(k):
                for b in range(2):
                    act.wait_ge(gathered.sem, gathered.at(b + 1) + k * 2)
                    nc.scalar.activation(xg[:, 4 * b:4 * b + 4, :], core.bank[6 + b][:, :].rearrange("p (c m) -> p c m", m=M), ACT.Copy)\
                        .then_inc(xg_ready.sem, 1)

            copy_gathered(0)
            with act.Fori(0, n_rounds(act)) as k:
                with act.Fori(0, R1) as i:
                    for w in range(2):
                        act.wait_ge(used.sem, used.at(2 * w + 1) + k * T + i * U)
                        nc.scalar.activation(sg[:, w, :], core.bank[2 * w][:, 0:M], ACT.Silu).then_inc(silued.sem, 1)
                act.wait_ge(used.sem, used.at(T) + k * T)
                for b in range(2):
                    nc.scalar.activation(yg[:, 512 * b:512 * b + 512], core.bank[4 + b][:, :], ACT.Copy).then_inc(y_kept.sem, 1)
                copy_gathered(k + 1)

        @block.vector
        def _(dve):
            def make_pick(k):
                e = expert_of(dve, k)
                for tt in range(2):
                    ins = nc.vector.tensor_scalar(pick[:, tt, :], core.iota, first[:, bass.ds(k, 1)], place_cols[:, tt, bass.ds(e, 1)],
                                                  ALU.add, ALU.is_equal)
                ins.then_inc(picks.sem, 1)

            make_pick(0)
            with dve.Fori(0, n_rounds(dve)) as k:
                dve.wait_ge(gathered.sem, gathered.at(2) + k * 2)
                make_pick(k + 1)
                e = expert_of(dve, k)
                nc.vector.tensor_tensor(off[:], core.col("partition", 0), first[:, bass.ds(k, 1)], ALU.add).then_inc(offs.sem, 1)
                dve.wait_ge(offs.sem, offs.at(1) + k)
                nc.vector.scalar_tensor_tensor(back[:, :], place_rows[:, bass.ds(e, 1), :].rearrange("p o n -> p (o n)"), off[:, 0:1],
                                               shares[:, bass.ds(e, 1), :].rearrange("p o n -> p (o n)"), ALU.is_equal, ALU.mult)\
                    .then_inc(backs.sem, 1)
                with dve.Fori(0, R1) as i:
                    for w in range(2):
                        dve.wait_ge(silued.sem, silued.at(w + 1) + k * FT + i * 2)
                        dve.wait_ge(used.sem, used.at(2 * w + 2) + k * T + i * U)
                        out = hid[:, bass.ds(i * 2 + w, 1), :].rearrange("p o n -> p (o n)")
                        nc.vector.tensor_tensor(out, sg[:, w, :], core.bank[2 * w + 1][:, 0:M], ALU.mult).then_inc(free.sem, 1)
                        dve.wait_ge(free.sem, free.at(2 + w + 1) + k * FT + i * 2)
                        dve.sem_inc(ready.sem, 1)
                for s in range(4):
                    dve.wait_ge(scattered.sem, scattered.at(s + 1) + k * 4)
                    for j in range(2):
                        m = 2 * s + j
                        nc.vector.scalar_tensor_tensor(x[:, m, :], core.bank[6 + s % 2][:, j * N:j * N + N], gate[:, m:m + 1], x[:, m, :],
                                                       ALU.mult, ALU.add).then_inc(added.sem, 1)



def as_columns(v):
    return np.ascontiguousarray(v.reshape(-1, P).T)


def as_tiles(w):
    k, m = w.shape
    return np.ascontiguousarray(w.reshape(k // P, P, m // P, P).transpose(2, 1, 0, 3)).reshape(m // P, P, k)


def constants():
    const = np.zeros((N_CONST, P, P), np.float32)
    const[0] = np.eye(P)
    for d in range(P):
        h = d % DH
        if h < DH // 2:
            const[1, d + DH // 2, d] = -1.0
        else:
            const[1, d - DH // 2, d] = 1.0
    const[2] = np.arange(P)[None, :]
    for e in range(EXPERTS):
        const[3 + e, e, :] = 1.0
    const[3 + EXPERTS] = np.triu(np.ones((P, P)), 1)
    i = np.arange(P)
    mask = np.zeros((LEVELS + 1, P, P), np.int32)
    for l in range(LEVELS):
        same = (i[:, None] >> (l + 1)) == (i[None, :] >> (l + 1))
        mask[l] = same & ((i[:, None] >> l) != (i[None, :] >> l))
    mask[LEVELS] = np.eye(P)
    return const, mask


def lay_out(x, c, ctx, c_ctx, w_ada, b_ada, w_in, w_gk2, b_gk, hg_lower_bounds, hg_norm, gla_norm,
            w_out, ln_gamma, ln_beta, peer_w_query, peer_sub_keys, peer_u, peer_v, c_2, positions_2,
            ada_w_2, ada_b_2, ln1_g_2, ln2_g_2, w_in_2, conv_w_2, conv_b_2, gate_a_w_2, gate_a_b_2,
            gate_x_w_2, gate_x_b_2, lru_lambda_2, lam_q1_2, lam_k1_2, lam_q2_2, lam_k2_2, subln_g_2,
            w_out_2, ffn_w_gate_2, ffn_w_up_2, ffn_w_down_2, moe_router_2, moe_w_gate_2, moe_w_up_2,
            moe_w_down_2, final_g_2):
    a = {}
    tokens = np.concatenate([ctx[0], x[0]], axis=0)
    a["x"] = np.ascontiguousarray(tokens.reshape(L, C, P).transpose(2, 1, 0))
    vec = np.zeros((P, NVEC), np.float32)

    def put(name, block):
        at, n = COLS[name]
        vec[:, at:at + n] = block

    cc = np.stack([c[0], c_ctx]).reshape(2, C, P).transpose(2, 1, 0).reshape(P, 2 * C)
    put("c", cc)
    put("b_ada", as_columns(b_ada))
    put("lb", as_columns(hg_lower_bounds))
    put("b_gk", as_columns(b_gk))
    put("hg_norm", as_columns(hg_norm))
    put("gla_norm", as_columns(gla_norm))
    for j in range(2):
        put(f"ln_gamma{j}", as_columns(ln_gamma[0, j]))
        put(f"ln_beta{j}", as_columns(ln_beta[0, j]))
    put("c_2", as_columns(c_2))
    put("final_g", as_columns(final_g_2))
    half = np.arange(P) % (DH // 2)
    put("inv_freq", (np.float32(10000.0) ** (-(2 * half).astype(np.float32) / np.float32(DH)))[:, None])
    put("one", 1.0)
    put("eps", EPS)
    put("halfpi", TWO_PI / 4)
    put("partition", np.arange(P, dtype=np.float32)[:, None])
    for l in range(DEPTH_2):
        for name, v in (("ada_b", ada_b_2), ("ln1_g", ln1_g_2), ("ln2_g", ln2_g_2), ("conv_w", conv_w_2), ("conv_b", conv_b_2),
                        ("gate_a_b", gate_a_b_2), ("gate_x_b", gate_x_b_2), ("lru_lambda", lru_lambda_2), ("subln_g", subln_g_2)):
            put(f"{name}{l}", as_columns(v[l]))
    a["vec"] = vec
    a["const"], a["mask"] = constants()
    a["w_ada"] = np.ascontiguousarray(w_ada[0].reshape(C, P, 6, D).transpose(2, 0, 1, 3)).reshape(6 * C, P, D)
    a["ada_w_2"] = np.ascontiguousarray(ada_w_2.reshape(DEPTH_2, C, P, 6, D).transpose(0, 3, 1, 2, 4)).reshape(DEPTH_2 * 6 * C, P, D)
    w = w_in[0]
    at = np.cumsum([0, 512, 512, 512, 512, 512, 256, 256, 512, 512, 16, 16])
    hq, hff, hfb, hi, hg, gq, gk, gv, gg = (w[:, at[i]:at[i + 1]] for i in range(9))
    a["w_in"] = as_tiles(np.concatenate([hff, hfb, gk, gq, hq, hg, gg, hi, gv], axis=1))
    a["w_rank"] = np.ascontiguousarray(w[:, at[9]:at[11]].reshape(C, P, 32).transpose(1, 0, 2))
    a["w_gk2"] = np.ascontiguousarray(w_gk2[0].transpose(1, 0, 2))
    a["w_out"] = as_tiles(w_out[0])
    a["w_query"] = as_tiles(peer_w_query[0])
    a["keys"] = np.ascontiguousarray(peer_sub_keys[0].transpose(2, 0, 1))
    a["peer_u"] = np.ascontiguousarray(peer_u[0].reshape(P, P, C, P).transpose(0, 3, 2, 1)).reshape(P, P, D)
    a["peer_v"] = peer_v[0].reshape(P, P, D)
    a["w_in_2"] = np.concatenate([as_tiles(w_in_2[l]) for l in range(DEPTH_2)])
    a["w_out_2"] = np.concatenate([as_tiles(w_out_2[l]) for l in range(DEPTH_2)])
    gates_w = np.zeros((DEPTH_2, P, 2, 4, P), np.float32)
    for l in range(DEPTH_2):
        for w_, src in enumerate((gate_a_w_2, gate_x_w_2)):
            for n in range(8):
                r = 64 * (n % 2)
                gates_w[l, r:r + 64, w_, n // 2, r:r + 64] = src[l, n]
    a["lru_gates"] = gates_w
    a["pos"] = positions_2[0]
    a["pos_cols"] = np.ascontiguousarray(positions_2[0].reshape(2, P).T)
    a["lam_rows"] = np.stack([lam_q1_2, lam_k1_2, lam_q2_2, lam_k2_2], axis=1)[None]
    a["ffn_gu"] = np.stack([as_tiles(ffn_w_gate_2[0]), as_tiles(ffn_w_up_2[0])])
    a["ffn_d"] = ffn_w_down_2[0].reshape(FT, P, D)
    a["moe_gu"] = np.stack([np.concatenate([as_tiles(w_[0, e]) for e in range(EXPERTS)]) for w_ in (moe_w_gate_2, moe_w_up_2)])
    a["moe_d"] = moe_w_down_2[0].reshape(EXPERTS * FT, P, D)
    a["router"] = np.ascontiguousarray(moe_router_2[0].reshape(C, P, EXPERTS).transpose(1, 0, 2))
    return a


def kernel(**inputs):
    import concourse.bacc as bacc
    from concourse.bass_utils import run_bass_kernel_spmd

    arrays = lay_out(**{k: np.asarray(v) for k, v in inputs.items()})
    nc = bacc.Bacc("TRN2", target_bir_lowering=False, num_devices=1)
    a = {}
    for name, v in arrays.items():
        a[name] = nc.dram_tensor(f"in_{name}", v.shape, mybir.dt.from_np(v.dtype), kind="ExternalInput").ap()
    a["out"] = nc.dram_tensor("out", [P, C, N], F32, kind="ExternalOutput").ap()
    kernel_program(nc, a)
    r = run_bass_kernel_spmd(nc, [{f"in_{k}": v for k, v in arrays.items()}], core_ids=[0])
    out = r.results[0]["out"]
    return np.ascontiguousarray(out.transpose(2, 1, 0)).reshape(1, N, D)
```
